# Optimizing a Trainium2 kernel written in Bass

```python
import jax, jax.numpy as jnp
from jax import lax
import numpy as np

D_MODEL = 1024
BATCH = 1
SEQ = 512
DEPTH = 2

N_A_LAYERS = DEPTH // 2
N_B_LAYERS = DEPTH - N_A_LAYERS
CONV_WIDTH = 3
HEAD_DIM = 128
KV_HEADS = D_MODEL // HEAD_DIM
DILATION_GROUPS = ((128, 1), (512, 4), (2048, 16))
N_GROUPS = len(DILATION_GROUPS)
Q_HEADS = N_GROUPS * KV_HEADS
ATTN_WIDTH = KV_HEADS * HEAD_DIM
ROPE_DIMS = HEAD_DIM // 4
ROPE_THETA = 500000.0
PEER_HEADS = 8
PEER_N_KEYS = 128
PEER_N_EXPERTS = PEER_N_KEYS ** 2
PEER_KEY_DIM = 256
PEER_HALF = PEER_KEY_DIM // 2
PEER_TOPK = 16
PEER_SELECTED = PEER_HEADS * PEER_TOPK
PEER_TOKEN_BLOCK = 128
PLE_DIM = 256
NORM_EPS = 1e-6

kernel_name = "yoco_shortconv_dilated_attn_peer"

def rms_norm(x, gain):
    xf = x.astype(jnp.float32)
    y = xf * lax.rsqrt(jnp.mean(xf * xf, axis=-1, keepdims=True) + NORM_EPS)
    return (y * gain.astype(jnp.float32)).astype(x.dtype)

def rope_tables(positions):
    inv_freq = 1.0 / (ROPE_THETA ** (jnp.arange(0, ROPE_DIMS, 2, dtype=jnp.float32) / ROPE_DIMS))
    ang = positions.astype(jnp.float32)[..., None] * inv_freq
    return jnp.cos(ang), jnp.sin(ang)

def apply_partial_rope(x, cos, sin):
    half = ROPE_DIMS // 2
    xf = x.astype(jnp.float32)
    x1, x2, rest = xf[..., :half], xf[..., half:ROPE_DIMS], xf[..., ROPE_DIMS:]
    c, s = cos[:, :, None, :], sin[:, :, None, :]
    out = jnp.concatenate([x1 * c - x2 * s, x2 * c + x1 * s, rest], axis=-1)
    return out.astype(x.dtype)

def short_conv_mixer(h, w_in, conv_w, w_out):
    b_gate, c_gate, u = jnp.split(h @ w_in, 3, axis=-1)
    z = lax.conv_general_dilated(c_gate * u, conv_w[:, None, :], window_strides=(1,),
                                 padding=((CONV_WIDTH - 1, 0),),
                                 dimension_numbers=('NWC', 'WIO', 'NWC'),
                                 feature_group_count=D_MODEL)
    return (b_gate * z) @ w_out

def dilated_window_attention(q, k, v, window, dilation):
    bsz, seq, nh, dh = q.shape
    span = window // dilation
    blk = span
    unit = dilation * blk
    s_pad = -(-seq // unit) * unit
    nblk = s_pad // unit
    pad = ((0, 0), (0, s_pad - seq), (0, 0), (0, 0))

    def to_blocks(t):
        return jnp.pad(t, pad).reshape(bsz, nblk, blk, dilation, nh, dh)

    def with_prev(t):
        prev = jnp.concatenate([jnp.zeros_like(t[:, :1]), t[:, :-1]], axis=1)
        return jnp.concatenate([prev, t], axis=2)

    qb = to_blocks(q)
    kw, vw = with_prev(to_blocks(k)), with_prev(to_blocks(v))
    scores = jnp.einsum('bnqrhd,bnkrhd->bnrhqk', qb, kw,
                        preferred_element_type=jnp.float32) * (dh ** -0.5)
    qi = jnp.arange(blk)[:, None]
    ki = jnp.arange(2 * blk)[None, :]
    dist = qi + blk - ki
    n_idx = jnp.arange(nblk)[:, None, None]
    valid = (dist >= 0) & (dist <= span) & (n_idx * blk + ki[None] - blk >= 0)
    scores = jnp.where(valid[None, :, None, None], scores, -jnp.inf)
    m = jnp.max(scores, axis=-1, keepdims=True)
    e = jnp.exp(scores - m)
    den = jnp.sum(e, axis=-1, keepdims=True)
    o = jnp.einsum('bnrhqk,bnkrhd->bnqrhd', e / den, vw.astype(jnp.float32))
    lse = (m + jnp.log(den))[..., 0]
    o = o.reshape(bsz, s_pad, nh, dh)[:, :seq]
    lse = jnp.transpose(lse, (0, 1, 4, 2, 3)).reshape(bsz, s_pad, nh)[:, :seq]
    return o, lse

def dilated_attention_mixer(h, w_q, q_gain, w_o, k_shared, v_shared, cos, sin):
    bsz, seq, _ = h.shape
    q = (h @ w_q).reshape(bsz, seq, Q_HEADS, HEAD_DIM)
    q = apply_partial_rope(rms_norm(q, q_gain), cos, sin)
    q = q.reshape(bsz, seq, N_GROUPS, KV_HEADS, HEAD_DIM)
    outs, lses = [], []
    for g, (window, dilation) in enumerate(DILATION_GROUPS):
        o_g, lse_g = dilated_window_attention(q[:, :, g], k_shared, v_shared, window, dilation)
        outs.append(o_g)
        lses.append(lse_g)
    weights = jax.nn.softmax(jnp.stack(lses, axis=0), axis=0)
    o = jnp.sum(weights[..., None] * jnp.stack(outs, axis=0), axis=0)
    return o.reshape(bsz, seq, ATTN_WIDTH).astype(h.dtype) @ w_o

def shared_kv(x, kv_gain, w_kv, k_gain, cos, sin):
    bsz, seq, _ = x.shape
    k, v = jnp.split(rms_norm(x, kv_gain) @ w_kv, 2, axis=-1)
    k = k.reshape(bsz, seq, KV_HEADS, HEAD_DIM)
    v = v.reshape(bsz, seq, KV_HEADS, HEAD_DIM)
    k = apply_partial_rope(rms_norm(k, k_gain), cos, sin)
    return k, v

def peer_channel_mixer(h, w_q, sub_keys, u, v):
    bsz, seq, dm = h.shape
    n_tok = bsz * seq
    hf = h.reshape(n_tok, dm)
    q = (hf @ w_q).astype(jnp.float32).reshape(n_tok, PEER_HEADS, 2, PEER_HALF)
    sub = jnp.einsum('thpc,hpkc->thpk', q, sub_keys.astype(jnp.float32))
    top_s, top_i = lax.top_k(sub, PEER_TOPK)
    cand_s = (top_s[:, :, 0, :, None] + top_s[:, :, 1, None, :]).reshape(n_tok, PEER_HEADS, PEER_TOPK ** 2)
    cand_i = (top_i[:, :, 0, :, None] * PEER_N_KEYS + top_i[:, :, 1, None, :]).reshape(n_tok, PEER_HEADS, PEER_TOPK ** 2)
    best_s, best_pos = lax.top_k(cand_s, PEER_TOPK)
    expert_idx = jnp.take_along_axis(cand_i, best_pos, axis=-1)
    gates = jax.nn.softmax(best_s, axis=-1)
    n_blk = n_tok // PEER_TOKEN_BLOCK

    def token_block(args):
        xb, idx, g = args
        act = jnp.einsum('cd,ced->ce', xb, u[idx], preferred_element_type=jnp.float32)
        a = (g * jax.nn.gelu(act, approximate=False)).astype(xb.dtype)
        return jnp.einsum('ce,ced->cd', a, v[idx])

    y = lax.map(token_block, (hf.reshape(n_blk, PEER_TOKEN_BLOCK, dm),
                              expert_idx.reshape(n_blk, PEER_TOKEN_BLOCK, PEER_SELECTED),
                              gates.reshape(n_blk, PEER_TOKEN_BLOCK, PEER_SELECTED)))
    return y.reshape(bsz, seq, dm)

def setup_inputs(seed: int = 0) -> dict:
    key = jax.random.key(seed)
    ks = jax.random.split(key, 24)
    f32 = jnp.float32

    def w(k, shape, fan_in):
        return jax.random.normal(k, shape, f32) * (fan_in ** -0.5)

    def gain(k, shape):
        return 1.0 + 0.01 * jax.random.normal(k, shape, f32)

    offsets = jax.random.randint(ks[2], (BATCH, 1), 0, 4096, dtype=jnp.int32)
    positions = offsets + jnp.arange(SEQ, dtype=jnp.int32)[None, :]
    return {
        "x": jax.random.normal(ks[0], (BATCH, SEQ, D_MODEL), f32),
        "p": jax.random.normal(ks[1], (DEPTH, BATCH, SEQ, PLE_DIM), f32),
        "positions": positions,
        "a_norm": gain(ks[3], (N_A_LAYERS, D_MODEL)),
        "a_w_in": w(ks[4], (N_A_LAYERS, D_MODEL, 3 * D_MODEL), D_MODEL),
        "a_conv": w(ks[5], (N_A_LAYERS, CONV_WIDTH, D_MODEL), CONV_WIDTH),
        "a_w_out": w(ks[6], (N_A_LAYERS, D_MODEL, D_MODEL), D_MODEL),
        "kv_norm": gain(ks[7], (D_MODEL,)),
        "w_kv": w(ks[8], (D_MODEL, 2 * ATTN_WIDTH), D_MODEL),
        "k_norm": gain(ks[9], (HEAD_DIM,)),
        "b_norm": gain(ks[10], (N_B_LAYERS, D_MODEL)),
        "b_w_q": w(ks[11], (N_B_LAYERS, D_MODEL, Q_HEADS * HEAD_DIM), D_MODEL),
        "q_norm": gain(ks[12], (N_B_LAYERS, HEAD_DIM)),
        "b_w_o": w(ks[13], (N_B_LAYERS, ATTN_WIDTH, D_MODEL), ATTN_WIDTH),
        "ffn_norm": gain(ks[14], (DEPTH, D_MODEL)),
        "peer_w_q": w(ks[15], (DEPTH, D_MODEL, PEER_HEADS * PEER_KEY_DIM), D_MODEL),
        "peer_sub_keys": w(ks[16], (DEPTH, PEER_HEADS, 2, PEER_N_KEYS, PEER_HALF), PEER_HALF),
        "peer_u": w(ks[17], (DEPTH, PEER_N_EXPERTS, D_MODEL), D_MODEL),
        "peer_v": w(ks[18], (DEPTH, PEER_N_EXPERTS, D_MODEL), PEER_TOPK),
        "ple_norm": gain(ks[19], (DEPTH, D_MODEL)),
        "ple_w_gate": w(ks[20], (DEPTH, D_MODEL, D_MODEL), D_MODEL),
        "ple_w_proj": w(ks[21], (DEPTH, PLE_DIM, D_MODEL), PLE_DIM),
    }

def reference(x, p, positions, a_norm, a_w_in, a_conv, a_w_out, kv_norm, w_kv, k_norm,
              b_norm, b_w_q, q_norm, b_w_o, ffn_norm, peer_w_q, peer_sub_keys, peer_u,
              peer_v, ple_norm, ple_w_gate, ple_w_proj):
    cos, sin = rope_tables(positions)
    k_sh, v_sh = None, None
    for i in range(DEPTH):
        if i < N_A_LAYERS:
            x = x + short_conv_mixer(rms_norm(x, a_norm[i]), a_w_in[i], a_conv[i], a_w_out[i])
        else:
            j = i - N_A_LAYERS
            x = x + dilated_attention_mixer(rms_norm(x, b_norm[j]), b_w_q[j], q_norm[j], b_w_o[j],
                                            k_sh, v_sh, cos, sin)
        x = x + peer_channel_mixer(rms_norm(x, ffn_norm[i]), peer_w_q[i], peer_sub_keys[i],
                                   peer_u[i], peer_v[i])
        x = x + jax.nn.sigmoid(rms_norm(x, ple_norm[i]) @ ple_w_gate[i]) * (p[i] @ ple_w_proj[i])
        if i == N_A_LAYERS - 1:
            k_sh, v_sh = shared_kv(x, kv_norm, w_kv, k_norm, cos, sin)
    return x


_drawn_inputs = setup_inputs


def setup_inputs(seed=0):
    import zlib

    import numpy as np

    out = dict(_drawn_inputs(seed))
    spreads = {}
    factors = {'a_norm': 3.351,
     'kv_norm': 31.06,
     'k_norm': 24.703,
     'b_norm': 30.61,
     'q_norm': 34.332,
     'ffn_norm': 34.536,
     'ple_norm': 177.314}
    for name, (base, spread) in spreads.items():
        noise = np.random.default_rng([zlib.crc32(name.encode()), seed]).standard_normal(out[name].shape)
        drawn = base * np.exp(spread * noise) if base else spread * noise
        out[name] = __import__('jax').numpy.asarray(drawn.astype(out[name].dtype))
    for name, factor in factors.items():
        out[name] = (out[name] * factor).astype(out[name].dtype)
    return out
```

```python
from contextlib import ExitStack

import numpy as np

import concourse.bass as bass
from concourse import mybir

P = 128
ALU = mybir.AluOpType
ACT = mybir.ActivationFunctionType
F32 = mybir.dt.float32
F32R = mybir.dt.float32r
BF16 = mybir.dt.bfloat16
I32 = mybir.dt.int32
U32 = mybir.dt.uint32
AX_X = mybir.AxisListType.X

D = 1024
SEQ = 512
TT = SEQ // P
DK = D // P
CONV_W = 3
DH = 128
KVH = D // DH
GROUPS = 3
DILATIONS = (1, 4, 16)
ROPE = DH // 4
HALF = ROPE // 2
THETA = 500000.0
PH = 8
NKEY = 128
TOPK = 16
NSEL = PH * TOPK
UNITS = TT * PH
EPS = 1e-6
LOWEST = -3.0e38
CHUNK = 2048
RAW = 4
SPLIT = 2
BODY = 4
CREDITS = 16
TWO_PI = 2.0 * np.pi


class Counter:

    def __init__(self, sem, credits=0):
        self.sem = sem
        self.base = credits


class Chain:

    def __init__(self, counter):
        self.counter = counter
        self.n = 0

    def link(self, eng, ins):
        ins.then_inc(self.counter.sem, 1)
        self.n += 1
        eng.wait_ge(self.counter.sem, self.counter.base + self.n)

    def close(self):
        self.counter.base += self.n
        self.n = 0

    def rewind(self, eng):
        eng.sem_inc(self.counter.sem, -self.n)
        self.n = 0


class Kernel:
    def __init__(self, nc, ctx, a):
        self.nc, self.ctx, self.a = nc, ctx, a
        self.counters = {}
        self.raw = self.tensor("raw", [P, RAW, CHUNK])
        self.chunks = 0
        self.raw_landed = [self.counter(f"raw_landed{s}").sem for s in range(RAW)]
        self.hi_ready = self.counter("hi_ready").sem
        self.lo_ready = self.counter("lo_ready").sem
        for name in ("turned_done", "turned_out", "rows_done", "rows_out", "ring_stored0", "ring_stored1",
                     "gates_done", "gates_used", "hot2_ready", "ys_done", "ys_added", "at_q_turned", "at_scores",
                     "at_masked", "at_w_turned", "at_w_out", "at_values", "at_out", "at_weights"):
            self.counter(name, CREDITS)
        self.x = self.tensor("x_res", [P, TT, D])
        self.ident = self.tensor("ident", [P, P])
        self.zero = self.tensor("zero", [P, 1])
        self.gains = self.tensor("gains", [P, 7, DK])
        self.iota = self.tensor("iota", [P, P])
        self.acts = nc.dram_tensor("expert_acts", (NKEY, P, SEQ), F32, kind="Internal").ap()
        self.dve = Chain(self.counter("dve_step"))

    def counter(self, name, credits=0):
        if name not in self.counters:
            self.counters[name] = Counter(self.ctx.enter_context(self.nc.semaphore(name)), credits)
        return self.counters[name]

    def tensor(self, name, shape, dt=F32, ctx=None):
        return (ctx or self.ctx).enter_context(self.nc.sbuf_tensor(name, shape, dt))

    def banks(self, name, ctx, n, shape=(P, 512), dt=F32):
        return [ctx.enter_context(self.nc.psum_tensor(f"{name}{b}", list(shape), dt)) for b in range(n)]


    def load_chunk(self, sp, src, i, k):
        slot = (self.chunks + k) % RAW
        sp.wait_ge(self.lo_ready, i * BODY + (self.chunks + k + 1))
        out = self.raw[:, slot, :]
        if len(src.shape) == 3:
            out = out.rearrange("p (b n) -> p b n", b=src.shape[1])
        sp.dma_start(out, src).then_inc(self.raw_landed[slot], 16)

    def load_rest(self, sp, total, src, after=None):
        if after is None:
            after = lambda i, k: None
        if total > RAW:
            with sp.Fori(0, total // BODY - 1) as i:
                for k in range(BODY):
                    self.load_chunk(sp, src(i * BODY + (k + RAW)), i, k + RAW)
                    after(i, k)
            for k in range(BODY):
                after(total // BODY - 1, k)
        else:
            for k in range(total):
                after(0, k)

    def load_first(self, sp, done, src):
        if src is None:
            return
        for k in range(RAW):
            slot = (self.chunks + done + k) % RAW
            sp.wait_ge(self.lo_ready, self.chunks + done + k + 1)
            s = src(k)
            out = self.raw[:, slot, :]
            if len(s.shape) == 3:
                out = out.rearrange("p (b n) -> p b n", b=s.shape[1])
            sp.dma_start(out, s).then_inc(self.raw_landed[slot], 16)

    def split_hi(self, act, used, i, k):
        c = self.chunks + k
        act.wait_ge(self.raw_landed[c % RAW], i * (16 * (BODY // RAW)) + 16 * (c // RAW + 1))
        products, per = used
        act.wait_ge(products.sem, i * (BODY * per) + (products.base + (k + 1 - SPLIT) * per))
        act.activation(self.hi[:, c % SPLIT, :], self.raw[:, c % RAW, :], ACT.Copy).then_inc(self.hi_ready, 1)

    def split_lo(self, dve, i, k):
        c = self.chunks + k
        dve.wait_ge(self.hi_ready, i * BODY + (c + 1))
        dve.tensor_tensor(self.lo[:, c % SPLIT, :], self.raw[:, c % RAW, :],
                          self.hi[:, c % SPLIT, :].bitcast(F32), ALU.subtract).then_inc(self.lo_ready, 1)

    def chunk_split(self, pe, i, k):
        pe.wait_ge(self.lo_ready, i * BODY + (self.chunks + k + 1 + RAW))

    def ahead(self, eng, total, lead, follow):
        trips = total // BODY
        lead(0, 0)
        if trips > 1:
            with eng.Fori(0, trips - 1) as i:
                for k in range(BODY):
                    lead(i, k + 1)
                    follow(i, k)
        for k in range(BODY):
            if k + 1 < BODY:
                lead(trips - 1, k + 1)
            follow(trips - 1, k)

    def split_tensors(self, ctx, tag):
        self.hi = self.tensor(f"w_hi_{tag}", [P, SPLIT, CHUNK], F32R, ctx)
        self.lo = self.tensor(f"w_lo_{tag}", [P, SPLIT, CHUNK], F32R, ctx)

    def three(self, pe, out, lhi, llo, rhi, rlo, first, last):
        pe.matmul(out, lhi, rhi, start=first, stop=False)
        pe.matmul(out, lhi, rlo, start=False, stop=False)
        return pe.matmul(out, llo, rhi, start=False, stop=last)


    def setup(self, first_src):
        a, nc = self.a, self.nc
        const = self.counter("const_ready")
        landed = self.counter("setup_landed")
        iota_i = self.tensor("iota_int", [P, P], I32)
        with nc.Block() as block:
            @block.sync
            def _(sp):
                sp.sem_inc(self.lo_ready, RAW)
                sp.dma_start(self.x[:], a["x"].rearrange("(t p) d -> p t d", p=P)).then_inc(landed.sem, 16)
                sp.dma_start(self.gains[:], a["gains"].rearrange("g p k -> p g k")).then_inc(landed.sem, 16)
                self.load_first(sp, 0, first_src)
                sp.wait_ge(landed.sem, 32)

            @block.scalar
            def _(act):
                for counter in self.counters.values():
                    if counter.base:
                        act.sem_inc(counter.sem, counter.base)

            @block.gpsimd
            def _(pool):
                pool.memset(self.zero[:], 0.0).then_inc(const.sem, 1)
                pool.memset(self.ident[:], 0.0).then_inc(const.sem, 1)
                pool.iota(iota_i[:], pattern=[[1, P]], base=0, channel_multiplier=0).then_inc(const.sem, 1)
                pool.wait_ge(const.sem, 3)
                pool.tensor_copy(self.iota[:], iota_i[:]).then_inc(const.sem, 1)
                pool.affine_select(out=self.ident[:], in_=self.ident[:], compare_op=ALU.not_equal, fill=1.0,
                                   base=0, pattern=[[-1, P]], channel_multiplier=1).then_inc(const.sem, 1)
        const.base += 5
        landed.base += 32


    def rsqrt_steps(self, dve, act_sqrt, v, y, t):
        ch = self.dve
        act_sqrt(v, t)
        ch.link(dve, dve.reciprocal(y, t))
        ch.link(dve, dve.tensor_tensor(t, y, y, ALU.mult))
        ch.link(dve, dve.tensor_tensor(t, t, v, ALU.mult))
        ch.link(dve, dve.tensor_scalar(t, t, -0.5, 1.5, ALU.mult, ALU.add))
        ch.link(dve, dve.tensor_tensor(y, y, t, ALU.mult))

    def norm(self, tag, gain, h_hi, h_lo):
        nc = self.nc
        sq = self.counter("norm_squares")
        root_in = self.counter("norm_root_in")
        root = self.counter("norm_root")
        scaled = self.counter("norm_scaled")
        turned = self.counter("norm_turned")
        hi_done = self.counter("norm_hi")
        lo_done = self.counter("norm_lo")
        with ExitStack() as ctx:
            xn = self.tensor(f"xn_{tag}", [P, TT, D], ctx=ctx)
            junk = self.tensor(f"junk_{tag}", [P, D], ctx=ctx)
            st = self.tensor(f"stat_{tag}", [P, 4, TT], ctx=ctx)
            bank = self.banks(f"turn_{tag}", ctx, 4)
            ss, v, y, t = (st[:, n, :] for n in range(4))
            g = self.gains[:, gain, :]
            with nc.Block() as block:
                @block.scalar
                def _(act):
                    for m in range(TT):
                        if m:
                            act.wait_ge(sq.sem, sq.base + m)
                        act.activation(junk[:], self.x[:, m, :], ACT.Square, accum_out=ss[:, m:m + 1]).then_inc(sq.sem, 1)
                    act.wait_ge(root_in.sem, root_in.base + 1)
                    act.activation(t, v, ACT.Sqrt).then_inc(root.sem, 1)
                    for k in range(DK):
                        act.wait_ge(turned.sem, turned.base + k + 1)
                        act.activation(h_hi[:, k, :], bank[k % 4][:], ACT.Copy, scale=g[:, k:k + 1]).then_inc(hi_done.sem, 1)

                @block.vector
                def _(dve):
                    dve.wait_ge(sq.sem, sq.base + TT)
                    dve.tensor_scalar(v, ss, 1.0 / D, EPS, ALU.mult, ALU.add).then_inc(root_in.sem, 1)
                    self.rsqrt_steps(dve, lambda v, t: dve.wait_ge(root.sem, root.base + 1), v, y, t)
                    for m in range(TT):
                        dve.tensor_scalar(xn[:, m, :], self.x[:, m, :], y[:, m:m + 1], None, ALU.mult).then_inc(scaled.sem, 1)
                    for k in range(DK):
                        dve.wait_ge(hi_done.sem, hi_done.base + k + 1)
                        dve.scalar_tensor_tensor(h_lo[:, k, :], bank[k % 4][:], g[:, k:k + 1], h_hi[:, k, :].bitcast(F32),
                                                 ALU.mult, ALU.subtract).then_inc(lo_done.sem, 1)
                    dve.wait_ge(lo_done.sem, lo_done.base + DK)

                @block.tensor
                def _(pe):
                    pe.wait_ge(scaled.sem, scaled.base + TT)
                    for k in range(DK):
                        if k >= 4:
                            pe.wait_ge(lo_done.sem, lo_done.base + k - 3)
                        for m in range(TT):
                            last = pe.transpose(bank[k % 4][:, m * P:(m + 1) * P], xn[:, m, k * P:(k + 1) * P], self.ident[:])
                        last.then_inc(turned.sem, 1)
            self.dve.close()
            for s, n in ((sq, TT), (root_in, 1), (root, 1), (scaled, TT), (turned, DK), (hi_done, DK), (lo_done, DK)):
                s.base += n

    def split_rows(self, tag, src_slice, h_hi, h_lo, nk):
        hi_done = self.counter("rows_hi")
        lo_done = self.counter("rows_lo")
        with self.nc.Block() as block:
            @block.scalar
            def _(act):
                for k in range(nk):
                    act.activation(h_hi[:, k, :], src_slice(k), ACT.Copy).then_inc(hi_done.sem, 1)

            @block.vector
            def _(dve):
                for k in range(nk):
                    dve.wait_ge(hi_done.sem, hi_done.base + k + 1)
                    dve.tensor_tensor(h_lo[:, k, :], src_slice(k), h_hi[:, k, :].bitcast(F32), ALU.subtract).then_inc(lo_done.sem, 1)
                dve.wait_ge(lo_done.sem, lo_done.base + nk)
        hi_done.base += nk
        lo_done.base += nk


    def loop_chunks(self, eng, total, chunk):
        trips = total // BODY
        if trips > 1:
            with eng.Fori(0, trips) as i:
                for k in range(BODY):
                    chunk(i, k)
        else:
            for k in range(total):
                chunk(0, k)

    def product_turned(self, tag, h_hi, h_lo, total, src, next_src, dst=None, store=None, func=ACT.Copy, route=None):
        done = self.counter("turned_done")
        out = self.counter("turned_out")
        with ExitStack() as ctx:
            self.split_tensors(ctx, tag)
            bank = self.banks(f"acc_{tag}", ctx, 4)
            if store:
                ring = self.tensor(f"ring_{tag}", [P, 2, 2 * SEQ], ctx=ctx)
                ring_sem = [self.counter(f"ring_stored{r}", CREDITS) for r in range(2)]
            unit = route(ctx) if route else None
            with self.nc.Block() as block:
                @block.sync
                def _(sp):
                    def put(i, k):
                        sp.wait_ge(out.sem, i * (2 * BODY) + (out.base + 2 * k + 2))
                        sp.dma_start(store(i * BODY + k).rearrange("b p t -> p b t"),
                                     ring[:, k % 2, :].rearrange("p (b t) -> p b t", b=2)).then_inc(ring_sem[k % 2].sem, 16)
                    self.load_rest(sp, total, src, put if store else None)
                    self.load_first(sp, total, next_src)
                    if store:
                        for r in range(2):
                            sp.wait_ge(ring_sem[r].sem, ring_sem[r].base + 16 * (total // 2))

                @block.scalar
                def _(act):
                    def evacuate(i, k):
                        for b in range(2):
                            n = 2 * k + b
                            act.wait_ge(done.sem, i * (2 * BODY) + (done.base + n + 1))
                            if store:
                                act.wait_ge(ring_sem[k % 2].sem, i * (16 * BODY // 2) + (ring_sem[k % 2].base + 16 * (k // 2)))
                                act.activation(ring[:, k % 2, b * SEQ:(b + 1) * SEQ], bank[n % 4][:], func).then_inc(out.sem, 1)
                            else:
                                at = (i * (2 * BODY) + n) * SEQ
                                act.activation(dst[:, bass.ds(at, SEQ)], bank[n % 4][:], func).then_inc(out.sem, 1)
                    self.ahead(act, total, lambda i, k: self.split_hi(act, (done, 2), i, k), evacuate)
                    act.wait_ge(out.sem, out.base + 2 * total)

                @block.vector
                def _(dve):
                    if unit:
                        unit(dve, self)
                    else:
                        self.loop_chunks(dve, total, lambda i, k: self.split_lo(dve, i, k))

                @block.tensor
                def _(pe):
                    def chunk(i, k):
                        self.chunk_split(pe, i, k)
                        s = (self.chunks + k) % SPLIT
                        for b in range(2):
                            n = 2 * k + b
                            pe.wait_ge(out.sem, i * (2 * BODY) + (out.base + n - 3))
                            for kk in range(DK):
                                w = slice((b * DK + kk) * P, (b * DK + kk + 1) * P)
                                last = self.three(pe, bank[n % 4][:], self.hi[:, s, w], self.lo[:, s, w],
                                                  h_hi[:, kk, :], h_lo[:, kk, :], kk == 0, kk == DK - 1)
                            last.then_inc(done.sem, 1)
                    self.loop_chunks(pe, total, chunk)
            done.base += 2 * total
            out.base += 2 * total
            if store:
                for r in range(2):
                    ring_sem[r].base += 16 * (total // 2)
            self.chunks += total

    def product_rows(self, tag, h_hi, h_lo, total, src, next_src, finish):
        done = self.counter("rows_done")
        out = self.counter("rows_out")
        with ExitStack() as ctx:
            self.split_tensors(ctx, tag)
            bank = self.banks(f"acc_{tag}", ctx, 8)
            with self.nc.Block() as block:
                @block.sync
                def _(sp):
                    self.load_rest(sp, total, src)
                    self.load_first(sp, total, next_src)

                @block.scalar
                def _(act):
                    self.loop_chunks(act, total, lambda i, k: self.split_hi(act, (done, TT), i, k))

                @block.vector
                def _(dve):
                    def evacuate(i, k):
                        if k % 2:
                            for m in range(TT):
                                dve.wait_ge(done.sem, i * (TT * BODY) + (done.base + TT * k + m + 1))
                                finish(dve, i * (BODY // 2) + k // 2, m, bank[(k // 2) % 2 * TT + m][:]).then_inc(out.sem, 1)
                    self.ahead(dve, total, lambda i, k: self.split_lo(dve, i, k), evacuate)
                    dve.wait_ge(out.sem, out.base + total * TT // 2)

                @block.tensor
                def _(pe):
                    def chunk(i, k):
                        self.chunk_split(pe, i, k)
                        s = (self.chunks + k) % SPLIT
                        for m in range(TT):
                            if k % 2 == 0:
                                pe.wait_ge(out.sem, i * (TT * BODY // 2) + (out.base + (k // 2 - 2) * TT + m + 1))
                            for kk in range(DK // 2):
                                w = slice(kk * 512, (kk + 1) * 512)
                                h = k % 2 * (DK // 2) + kk
                                t = slice(m * P, (m + 1) * P)
                                last = self.three(pe, bank[(k // 2) % 2 * TT + m][:], h_hi[:, h, t], h_lo[:, h, t],
                                                  self.hi[:, s, w], self.lo[:, s, w], h == 0, h == DK - 1)
                            last.then_inc(done.sem, 1)
                    self.loop_chunks(pe, total, chunk)
            done.base += TT * total
            out.base += TT * total // 2
            self.chunks += total


    def peer(self, layer, next_src):
        a = self.a
        wq = a["peer_wq"][layer]
        u = a["peer_u"][layer]
        v = a["peer_v"][layer].rearrange("(i1 i2) d -> i1 i2 d", i2=NKEY)
        wq_src = lambda c: wq[bass.ds(c, 1)].rearrange("a p n -> p a n")
        u_src = lambda c: u[bass.ds(c * 2, 2)].rearrange("b p n -> p b n")
        with ExitStack() as ctx:
            best = self.tensor(f"best{layer}", [P, UNITS, TOPK], ctx=ctx)
            picks = self.tensor(f"picks{layer}", [P, 2, UNITS * TOPK], ctx=ctx)
            with ExitStack() as h_ctx:
                h_hi = self.tensor(f"h_hi_p{layer}", [P, DK, SEQ], F32R, h_ctx)
                h_lo = self.tensor(f"h_lo_p{layer}", [P, DK, SEQ], F32R, h_ctx)
                self.norm(f"p{layer}", 3 + layer, h_hi, h_lo)
                sub = self.tensor(f"sub{layer}", [P, UNITS * 2 * NKEY], ctx=h_ctx)
                with ExitStack() as q_ctx:
                    qT = self.tensor(f"qT{layer}", [P, 2 * PH * SEQ], ctx=q_ctx)
                    self.product_turned(f"pq{layer}", h_hi, h_lo, PH, wq_src, u_src, dst=qT)
                    self.sub_scores(layer, qT, sub)
                self.product_turned(
                    f"pu{layer}", h_hi, h_lo, NKEY // 2, u_src, None, func=ACT.Gelu,
                    store=lambda c: self.acts[bass.ds(c * 2, 2)],
                    route=lambda c: self.router(c, layer, sub, best, picks))
            self.gate_matrix(layer, best, picks, v)
            self.expert_sum(layer, v, next_src)

    def v_src(self, v):
        return lambda g, k: v[:, bass.ds(g * 8 + 4 * (k % 2), 4), 512 * (k // 2):512 * (k // 2) + 512]

    def sub_scores(self, layer, qT, sub):
        keys_sem = self.counter("keys_landed")
        done = self.counter("sub_done")
        out = self.counter("sub_out")
        fills = UNITS // 2
        with ExitStack() as ctx:
            keys = self.tensor(f"keys{layer}", [P, 2 * PH, NKEY], ctx=ctx)
            bank = self.banks(f"sub_acc{layer}", ctx, 4)
            with self.nc.Block() as block:
                @block.sync
                def _(sp):
                    sp.dma_start(keys[:], self.a["peer_keys"][layer]).then_inc(keys_sem.sem, 16)

                @block.scalar
                def _(act):
                    for n in range(fills):
                        act.wait_ge(done.sem, done.base + n + 1)
                        act.activation(sub[:, n * 512:(n + 1) * 512], bank[n % 4][:], ACT.Copy).then_inc(out.sem, 1)
                    act.wait_ge(out.sem, out.base + fills)

                @block.tensor
                def _(pe):
                    pe.wait_ge(keys_sem.sem, keys_sem.base + 16)
                    for n in range(fills):
                        m, pair = divmod(n, PH // 2)
                        if n >= 4:
                            pe.wait_ge(out.sem, out.base + n - 3)
                        for j in range(4):
                            hp = pair * 4 + j
                            last = pe.matmul(bank[n % 4][:, j * NKEY:(j + 1) * NKEY],
                                             qT[:, hp * SEQ + m * P:hp * SEQ + (m + 1) * P], keys[:, hp, :],
                                             start=True, stop=True)
                        last.then_inc(done.sem, 1)
            keys_sem.base += 16
            done.base += fills
            out.base += fills

    def router(self, ctx, layer, sub, best, picks):
        s = self.tensor(f"scores{layer}", [P, 2, NKEY], ctx=ctx)
        s2 = self.tensor(f"scores_less_8{layer}", [P, 2, NKEY], ctx=ctx)
        vals = self.tensor(f"vals{layer}", [P, 2, TOPK], ctx=ctx)
        idx = self.tensor(f"idx{layer}", [P, 2, TOPK], U32, ctx)
        idxf = self.tensor(f"idxf{layer}", [P, 2, TOPK], ctx=ctx)
        cand = self.tensor(f"cand{layer}", [P, TOPK * TOPK], ctx=ctx)
        cand2 = self.tensor(f"cand_less_8{layer}", [P, TOPK * TOPK], ctx=ctx)
        top = self.tensor(f"top{layer}", [P, TOPK], ctx=ctx)
        pos = self.tensor(f"pos{layer}", [P, TOPK], U32, ctx)
        posij = self.tensor(f"posij{layer}", [P, 2, TOPK], U32, ctx)
        posf = self.tensor(f"posf{layer}", [P, 2, TOPK], ctx=ctx)
        hot = self.tensor(f"hot{layer}", [P, 2, TOPK, TOPK], ctx=ctx)
        hot2 = self.tensor(f"hot_times_key{layer}", [P, 2, TOPK, TOPK], ctx=ctx)

        def top16(dve, link, values, rest, v16, i16):
            link(dve, dve.max(v16[:, 0:8], values))
            link(dve, dve.max_index(i16[:, 0:8], v16[:, 0:8], values))
            link(dve, dve.match_replace(rest, v16[:, 0:8], values, LOWEST))
            link(dve, dve.max(v16[:, 8:16], rest))
            link(dve, dve.max_index(i16[:, 8:16], v16[:, 8:16], rest))

        def one(dve, unit):
            link = self.dve.link
            link(dve, dve.tensor_copy(s[:].rearrange("p a k -> p (a k)"), sub[:, bass.ds(unit * (2 * NKEY), 2 * NKEY)]))
            for half in range(2):
                top16(dve, link, s[:, half, :], s2[:, half, :], vals[:, half, :], idx[:, half, :])
            link(dve, dve.tensor_copy(idxf[:], idx[:]))
            link(dve, dve.tensor_tensor(cand[:].rearrange("p (i j) -> p i j", i=TOPK),
                                        vals[:, 0, :].unsqueeze(2).to_broadcast([P, TOPK, TOPK]),
                                        vals[:, 1, :].unsqueeze(1).to_broadcast([P, TOPK, TOPK]), ALU.add))
            top16(dve, link, cand[:], cand2[:], top[:], pos[:])
            link(dve, dve.tensor_scalar(posij[:, 0, :], pos[:], 4, None, ALU.logical_shift_right))
            link(dve, dve.tensor_scalar(posij[:, 1, :], pos[:], TOPK - 1, None, ALU.bitwise_and))
            link(dve, dve.tensor_copy(posf[:], posij[:]))
            link(dve, dve.tensor_tensor(hot[:].rearrange("p a s c -> p (a s) c"),
                                        posf[:].rearrange("p a s -> p (a s)").unsqueeze(2).to_broadcast([P, 2 * TOPK, TOPK]),
                                        self.iota[:, 0:TOPK].unsqueeze(1).to_broadcast([P, 2 * TOPK, TOPK]), ALU.is_equal))
            for half in range(2):
                link(dve, dve.tensor_tensor(hot2[:, half], hot[:, half],
                                            idxf[:, half, :].unsqueeze(1).to_broadcast([P, TOPK, TOPK]), ALU.mult))
            link(dve, dve.tensor_reduce(picks[:, :, bass.ds(unit * TOPK, TOPK)], hot2[:], AX_X, ALU.add))
            link(dve, dve.tensor_copy(best[:, bass.ds(unit, 1), :].rearrange("p a s -> p (a s)"), top[:]))

        def run(dve, kernel):
            with dve.Fori(0, UNITS // 2) as i:
                self.dve.close()
                for k in range(BODY):
                    self.split_lo(dve, i, k)
                    if k % 2:
                        one(dve, i * 2 + k // 2)
                self.dve.rewind(dve)
        return run

    def gate_matrix(self, layer, best, picks, v):
        nc = self.nc
        c = self.counter
        gate_in, gate_exp, gated = c("gate_in"), c("gate_exp"), c("gated")
        tdone, tout = c("pick_turned"), c("pick_out")
        hot1, hot2, mdone, mult = c("hot1_ready"), c("hot2_ready"), c("gates_done"), c("gates_used")
        diffed, absed = c("diff_ready"), c("abs_ready")
        tile_in = [c(f"tile_in{r}") for r in range(2)]
        tile_out = [c(f"tile_out{r}") for r in range(2)]
        BT = 16
        QUADS = P // 4
        with ExitStack() as ctx:
            t = lambda n, s, dt=F32: self.tensor(f"{n}{layer}", s, dt, ctx)
            small = t("gate_small", [P, 2, UNITS])
            gates = t("gates", [P, UNITS, TOPK])
            turned = t("picks_turned", [P, 3, SEQ])
            tile = t("act_tile", [P, 2, NKEY, P])
            oh1 = t("hot1", [P, 2, 4, P])
            oh2 = t("hot2x", [P, 2, 4, P])
            diff = t("key_less_i2", [P, 2, 4, P])
            bank = self.banks(f"gm{layer}", ctx, 4)
            tbank = self.banks(f"gt{layer}", ctx, 3)
            flat = lambda ap: ap.rearrange("p u s -> p (u s)")
            iota4 = self.iota[:].unsqueeze(1).to_broadcast([P, 4, P])
            with nc.Block() as block:
                @block.sync
                def _(sp):
                    def load(m):
                        sp.dma_start(tile[:, m % 2], self.acts[:, :, m * P:(m + 1) * P].rearrange("i p t -> p i t")).then_inc(tile_in[m % 2].sem, 16)
                    load(0)
                    load(1)
                    for m in range(TT):
                        sp.wait_ge(mult.sem, mult.base + (m + 1) * QUADS)
                        sp.dma_start(self.acts[:, :, m * P:(m + 1) * P].rearrange("i p t -> p i t"), tile[:, m % 2]).then_inc(tile_out[m % 2].sem, 16)
                        if m + 2 < TT:
                            sp.wait_ge(tile_out[m % 2].sem, tile_out[m % 2].base + 16)
                            load(m + 2)
                    src = self.v_src(v)
                    self.load_first(sp, 0, lambda k: src(0, k))
                    for r in range(2):
                        sp.wait_ge(tile_out[r].sem, tile_out[r].base + 32)

                @block.scalar
                def _(act):
                    act.wait_ge(gate_in.sem, gate_in.base + 1)
                    act.activation(gates[:], gates[:], ACT.Exp).then_inc(gate_exp.sem, 1)
                    for n in range(3):
                        act.wait_ge(tdone.sem, tdone.base + n + 1)
                        act.activation(turned[:, n, :], tbank[n][:], ACT.Copy).then_inc(tout.sem, 1)

                    for m in range(TT):
                        with act.Fori(0, P // BT) as i:
                            for q in range(BT // 4):
                                n = m * QUADS + q
                                act.wait_ge(diffed.sem, i * (BT // 4) + (diffed.base + n + 1))
                                act.wait_ge(mdone.sem, i * (BT // 4) + (mdone.base + n - 1))
                                act.activation(diff[:, q % 2], diff[:, q % 2], ACT.Abs).then_inc(absed.sem, 1)
                                act.wait_ge(absed.sem, i * (BT // 4) + (absed.base + n + 1))
                                act.activation(oh2[:, q % 2], diff[:, q % 2], ACT.Relu, bias=1.0, scale=-1.0).then_inc(hot2.sem, 1)

                @block.gpsimd
                def _(pool):
                    pool.wait_ge(tout.sem, tout.base + 3)
                    for m in range(TT):
                        with pool.Fori(0, P // BT) as i:
                            for q in range(BT // 4):
                                n = m * QUADS + q
                                pool.wait_ge(hot2.sem, i * (BT // 4) + (hot2.base + n - 1))
                                pool.tensor_tensor(diff[:, q % 2], iota4,
                                                   turned[:, 1, bass.ds(i * BT + (m * P + 4 * q), 4)].unsqueeze(2).to_broadcast([P, 4, P]),
                                                   ALU.subtract).then_inc(diffed.sem, 1)

                @block.vector
                def _(dve):
                    ch = self.dve
                    ch.link(dve, dve.tensor_tensor(gates[:], best[:], best[:, :, 0:1].to_broadcast([P, UNITS, TOPK]), ALU.subtract))
                    dve.sem_inc(gate_in.sem, 1)
                    dve.wait_ge(gate_exp.sem, gate_exp.base + 1)
                    ch.link(dve, dve.tensor_reduce(small[:, 0, :], gates[:], AX_X, ALU.add))
                    ch.link(dve, dve.reciprocal(small[:, 1, :], small[:, 0, :]))
                    dve.tensor_tensor(gates[:], gates[:], small[:, 1, :].unsqueeze(2).to_broadcast([P, UNITS, TOPK]), ALU.mult).then_inc(gated.sem, 1)
                    dve.wait_ge(tout.sem, tout.base + 3)

                    def hot(m, i, q):
                        n = m * QUADS + q
                        dve.wait_ge(mdone.sem, i * (BT // 4) + (mdone.base + n - 1))
                        for r in range(4):
                            at = i * BT + (m * P + 4 * q + r)
                            last = dve.tensor_scalar(oh1[:, q % 2, r, :], self.iota[:], turned[:, 0, bass.ds(at, 1)],
                                                     turned[:, 2, bass.ds(at, 1)], ALU.is_equal, ALU.mult)
                        last.then_inc(hot1.sem, 1)

                    def multiply(m, i, q):
                        n = m * QUADS + q
                        dve.wait_ge(mdone.sem, i * (BT // 4) + (mdone.base + n + 1))
                        at = tile[:, m % 2, :, bass.ds(i * BT + 4 * q, 4)].rearrange("p i t -> p t i")
                        dve.tensor_tensor(at, at, bank[q % 4][:].rearrange("p (t i) -> p t i", t=4), ALU.mult).then_inc(mult.sem, 1)

                    for m in range(TT):
                        dve.wait_ge(tile_in[m % 2].sem, tile_in[m % 2].base + 16 * (m // 2 + 1))
                        with dve.Fori(0, P // BT) as i:
                            hot(m, i, 0)
                            for q in range(BT // 4):
                                if q + 1 < BT // 4:
                                    hot(m, i, q + 1)
                                multiply(m, i, q)
                    dve.wait_ge(mult.sem, mult.base + TT * QUADS)

                @block.tensor
                def _(pe):
                    for n, src in enumerate((picks[:, 0, :], picks[:, 1, :], flat(gates[:]))):
                        if n == 2:
                            pe.wait_ge(gated.sem, gated.base + 1)
                        for m in range(TT):
                            last = pe.transpose(tbank[n][:, m * P:(m + 1) * P], src[:, m * P:(m + 1) * P], self.ident[:])
                        last.then_inc(tdone.sem, 1)
                    for m in range(TT):
                        with pe.Fori(0, P // BT) as i:
                            for q in range(BT // 4):
                                n = m * QUADS + q
                                pe.wait_ge(hot1.sem, i * (BT // 4) + (hot1.base + n + 1))
                                pe.wait_ge(hot2.sem, i * (BT // 4) + (hot2.base + n + 1))
                                pe.wait_ge(mult.sem, i * (BT // 4) + (mult.base + n - 3))
                                for r in range(4):
                                    last = pe.matmul(bank[q % 4][:, r * P:(r + 1) * P], oh1[:, q % 2, r, :], oh2[:, q % 2, r, :],
                                                     start=True, stop=True)
                                last.then_inc(mdone.sem, 1)
            self.dve.close()
            for s, n in ((gate_in, 1), (gate_exp, 1), (gated, 1), (tdone, 3), (tout, 3), (hot1, TT * QUADS),
                         (hot2, TT * QUADS), (diffed, TT * QUADS), (absed, TT * QUADS), (mdone, TT * QUADS), (mult, TT * QUADS), (tile_in[0], 32), (tile_in[1], 32),
                         (tile_out[0], 32), (tile_out[1], 32)):
                s.base += n

    def expert_sum(self, layer, v, next_src):
        nc = self.nc
        c = self.counter
        G = NKEY // 8
        BODY2 = 2 * BODY
        done, out, a_hi_n, a_lo_n = c("ys_done"), c("ys_added"), c("a_hi_ready"), c("a_lo_ready")
        a_in = [c(f"a_in{r}") for r in range(2)]
        src = self.v_src(v)
        ch = self.chunks
        with ExitStack() as ctx:
            self.split_tensors(ctx, f"v{layer}")
            a_raw = self.tensor(f"a_raw{layer}", [P, 2, 8, SEQ], ctx=ctx)
            a_hi = self.tensor(f"a_hi{layer}", [P, 2, 8, SEQ], F32R, ctx)
            a_lo = self.tensor(f"a_lo{layer}", [P, 2, 8, SEQ], F32R, ctx)
            bank = self.banks(f"y{layer}", ctx, 8)

            def pairs(eng, step):
                with eng.Fori(0, G // 2) as i:
                    for k in range(BODY2):
                        step(i, k)

            def ahead(eng, lead, follow, first):
                first()
                lead(0, 0)
                with eng.Fori(0, G // 2 - 1) as i:
                    for k in range(BODY2):
                        lead(i, k + 1)
                        follow(i, k, False)
                for k in range(BODY2):
                    if k + 1 < BODY2:
                        lead(G // 2 - 1, k + 1)
                    follow(G // 2 - 1, k, k >= BODY)

            def hi(act, i, k):
                act.wait_ge(self.raw_landed[(ch + k) % RAW], i * (16 * BODY2 // RAW) + 16 * ((ch + k) // RAW + 1))
                act.wait_ge(done.sem, i * (TT * BODY2) + (done.base + TT * (k + 1 - SPLIT)))
                act.activation(self.hi[:, (ch + k) % SPLIT, :], self.raw[:, (ch + k) % RAW, :], ACT.Copy).then_inc(self.hi_ready, 1)

            def lo(dve, i, k):
                dve.wait_ge(self.hi_ready, i * BODY2 + (ch + k + 1))
                dve.tensor_tensor(self.lo[:, (ch + k) % SPLIT, :], self.raw[:, (ch + k) % RAW, :],
                                  self.hi[:, (ch + k) % SPLIT, :].bitcast(F32), ALU.subtract).then_inc(self.lo_ready, 1)

            def a_piece(k):
                return (k // 4) % 2, slice(2 * (k % 4), 2 * (k % 4) + 2)

            with nc.Block() as block:
                @block.sync
                def _(sp):
                    def load_a(g, r):
                        sp.dma_start(a_raw[:, r], self.acts[bass.ds(g * 8, 8)].rearrange("i p t -> p i t")).then_inc(a_in[r].sem, 16)
                    load_a(0, 0)
                    load_a(1, 1)

                    def load_v(i, k):
                        sp.wait_ge(self.lo_ready, i * BODY2 + (ch + k + 1))
                        slot = (ch + k) % RAW
                        sp.dma_start(self.raw[:, slot, :].rearrange("p (b n) -> p b n", b=4),
                                     src(i * 2 + k // 4, k % 4)).then_inc(self.raw_landed[slot], 16)
                    with sp.Fori(0, G // 2 - 1) as i:
                        for k in range(BODY2):
                            load_v(i, k + RAW)
                            if k % 4 == 3:
                                sp.wait_ge(a_lo_n.sem, i * BODY2 + (a_lo_n.base + k + 1))
                                load_a(i * 2 + (k // 4 + 2), k // 4)
                    for k in range(BODY2 - RAW):
                        load_v(G // 2 - 1, k + RAW)
                    self.load_first(sp, 4 * G, next_src)

                @block.scalar
                def _(act):
                    def a_split(slot, part):
                        act.activation(a_hi[:, slot, part, :], a_raw[:, slot, part, :], ACT.Copy).then_inc(a_hi_n.sem, 1)

                    def first():
                        act.wait_ge(a_in[0].sem, a_in[0].base + 16)
                        for k in range(4):
                            a_split(0, a_piece(k)[1])

                    def follow(i, k, last):
                        if last:
                            return
                        r, part = a_piece(k + 4)
                        if k % 4 == 0:
                            act.wait_ge(a_in[r].sem, i * 16 + (a_in[r].base + 16 * ((k + 4) // 8 + 1)))
                            act.wait_ge(done.sem, i * (TT * BODY2) + (done.base + TT * k))
                        a_split(r, part)
                    ahead(act, lambda i, k: hi(act, i, k), follow, first)

                @block.vector
                def _(dve):
                    def a_split(slot, part, n, i):
                        dve.wait_ge(a_hi_n.sem, i * BODY2 + (a_hi_n.base + n + 1))
                        dve.tensor_tensor(a_lo[:, slot, part, :], a_raw[:, slot, part, :],
                                          a_hi[:, slot, part, :].bitcast(F32), ALU.subtract).then_inc(a_lo_n.sem, 1)

                    def first():
                        for k in range(4):
                            a_split(0, a_piece(k)[1], k, 0)

                    def follow(i, k, last):
                        if not last:
                            r, part = a_piece(k + 4)
                            a_split(r, part, k + 4, i)
                        if k % 2:
                            half = k // 2 % 2
                            for m in range(TT):
                                dve.wait_ge(done.sem, i * (TT * BODY2) + (done.base + TT * k + m + 1))
                                at = self.x[:, m, half * 512:half * 512 + 512]
                                dve.tensor_tensor(at, at, bank[half * TT + m][:], ALU.add).then_inc(out.sem, 1)
                    ahead(dve, lambda i, k: lo(dve, i, k), follow, first)
                    dve.wait_ge(out.sem, out.base + 2 * TT * G)

                @block.tensor
                def _(pe):
                    def chunk(i, k):
                        pe.wait_ge(self.lo_ready, i * BODY2 + (ch + k + 1 + RAW))
                        s = (ch + k) % SPLIT
                        r, half = k // 4, k // 2 % 2
                        if k % 4 == 0:
                            pe.wait_ge(a_lo_n.sem, i * BODY2 + (a_lo_n.base + k + 4))
                        for m in range(TT):
                            t = slice(m * P, (m + 1) * P)
                            if k % 2 == 0:
                                pe.wait_ge(out.sem, i * (4 * TT) + (out.base + (k // 2 - 2) * TT + m + 1))
                            for e in range(4):
                                j = 4 * (k % 2) + e
                                w = slice(e * 512, (e + 1) * 512)
                                last = self.three(pe, bank[half * TT + m][:], a_hi[:, r, j, t], a_lo[:, r, j, t],
                                                  self.hi[:, s, w], self.lo[:, s, w], j == 0, j == 7)
                            last.then_inc(done.sem, 1)
                    pairs(pe, chunk)
            for s, n in ((done, TT * 4 * G), (out, 2 * TT * G), (a_hi_n, 4 * G), (a_lo_n, 4 * G), (a_in[0], 8 * G), (a_in[1], 8 * G)):
                s.base += n
            self.chunks += 4 * G


    def conv_mixer(self, next_src):
        a = self.a
        chain = self.dve
        taps_sem = self.counter("taps_landed")
        with ExitStack() as ctx:
            h_hi = self.tensor("h_hi_c", [P, DK, SEQ], F32R, ctx)
            h_lo = self.tensor("h_lo_c", [P, DK, SEQ], F32R, ctx)
            w_in = lambda c: a["a_w_in"][bass.ds(c, 1)].rearrange("a p n -> p a n")
            w_out = lambda c: a["a_w_out"][bass.ds(c, 1)].rearrange("a p n -> p a n")
            self.norm("c", 0, h_hi, h_lo)
            with ExitStack() as ctx2:
                bcu = self.tensor("bcu", [P, 3 * DK * SEQ], ctx=ctx2)
                self.product_turned("cin", h_hi, h_lo, 3 * DK // 2, w_in, w_out, dst=bcu)
                v = bcu[:].rearrange("p (g k t) -> p g k t", g=3, t=SEQ)
                b, c, u = v[:, 0], v[:, 1], v[:, 2]
                PAD = CONV_W - 1
                cu = self.tensor("cu", [P, DK, PAD + SEQ], ctx=ctx2)
                taps = self.tensor("taps", [P, CONV_W, DK], ctx=ctx2)
                with self.nc.Block() as block:
                    @block.sync
                    def _(sp):
                        sp.dma_start(taps[:], a["a_conv"].rearrange("w p k -> p w k")).then_inc(taps_sem.sem, 16)

                    @block.vector
                    def _(dve):
                        chain.link(dve, dve.memset(cu[:, :, 0:PAD], 0.0))
                        chain.link(dve, dve.tensor_tensor(cu[:, :, PAD:], c, u, ALU.mult))
                        dve.wait_ge(taps_sem.sem, taps_sem.base + 16)
                        for k in range(DK):
                            chain.link(dve, dve.tensor_scalar(c[:, k, :], cu[:, k, 0:SEQ], taps[:, 0, k:k + 1], None, ALU.mult))
                            for w in range(1, CONV_W):
                                chain.link(dve, dve.scalar_tensor_tensor(c[:, k, :], cu[:, k, w:w + SEQ], taps[:, w, k:k + 1],
                                                                         c[:, k, :], ALU.mult, ALU.add))
                        chain.link(dve, dve.tensor_tensor(b, b, c, ALU.mult))
                chain.close()
                taps_sem.base += 16
                self.split_rows("c", lambda k: b[:, k, :], h_hi, h_lo, DK)
            self.product_rows("cout", h_hi, h_lo, 4, w_out, next_src, self.add_to_x)

    def add_to_x(self, dve, nb, m, bank):
        at = self.x[:, m, bass.ds(nb * 512, 512)]
        return dve.tensor_tensor(at, at, bank, ALU.add)


    def ple(self, layer, next_src):
        a, nc = self.a, self.nc
        landed = self.counter("ple_landed")
        hi_n, lo_n, done, out, sig = (self.counter(n) for n in ("ple_hi", "ple_lo", "ple_done", "ple_out", "ple_sig"))
        KP = 2
        w_gate = lambda c: a["ple_wg"][layer][bass.ds(c, 1)].rearrange("a p n -> p a n")
        with ExitStack() as ctx:
            h_hi = self.tensor(f"h_hi_e{layer}", [P, DK, SEQ], F32R, ctx)
            h_lo = self.tensor(f"h_lo_e{layer}", [P, DK, SEQ], F32R, ctx)
            self.norm(f"e{layer}", 5 + layer, h_hi, h_lo)
            proj = self.tensor(f"proj{layer}", [P, TT, D], ctx=ctx)
            gate = self.tensor(f"gate{layer}", [P, TT, D], ctx=ctx)
            with ExitStack() as ctx2:
                t = lambda n, s, dt=F32: self.tensor(f"{n}{layer}", s, dt, ctx2)
                pt, pt_hi, pt_lo = t("pT", [P, KP, SEQ]), t("pT_hi", [P, KP, SEQ], F32R), t("pT_lo", [P, KP, SEQ], F32R)
                wp, wp_hi, wp_lo = t("wp", [P, KP, D]), t("wp_hi", [P, KP, D], F32R), t("wp_lo", [P, KP, D], F32R)
                bank = self.banks(f"pp{layer}", ctx2, 8)
                with nc.Block() as block:
                    @block.sync
                    def _(sp):
                        sp.dma_start(pt[:], a["p"][layer].rearrange("k p t -> p k t")).then_inc(landed.sem, 16)
                        sp.dma_start(wp[:], a["ple_wp"][layer].rearrange("k p n -> p k n")).then_inc(landed.sem, 16)

                    @block.scalar
                    def _(act):
                        act.wait_ge(landed.sem, landed.base + 32)
                        act.activation(pt_hi[:], pt[:], ACT.Copy).then_inc(hi_n.sem, 1)
                        act.activation(wp_hi[:], wp[:], ACT.Copy).then_inc(hi_n.sem, 1)

                    @block.vector
                    def _(dve):
                        dve.wait_ge(hi_n.sem, hi_n.base + 1)
                        dve.tensor_tensor(pt_lo[:], pt[:], pt_hi[:].bitcast(F32), ALU.subtract).then_inc(lo_n.sem, 1)
                        dve.wait_ge(hi_n.sem, hi_n.base + 2)
                        dve.tensor_tensor(wp_lo[:], wp[:], wp_hi[:].bitcast(F32), ALU.subtract).then_inc(lo_n.sem, 1)
                        for n in range(8):
                            dve.wait_ge(done.sem, done.base + n + 1)
                            m, nb = divmod(n, 2)
                            dve.tensor_copy(proj[:, m, nb * 512:(nb + 1) * 512], bank[n][:]).then_inc(out.sem, 1)
                        dve.wait_ge(out.sem, out.base + 8)

                    @block.tensor
                    def _(pe):
                        pe.wait_ge(lo_n.sem, lo_n.base + 2)
                        for n in range(8):
                            m, nb = divmod(n, 2)
                            for k in range(KP):
                                t_, w = slice(m * P, (m + 1) * P), slice(nb * 512, (nb + 1) * 512)
                                last = self.three(pe, bank[n][:], pt_hi[:, k, t_], pt_lo[:, k, t_], wp_hi[:, k, w], wp_lo[:, k, w],
                                                  k == 0, k == KP - 1)
                            last.then_inc(done.sem, 1)
                for s, n in ((landed, 32), (hi_n, 2), (lo_n, 2), (done, 8), (out, 8)):
                    s.base += n
            self.product_rows(f"e{layer}", h_hi, h_lo, 4, w_gate, next_src,
                              lambda dve, nb, m, bank: dve.tensor_copy(gate[:, m, bass.ds(nb * 512, 512)], bank))
            with nc.Block() as block:
                @block.scalar
                def _(act):
                    for m in range(TT):
                        act.activation(gate[:, m, :], gate[:, m, :], ACT.Sigmoid).then_inc(sig.sem, 1)

                @block.vector
                def _(dve):
                    for m in range(TT):
                        dve.wait_ge(sig.sem, sig.base + m + 1)
                        self.dve.link(dve, dve.tensor_tensor(gate[:, m, :], gate[:, m, :], proj[:, m, :], ALU.mult))
                        self.dve.link(dve, dve.tensor_tensor(self.x[:, m, :], self.x[:, m, :], gate[:, m, :], ALU.add))
            self.dve.close()
            sig.base += TT


    def rope_tables(self, ctx):
        nc, a, ch = self.nc, self.a, self.dve
        landed, const, folded, made = (self.counter(n) for n in ("pos_landed", "freq_ready", "angle_folded", "rope_made"))
        self.cos = self.tensor("rope_cos", [P, TT, HALF], ctx=ctx)
        self.sin = self.tensor("rope_sin", [P, TT, HALF], ctx=ctx)
        self.mask1 = self.tensor("mask_dilation1", [P, 2 * P], ctx=ctx)
        self.masks = [self.mask1] + [self.tensor(f"mask_dilation{d}", [P, SEQ], ctx=ctx) for d in DILATIONS[1:]]
        self.qk_gain = self.tensor("qk_gain", [P, 2, DH], ctx=ctx)
        freqs = (np.float32(1.0) / (np.float32(THETA) ** (np.arange(0, ROPE, 2, dtype=np.float32) / np.float32(ROPE)))).astype(np.float32)
        C1 = 6.28125
        C2 = float(np.float32(np.round((TWO_PI - C1) * 2 ** 21) / 2 ** 21))
        C3 = float(np.float32(TWO_PI - C1 - C2))
        MAGIC = 1.5 * 2 ** 23
        PI = float(np.nextafter(np.float32(np.pi), np.float32(0)))
        with ExitStack() as ctx2:
            t = lambda n, s, dt=F32: self.tensor(n, s, dt, ctx2)
            pos, posf, freq = t("pos", [P, TT], I32), t("pos_f", [P, TT]), t("freq", [P, HALF])
            ang, turns, fold = t("angle", [P, TT, HALF]), t("turns", [P, TT, HALF]), t("folded", [P, 2, TT, HALF])
            diff, dif2 = t("diff", [P, SEQ], I32), t("diff_mod", [P, SEQ], I32)
            with nc.Block() as block:
                @block.sync
                def _(sp):
                    sp.dma_start(pos[:], a["positions"]).then_inc(landed.sem, 16)
                    sp.dma_start(self.qk_gain[:, 0:1, :], a["k_norm"].partition_broadcast(P)).then_inc(landed.sem, 16)
                    sp.dma_start(self.qk_gain[:, 1:2, :], a["q_norm"].partition_broadcast(P)).then_inc(landed.sem, 16)
                    sp.wait_ge(landed.sem, landed.base + 48)

                @block.gpsimd
                def _(pool):
                    for j in range(HALF):
                        pool.memset(freq[:, j:j + 1], float(freqs[j])).then_inc(const.sem, 1)
                    pool.memset(self.mask1[:], 0.0).then_inc(const.sem, 1)
                    pool.iota(diff[:], pattern=[[-1, SEQ]], base=SEQ, channel_multiplier=1).then_inc(const.sem, 1)
                    pool.wait_ge(const.sem, const.base + HALF + 1)
                    pool.affine_select(out=self.mask1[:], in_=self.mask1[:], compare_op=ALU.is_ge, fill=LOWEST,
                                       base=P, pattern=[[-1, 2 * P]], channel_multiplier=1).then_inc(const.sem, 1)
                    pool.wait_ge(const.sem, const.base + HALF + 3)
                    pool.affine_select(out=self.mask1[:], in_=self.mask1[:], compare_op=ALU.is_ge, fill=LOWEST,
                                       base=0, pattern=[[1, 2 * P]], channel_multiplier=-1).then_inc(const.sem, 1)
                    for n in range(2):
                        mask = self.masks[n + 1]
                        pool.wait_ge(made.sem, made.base + n + 1)
                        pool.affine_select(out=mask[:], in_=mask[:], compare_op=ALU.is_ge, fill=LOWEST,
                                           base=SEQ - P, pattern=[[-1, SEQ]], channel_multiplier=1).then_inc(const.sem, 1)

                @block.vector
                def _(dve):
                    link = lambda ins: ch.link(dve, ins)
                    dve.wait_ge(const.sem, const.base + HALF + 2)
                    for n, d in enumerate(DILATIONS[1:]):
                        mask = self.masks[n + 1]
                        link(dve.tensor_scalar(dif2[:], diff[:], d - 1, None, ALU.bitwise_and))
                        link(dve.tensor_scalar(mask[:], dif2[:], 0.0, None, ALU.is_equal))
                        dve.tensor_scalar(mask[:], mask[:], -1.0, -LOWEST, ALU.add, ALU.mult).then_inc(made.sem, 1)
                    dve.wait_ge(landed.sem, landed.base + 48)
                    link(dve.tensor_copy(posf[:], pos[:]))
                    link(dve.tensor_tensor(ang[:], posf[:].unsqueeze(2).to_broadcast([P, TT, HALF]),
                                           freq[:].unsqueeze(1).to_broadcast([P, TT, HALF]), ALU.mult))
                    for n, quarter in enumerate((0.0, 0.25)):
                        f = fold[:, n]
                        link(dve.tensor_scalar(turns[:], ang[:], float(1 / TWO_PI), quarter, ALU.mult, ALU.add))
                        link(dve.tensor_scalar(turns[:], turns[:], MAGIC, None, ALU.add))
                        link(dve.tensor_scalar(turns[:], turns[:], -MAGIC, None, ALU.add))
                        link(dve.scalar_tensor_tensor(f, turns[:], -C1, ang[:], ALU.mult, ALU.add))
                        link(dve.scalar_tensor_tensor(f, turns[:], -C2, f, ALU.mult, ALU.add))
                        link(dve.scalar_tensor_tensor(f, turns[:], -C3, f, ALU.mult, ALU.add))
                        link(dve.tensor_scalar(f, f, float(quarter * TWO_PI), PI, ALU.add, ALU.min))
                        link(dve.tensor_scalar(f, f, -PI, None, ALU.max))
                    dve.sem_inc(folded.sem, 1)

                @block.scalar
                def _(act):
                    act.wait_ge(folded.sem, folded.base + 1)
                    act.activation(self.sin[:], fold[:, 0], ACT.Sin)
                    act.activation(self.cos[:], fold[:, 1], ACT.Sin)
            ch.close()
            for s, n in ((landed, 48), (const, HALF + 6), (folded, 1), (made, 2)):
                s.base += n

    def head_norm_rope(self, tag, buf, heads, gain):
        ch = self.dve
        sq, root_in, root = (self.counter(n) for n in ("head_squares", "head_root_in", "head_root"))
        with ExitStack() as ctx:
            t = lambda n, s: self.tensor(f"{n}_{tag}", s, F32, ctx)
            tmp = t("head_sq", [P, 2, heads * DH])
            st = t("head_stat", [P, 4, heads])
            rot = t("head_rot", [P, 4, heads, HALF])
            with self.nc.Block() as block:
                @block.scalar
                def _(act):
                    for m in range(TT):
                        if m >= 1:
                            act.wait_ge(root_in.sem, root_in.base + m)
                        act.activation(tmp[:, m % 2, :], buf[:, m, :], ACT.Square).then_inc(sq.sem, 1)
                        act.wait_ge(root_in.sem, root_in.base + m + 1)
                        act.activation(st[:, 3, :], st[:, 1, :], ACT.Sqrt).then_inc(root.sem, 1)

                @block.vector
                def _(dve):
                    link = lambda ins: ch.link(dve, ins)
                    for m in range(TT):
                        x3 = buf[:, m, :].rearrange("p (h d) -> p h d", d=DH)
                        ss, v, y, r = (st[:, n, :] for n in range(4))
                        dve.wait_ge(sq.sem, sq.base + m + 1)
                        link(dve.tensor_reduce(ss, tmp[:, m % 2, :].rearrange("p (h d) -> p h d", d=DH), AX_X, ALU.add))
                        dve.tensor_scalar(v, ss, 1.0 / DH, EPS, ALU.mult, ALU.add).then_inc(root_in.sem, 1)
                        self.rsqrt_steps(dve, lambda v, t: dve.wait_ge(root.sem, root.base + m + 1), v, y, r)
                        link(dve.tensor_tensor(x3, x3, y.unsqueeze(2).to_broadcast([P, heads, DH]), ALU.mult))
                        link(dve.tensor_tensor(x3, x3, gain.to_broadcast([P, heads, DH]), ALU.mult))
                        c = self.cos[:, m, :].unsqueeze(1).to_broadcast([P, heads, HALF])
                        s = self.sin[:, m, :].unsqueeze(1).to_broadcast([P, heads, HALF])
                        x1, x2 = x3[:, :, 0:HALF], x3[:, :, HALF:ROPE]
                        for n, (xx, w) in enumerate(((x1, c), (x2, s), (x2, c), (x1, s))):
                            link(dve.tensor_tensor(rot[:, n], xx, w, ALU.mult))
                        link(dve.tensor_tensor(x1, rot[:, 0], rot[:, 1], ALU.subtract))
                        link(dve.tensor_tensor(x2, rot[:, 2], rot[:, 3], ALU.add))
            ch.close()
            for s in (sq, root_in, root):
                s.base += TT

    def turn(self, tag, src, put_hi, put_lo=None):
        turned, hi_done, lo_done = (self.counter(n) for n in ("turn_turned", "turn_hi", "turn_lo"))
        last_done = lo_done if put_lo else hi_done
        with ExitStack() as ctx:
            bank = self.banks(f"turn_{tag}", ctx, 4)
            with self.nc.Block() as block:
                @block.scalar
                def _(act):
                    for k in range(DK):
                        act.wait_ge(turned.sem, turned.base + k + 1)
                        put_hi(act, k, bank[k % 4][:]).then_inc(hi_done.sem, 1)

                @block.vector
                def _(dve):
                    if put_lo:
                        for k in range(DK):
                            dve.wait_ge(hi_done.sem, hi_done.base + k + 1)
                            put_lo(dve, k, bank[k % 4][:]).then_inc(lo_done.sem, 1)

                @block.tensor
                def _(pe):
                    for k in range(DK):
                        if k >= 4:
                            pe.wait_ge(last_done.sem, last_done.base + k - 3)
                        for m in range(TT):
                            last = pe.transpose(bank[k % 4][:, m * P:(m + 1) * P], src[:, m, k * P:(k + 1) * P], self.ident[:])
                        last.then_inc(turned.sem, 1)
            turned.base += DK
            hi_done.base += DK
            if put_lo:
                lo_done.base += DK

    def attention_mixer(self, next_src):
        a = self.a
        part = lambda w: lambda c: w[bass.ds(c, 1)].rearrange("a p n -> p a n")
        wk, wv, wq, wo = part(a["w_k"]), part(a["w_v"]), part(a["b_w_q"]), part(a["b_w_o"])
        with ExitStack() as ctx:
            self.rope_tables(ctx)
            kT = self.tensor("kT", [P, KVH * SEQ], ctx=ctx)
            v_sb = self.tensor("v_sb", [P, TT, D], ctx=ctx)
            with ExitStack() as c2:
                h_hi = self.tensor("h_hi_kv", [P, DK, SEQ], F32R, c2)
                h_lo = self.tensor("h_lo_kv", [P, DK, SEQ], F32R, c2)
                self.norm("kv", 1, h_hi, h_lo)
                k_sb = self.tensor("k_sb", [P, TT, D], ctx=c2)
                copy_to = lambda dst: lambda dve, nb, m, bank: dve.tensor_copy(dst[:, m, bass.ds(nb * 512, 512)], bank)
                self.product_rows("k", h_hi, h_lo, 4, wk, wv, copy_to(k_sb))
                self.product_rows("v", h_hi, h_lo, 4, wv, wq, copy_to(v_sb))
                self.head_norm_rope("k", k_sb, KVH, self.qk_gain[:, 0:1, :])
                self.turn("k", k_sb, lambda act, k, bank: act.activation(kT[:, k * SEQ:(k + 1) * SEQ], bank, ACT.Copy))
            with ExitStack() as c2:
                q_sb = self.tensor("q_sb", [P, TT, GROUPS * D], ctx=c2)
                with ExitStack() as c3:
                    h_hi = self.tensor("h_hi_q", [P, DK, SEQ], F32R, c3)
                    h_lo = self.tensor("h_lo_q", [P, DK, SEQ], F32R, c3)
                    self.norm("q", 2, h_hi, h_lo)
                    self.product_rows("q", h_hi, h_lo, 12, wq, wo, copy_to(q_sb))
                self.head_norm_rope("q", q_sb, GROUPS * KVH, self.qk_gain[:, 1:2, :])
                o_sb = q_sb[:, :, 0:D]
                self.attend(q_sb, kT, v_sb, o_sb)
                h_hi = self.tensor("o_hi", [P, DK, SEQ], F32R, c2)
                h_lo = self.tensor("o_lo", [P, DK, SEQ], F32R, c2)
                self.turn("o", o_sb, lambda act, k, bank: act.activation(h_hi[:, k, :], bank, ACT.Copy),
                          lambda dve, k, bank: dve.tensor_tensor(h_lo[:, k, :], bank, h_hi[:, k, :].bitcast(F32), ALU.subtract))
                self.product_rows("o", h_hi, h_lo, 4, wo, next_src, self.add_to_x)

    def attend(self, q_sb, kT, v_sb, o_sb):
        nc, ch = self.nc, self.dve
        names = ("at_staged", "at_q_turned", "at_q_out", "at_scores", "at_masked", "at_max", "at_exp",
                 "at_weights", "at_w_turned", "at_w_out", "at_values", "at_out")
        staged, q_turned, q_out, scores, masked, maxed, exped, weights, w_turned, w_out, values, out = (self.counter(n) for n in names)
        with ExitStack() as ctx:
            t = lambda n, s: self.tensor(n, s, F32, ctx)
            qh = t("q_head", [P, TT, GROUPS, DH])
            qT = t("q_head_turned", [P, GROUPS, SEQ])
            S = t("scores_row", [P, 2, 2 * P + 2 * SEQ])
            W = t("weights_sum", [P, 2, SEQ])
            wT = t("weights_turned", [P, 2, SEQ])
            st = t("softmax_stat", [P, 4, TT])
            sets = [self.banks(f"s{r}_", ctx, GROUPS) for r in range(2)]
            w_bank, o_bank = self.banks("wv", ctx, 2)
            top, neg, den, inv = (st[:, n, :] for n in range(4))

            def spans(m):
                w = (m + 1) * P
                g0 = 0 if m else P
                return [(g0, 2 * P, g0), (2 * P, 2 * P + w, SEQ - w), (2 * P + w, 2 * P + 2 * w, SEQ - w)]

            with nc.Block() as block:
                @block.gpsimd
                def _(pool):
                    with pool.Fori(0, KVH) as h:
                        pool.wait_ge(q_turned.sem, h * GROUPS + q_turned.base)
                        for g in range(GROUPS):
                            last = pool.tensor_copy(qh[:, :, g, :], q_sb[:, :, bass.ds(h * DH + g * D, DH)])
                            last.then_inc(staged.sem, 1)

                @block.tensor
                def _(pe):
                    def score(h, m):
                        pe.wait_ge(masked.sem, h * TT + (masked.base + m - 1))
                        keys = max(m - 1, 0) * P
                        for g in range(GROUPS):
                            lo, hi, _ = spans(m)[g]
                            first = keys if g == 0 else 0
                            last = pe.matmul(sets[m % 2][g][:, 0:hi - lo], qT[:, g, m * P:(m + 1) * P],
                                             kT[:, bass.ds(h * SEQ + first, hi - lo)], start=True, stop=True)
                        last.then_inc(scores.sem, 1)

                    def value(h, m):
                        pe.wait_ge(weights.sem, h * TT + (weights.base + m + 1))
                        pe.wait_ge(w_out.sem, h * TT + (w_out.base + m))
                        for b in range(m + 1):
                            last = pe.transpose(w_bank[:, b * P:(b + 1) * P], W[:, m % 2, b * P:(b + 1) * P], self.ident[:])
                        last.then_inc(w_turned.sem, 1)
                        pe.wait_ge(w_out.sem, h * TT + (w_out.base + m + 1))
                        pe.wait_ge(out.sem, h * TT + (out.base + m))
                        for b in range(m + 1):
                            last = pe.matmul(o_bank[:, 0:DH], wT[:, m % 2, b * P:(b + 1) * P],
                                             v_sb[:].rearrange("p m d -> p (m d)")[:, bass.ds(h * DH + b * D, DH)],
                                             start=b == 0, stop=b == m)
                        last.then_inc(values.sem, 1)

                    with pe.Fori(0, KVH) as h:
                        pe.wait_ge(masked.sem, h * TT + masked.base)
                        for g in range(GROUPS):
                            pe.wait_ge(staged.sem, h * GROUPS + (staged.base + g + 1))
                            for m in range(TT):
                                last = pe.transpose(sets[1][g][:, m * P:(m + 1) * P], qh[:, m, g, :], self.ident[:])
                            last.then_inc(q_turned.sem, 1)
                        pe.wait_ge(q_out.sem, h * GROUPS + (q_out.base + GROUPS))
                        score(h, 0)
                        score(h, 1)
                        for m in range(TT):
                            if m + 2 < TT:
                                score(h, m + 2)
                            value(h, m)

                @block.scalar
                def _(act):
                    def exp(h, m):
                        act.wait_ge(maxed.sem, h * TT + (maxed.base + m + 1))
                        lo, hi = spans(m)[0][0], spans(m)[2][1]
                        act.activation(S[:, m % 2, lo:hi], S[:, m % 2, lo:hi], ACT.Exp, bias=neg[:, m:m + 1],
                                       accum_out=den[:, m:m + 1]).then_inc(exped.sem, 1)

                    def turned(h, m):
                        act.wait_ge(w_turned.sem, h * TT + (w_turned.base + m + 1))
                        act.wait_ge(values.sem, h * TT + (values.base + m - 1))
                        act.activation(wT[:, m % 2, 0:(m + 1) * P], w_bank[:, 0:(m + 1) * P], ACT.Copy).then_inc(w_out.sem, 1)

                    with act.Fori(0, KVH) as h:
                        act.wait_ge(scores.sem, h * TT + scores.base)
                        for g in range(GROUPS):
                            act.wait_ge(q_turned.sem, h * GROUPS + (q_turned.base + g + 1))
                            act.activation(qT[:, g, :], sets[1][g][:], ACT.Copy).then_inc(q_out.sem, 1)
                        exp(h, 0)
                        exp(h, 1)
                        for m in range(TT):
                            turned(h, m)
                            if m + 2 < TT:
                                exp(h, m + 2)

                @block.vector
                def _(dve):
                    link = lambda ins: ch.link(dve, ins)

                    def mask(h, m):
                        dve.wait_ge(scores.sem, h * TT + (scores.base + m + 1))
                        dve.wait_ge(weights.sem, h * TT + (weights.base + m - 1))
                        for g in range(GROUPS):
                            lo, hi, at = spans(m)[g]
                            last = dve.scalar_tensor_tensor(S[:, m % 2, lo:hi], sets[m % 2][g][:, 0:hi - lo], DH ** -0.5,
                                                            self.masks[g][:, at:at + hi - lo], ALU.mult, ALU.add)
                            if g < GROUPS - 1:
                                link(last)
                        last.then_inc(masked.sem, 1)
                        dve.wait_ge(masked.sem, h * TT + (masked.base + m + 1))
                        link(dve.tensor_reduce(top[:, m:m + 1], S[:, m % 2, spans(m)[0][0]:spans(m)[2][1]], AX_X, ALU.max))
                        dve.tensor_scalar(neg[:, m:m + 1], top[:, m:m + 1], -1.0, None, ALU.mult).then_inc(maxed.sem, 1)

                    def weigh(h, m):
                        dve.wait_ge(exped.sem, h * TT + (exped.base + m + 1))
                        dve.wait_ge(out.sem, h * TT + (out.base + m + 1 - TT))
                        link(dve.reciprocal(inv[:, m:m + 1], den[:, m:m + 1]))
                        dve.wait_ge(w_turned.sem, h * TT + (w_turned.base + m - 1))
                        row = S[:, m % 2, :]
                        sp0, sp1, sp2 = spans(m)
                        link(dve.tensor_tensor(W[:, m % 2, 0:(m + 1) * P], row[:, sp1[0]:sp1[1]], row[:, sp2[0]:sp2[1]], ALU.add))
                        at = W[:, m % 2, max(m - 1, 0) * P:(m + 1) * P]
                        dve.tensor_tensor(at, at, row[:, sp0[0]:sp0[1]], ALU.add).then_inc(weights.sem, 1)

                    def put(h, m):
                        dve.wait_ge(values.sem, h * TT + (values.base + m + 1))
                        dve.tensor_scalar(o_sb[:, m, bass.ds(h * DH, DH)], o_bank[:, 0:DH], inv[:, m:m + 1], None,
                                          ALU.mult).then_inc(out.sem, 1)

                    with dve.Fori(0, KVH) as h:
                        ch.close()
                        mask(h, 0)
                        mask(h, 1)
                        for m in range(TT):
                            weigh(h, m)
                            if m + 2 < TT:
                                mask(h, m + 2)
                            if m:
                                put(h, m - 1)
                        put(h, TT - 1)
                        ch.rewind(dve)
                    dve.wait_ge(out.sem, out.base + TT * KVH)
            for s, n in ((staged, GROUPS * KVH), (q_turned, GROUPS * KVH), (q_out, GROUPS * KVH)) + tuple(
                    (s, TT * KVH) for s in (scores, masked, maxed, exped, weights, w_turned, w_out, values, out)):
                s.base += n

    def finish(self, out):
        stored = self.counter("x_stored")
        with self.nc.Block() as block:
            @block.sync
            def _(sp):
                sp.dma_start(out.rearrange("(t p) d -> p t d", p=P), self.x[:]).then_inc(stored.sem, 16)
                sp.wait_ge(stored.sem, 16)


def build(nc, a, out):
    with ExitStack() as ctx:
        k = Kernel(nc, ctx, a)
        first = lambda w: lambda c: w[bass.ds(c, 1)].rearrange("a p n -> p a n")
        k.setup(first(a["a_w_in"]))
        k.conv_mixer(first(a["peer_wq"][0]))
        k.peer(0, first(a["ple_wg"][0]))
        k.ple(0, first(a["w_k"]))
        k.attention_mixer(first(a["peer_wq"][1]))
        k.peer(1, first(a["ple_wg"][1]))
        k.ple(1, None)
        k.finish(out)


def slices_turned(w):
    n = w.shape[-1] // (2 * P)
    return np.ascontiguousarray(w.reshape(DK, P, n, 2, P).transpose(2, 1, 3, 0, 4)).reshape(n, P, CHUNK)


def slices_rows(w):
    n = w.shape[-1] // 512
    return np.ascontiguousarray(w.reshape(2, DK // 2, P, n, 512).transpose(3, 0, 2, 1, 4)).reshape(2 * n, P, CHUNK)


def kernel(x, p, positions, a_norm, a_w_in, a_conv, a_w_out, kv_norm, w_kv, k_norm, b_norm, b_w_q, q_norm, b_w_o,
           ffn_norm, peer_w_q, peer_sub_keys, peer_u, peer_v, ple_norm, ple_w_gate, ple_w_proj):
    import concourse.bacc as bacc
    from concourse.bass_utils import run_bass_kernel_spmd

    f = np.asarray
    column = lambda g: f(g).reshape(DK, P).T
    layers = range(2)
    arrays = {
        "x": f(x)[0],
        "p": np.stack([np.ascontiguousarray(f(p)[i, 0].T).reshape(2, P, SEQ) for i in layers]),
        "positions": np.ascontiguousarray(f(positions).reshape(TT, P).T),
        "gains": np.stack([column(g) for g in (f(a_norm)[0], kv_norm, f(b_norm)[0], f(ffn_norm)[0], f(ffn_norm)[1],
                                               f(ple_norm)[0], f(ple_norm)[1])]),
        "a_w_in": slices_turned(f(a_w_in)[0]),
        "a_conv": np.ascontiguousarray(f(a_conv)[0].reshape(CONV_W, DK, P).transpose(0, 2, 1)),
        "a_w_out": slices_rows(f(a_w_out)[0]),
        "w_k": slices_rows(f(w_kv)[:, :D]),
        "w_v": slices_rows(f(w_kv)[:, D:]),
        "k_norm": f(k_norm).reshape(1, DH),
        "q_norm": f(q_norm).reshape(1, DH),
        "b_w_q": slices_rows(f(b_w_q)[0]),
        "b_w_o": slices_rows(f(b_w_o)[0]),
        "peer_wq": np.stack([slices_turned(f(peer_w_q)[i]) for i in layers]),
        "peer_keys": np.ascontiguousarray(f(peer_sub_keys).reshape(2, 2 * PH, NKEY, P).transpose(0, 3, 1, 2)),
        "peer_u": np.stack([np.ascontiguousarray(f(peer_u)[i].reshape(NKEY, NKEY, DK, P).transpose(1, 3, 2, 0))
                            .reshape(NKEY, P, DK * NKEY) for i in layers]),
        "peer_v": f(peer_v),
        "ple_wg": np.stack([slices_rows(f(ple_w_gate)[i]) for i in layers]),
        "ple_wp": f(ple_w_proj).reshape(2, 2, P, D),
    }
    nc = bacc.Bacc("TRN2", target_bir_lowering=False, num_devices=1)
    ins, aps = {}, {}
    for name, value in arrays.items():
        value = np.ascontiguousarray(value)
        ins[f"in_{name}"] = value
        aps[name] = nc.dram_tensor(f"in_{name}", value.shape, mybir.dt.from_np(value.dtype), kind="ExternalInput").ap()
    out = nc.dram_tensor("out_x", (SEQ, D), F32, kind="ExternalOutput").ap()
    build(nc, aps, out)
    r = run_bass_kernel_spmd(nc, [ins], core_ids=[0])
    return r.results[0]["out_x"].reshape(1, SEQ, D)
```

```python
from contextlib import ExitStack

import numpy as np

import concourse.bass as bass
from concourse import mybir

P = 128
ALU = mybir.AluOpType
ACT = mybir.ActivationFunctionType
F32 = mybir.dt.float32
F32R = mybir.dt.float32r
BF16 = mybir.dt.bfloat16
I32 = mybir.dt.int32
U32 = mybir.dt.uint32
AX_X = mybir.AxisListType.X

D = 1024
SEQ = 512
TT = SEQ // P
DK = D // P
CONV_W = 3
DH = 128
KVH = D // DH
GROUPS = 3
DILATIONS = (1, 4, 16)
ROPE = DH // 4
HALF = ROPE // 2
THETA = 500000.0
PH = 8
NKEY = 128
TOPK = 16
NSEL = PH * TOPK
UNITS = TT * PH
EPS = 1e-6
LOWEST = -3.0e38
CHUNK = 2048
RAW = 4
SPLIT = 2
BODY = 4
CREDITS = 32
GT = 32
QUAD = 4
TWO_PI = 2.0 * np.pi


class Counter:

    def __init__(self, sem, credits=0):
        self.sem = sem
        self.base = credits


class Chain:

    def __init__(self, counter):
        self.counter = counter
        self.n = 0

    def link(self, eng, ins):
        ins.then_inc(self.counter.sem, 1)
        self.n += 1
        eng.wait_ge(self.counter.sem, self.counter.base + self.n)

    def close(self):
        self.counter.base += self.n
        self.n = 0

    def rewind(self, eng):
        eng.sem_inc(self.counter.sem, -self.n)
        self.n = 0


class Kernel:
    def __init__(self, nc, ctx, a):
        self.nc, self.ctx, self.a = nc, ctx, a
        self.counters = {}
        self.raw = self.tensor("raw", [P, RAW, CHUNK])
        self.chunks = 0
        self.raw_landed = [self.counter(f"raw_landed{s}").sem for s in range(RAW)]
        self.hi_ready = self.counter("hi_ready").sem
        self.lo_ready = self.counter("lo_ready").sem
        for name in ("turned_done", "turned_out", "rows_done", "rows_out", "ring_stored0", "ring_stored1",
                     "quad_done", "quad_out", "hot2_ready", "gates_stored0", "gates_stored1", "ys_done", "ys_added", "at_q_turned", "at_scores",
                     "at_masked", "at_w_turned", "at_w_out", "at_values", "at_out", "at_weights"):
            self.counter(name, CREDITS)
        self.x = self.tensor("x_res", [P, TT, D])
        self.ident = self.tensor("ident", [P, P])
        self.zero = self.tensor("zero", [P, 1])
        self.gains = self.tensor("gains", [P, 7, DK])
        self.iota = self.tensor("iota", [P, P])
        self.acts = nc.dram_tensor("expert_acts", (NKEY, P, SEQ), F32, kind="Internal").ap()
        self.gates = nc.dram_tensor("expert_gates", (SEQ // GT, P, NKEY, GT), F32, kind="Internal").ap()
        self.dve = Chain(self.counter("dve_step"))

    def counter(self, name, credits=0):
        if name not in self.counters:
            self.counters[name] = Counter(self.ctx.enter_context(self.nc.semaphore(name)), credits)
        return self.counters[name]

    def tensor(self, name, shape, dt=F32, ctx=None):
        return (ctx or self.ctx).enter_context(self.nc.sbuf_tensor(name, shape, dt))

    def banks(self, name, ctx, n, shape=(P, 512), dt=F32):
        return [ctx.enter_context(self.nc.psum_tensor(f"{name}{b}", list(shape), dt)) for b in range(n)]


    def load_chunk(self, sp, src, i, k):
        slot = (self.chunks + k) % RAW
        sp.wait_ge(self.lo_ready, i * BODY + (self.chunks + k + 1))
        out = self.raw[:, slot, :]
        if len(src.shape) == 3:
            out = out.rearrange("p (b n) -> p b n", b=src.shape[1])
        sp.dma_start(out, src).then_inc(self.raw_landed[slot], 16)

    def load_rest(self, sp, total, src):
        if total > RAW:
            with sp.Fori(0, total // BODY - 1) as i:
                for k in range(BODY):
                    self.load_chunk(sp, src(i * BODY + (k + RAW)), i, k + RAW)

    def load_first(self, sp, done, src):
        if src is None:
            return
        for k in range(RAW):
            slot = (self.chunks + done + k) % RAW
            sp.wait_ge(self.lo_ready, self.chunks + done + k + 1)
            s = src(k)
            out = self.raw[:, slot, :]
            if len(s.shape) == 3:
                out = out.rearrange("p (b n) -> p b n", b=s.shape[1])
            sp.dma_start(out, s).then_inc(self.raw_landed[slot], 16)

    def split_hi(self, act, used, i, k):
        c = self.chunks + k
        act.wait_ge(self.raw_landed[c % RAW], i * (16 * (BODY // RAW)) + 16 * (c // RAW + 1))
        products, per = used
        act.wait_ge(products.sem, i * (BODY * per) + (products.base + (k + 1 - SPLIT) * per))
        act.activation(self.hi[:, c % SPLIT, :], self.raw[:, c % RAW, :], ACT.Copy).then_inc(self.hi_ready, 1)

    def split_lo(self, dve, i, k):
        c = self.chunks + k
        dve.wait_ge(self.hi_ready, i * BODY + (c + 1))
        dve.tensor_tensor(self.lo[:, c % SPLIT, :], self.raw[:, c % RAW, :],
                          self.hi[:, c % SPLIT, :].bitcast(F32), ALU.subtract).then_inc(self.lo_ready, 1)

    def chunk_split(self, pe, i, k):
        pe.wait_ge(self.lo_ready, i * BODY + (self.chunks + k + 1 + RAW))

    def ahead(self, eng, total, lead, follow):
        trips = total // BODY
        lead(0, 0)
        if trips > 1:
            with eng.Fori(0, trips - 1) as i:
                for k in range(BODY):
                    lead(i, k + 1)
                    follow(i, k)
        for k in range(BODY):
            if k + 1 < BODY:
                lead(trips - 1, k + 1)
            follow(trips - 1, k)

    def split_tensors(self, ctx, tag):
        self.hi = self.tensor(f"w_hi_{tag}", [P, SPLIT, CHUNK], F32R, ctx)
        self.lo = self.tensor(f"w_lo_{tag}", [P, SPLIT, CHUNK], F32R, ctx)

    def three(self, pe, out, lhi, llo, rhi, rlo, first, last):
        pe.matmul(out, lhi, rhi, start=first, stop=False)
        pe.matmul(out, lhi, rlo, start=False, stop=False)
        return pe.matmul(out, llo, rhi, start=False, stop=last)


    def setup(self, first_src):
        a, nc = self.a, self.nc
        const = self.counter("const_ready")
        landed = self.counter("setup_landed")
        iota_i = self.tensor("iota_int", [P, P], I32)
        with nc.Block() as block:
            @block.sync
            def _(sp):
                sp.sem_inc(self.lo_ready, RAW)
                sp.dma_start(self.x[:], a["x"].rearrange("(t p) d -> p t d", p=P)).then_inc(landed.sem, 16)
                sp.dma_start(self.gains[:], a["gains"].rearrange("g p k -> p g k")).then_inc(landed.sem, 16)
                self.load_first(sp, 0, first_src)
                sp.wait_ge(landed.sem, 32)

            @block.scalar
            def _(act):
                for counter in self.counters.values():
                    if counter.base:
                        act.sem_inc(counter.sem, counter.base)

            @block.gpsimd
            def _(pool):
                pool.memset(self.zero[:], 0.0).then_inc(const.sem, 1)
                pool.memset(self.ident[:], 0.0).then_inc(const.sem, 1)
                pool.iota(iota_i[:], pattern=[[1, P]], base=0, channel_multiplier=0).then_inc(const.sem, 1)
                pool.wait_ge(const.sem, 3)
                pool.tensor_copy(self.iota[:], iota_i[:]).then_inc(const.sem, 1)
                pool.affine_select(out=self.ident[:], in_=self.ident[:], compare_op=ALU.not_equal, fill=1.0,
                                   base=0, pattern=[[-1, P]], channel_multiplier=1).then_inc(const.sem, 1)
        const.base += 5
        landed.base += 32


    def rsqrt_steps(self, dve, act_sqrt, v, y, t):
        ch = self.dve
        act_sqrt(v, t)
        ch.link(dve, dve.reciprocal(y, t))
        ch.link(dve, dve.tensor_tensor(t, y, y, ALU.mult))
        ch.link(dve, dve.tensor_tensor(t, t, v, ALU.mult))
        ch.link(dve, dve.tensor_scalar(t, t, -0.5, 1.5, ALU.mult, ALU.add))
        ch.link(dve, dve.tensor_tensor(y, y, t, ALU.mult))

    def norm(self, tag, gain, h_hi, h_lo):
        nc = self.nc
        sq = self.counter("norm_squares")
        root_in = self.counter("norm_root_in")
        root = self.counter("norm_root")
        scaled = self.counter("norm_scaled")
        turned = self.counter("norm_turned")
        hi_done = self.counter("norm_hi")
        lo_done = self.counter("norm_lo")
        with ExitStack() as ctx:
            xn = self.tensor(f"xn_{tag}", [P, TT, D], ctx=ctx)
            junk = self.tensor(f"junk_{tag}", [P, D], ctx=ctx)
            st = self.tensor(f"stat_{tag}", [P, 4, TT], ctx=ctx)
            bank = self.banks(f"turn_{tag}", ctx, 4)
            ss, v, y, t = (st[:, n, :] for n in range(4))
            g = self.gains[:, gain, :]
            with nc.Block() as block:
                @block.scalar
                def _(act):
                    for m in range(TT):
                        if m:
                            act.wait_ge(sq.sem, sq.base + m)
                        act.activation(junk[:], self.x[:, m, :], ACT.Square, accum_out=ss[:, m:m + 1]).then_inc(sq.sem, 1)
                    act.wait_ge(root_in.sem, root_in.base + 1)
                    act.activation(t, v, ACT.Sqrt).then_inc(root.sem, 1)
                    for k in range(DK):
                        act.wait_ge(turned.sem, turned.base + k + 1)
                        act.activation(h_hi[:, k, :], bank[k % 4][:], ACT.Copy, scale=g[:, k:k + 1]).then_inc(hi_done.sem, 1)

                @block.vector
                def _(dve):
                    dve.wait_ge(sq.sem, sq.base + TT)
                    dve.tensor_scalar(v, ss, 1.0 / D, EPS, ALU.mult, ALU.add).then_inc(root_in.sem, 1)
                    self.rsqrt_steps(dve, lambda v, t: dve.wait_ge(root.sem, root.base + 1), v, y, t)
                    for m in range(TT):
                        dve.tensor_scalar(xn[:, m, :], self.x[:, m, :], y[:, m:m + 1], None, ALU.mult).then_inc(scaled.sem, 1)
                    for k in range(DK):
                        dve.wait_ge(hi_done.sem, hi_done.base + k + 1)
                        dve.scalar_tensor_tensor(h_lo[:, k, :], bank[k % 4][:], g[:, k:k + 1], h_hi[:, k, :].bitcast(F32),
                                                 ALU.mult, ALU.subtract).then_inc(lo_done.sem, 1)
                    dve.wait_ge(lo_done.sem, lo_done.base + DK)

                @block.tensor
                def _(pe):
                    pe.wait_ge(scaled.sem, scaled.base + TT)
                    for k in range(DK):
                        if k >= 4:
                            pe.wait_ge(lo_done.sem, lo_done.base + k - 3)
                        for m in range(TT):
                            last = pe.transpose(bank[k % 4][:, m * P:(m + 1) * P], xn[:, m, k * P:(k + 1) * P], self.ident[:])
                        last.then_inc(turned.sem, 1)
            self.dve.close()
            for s, n in ((sq, TT), (root_in, 1), (root, 1), (scaled, TT), (turned, DK), (hi_done, DK), (lo_done, DK)):
                s.base += n

    def split_rows(self, tag, src_slice, h_hi, h_lo, nk):
        hi_done = self.counter("rows_hi")
        lo_done = self.counter("rows_lo")
        with self.nc.Block() as block:
            @block.scalar
            def _(act):
                for k in range(nk):
                    act.activation(h_hi[:, k, :], src_slice(k), ACT.Copy).then_inc(hi_done.sem, 1)

            @block.vector
            def _(dve):
                for k in range(nk):
                    dve.wait_ge(hi_done.sem, hi_done.base + k + 1)
                    dve.tensor_tensor(h_lo[:, k, :], src_slice(k), h_hi[:, k, :].bitcast(F32), ALU.subtract).then_inc(lo_done.sem, 1)
                dve.wait_ge(lo_done.sem, lo_done.base + nk)
        hi_done.base += nk
        lo_done.base += nk


    def loop_chunks(self, eng, total, chunk):
        trips = total // BODY
        if trips > 1:
            with eng.Fori(0, trips) as i:
                for k in range(BODY):
                    chunk(i, k)
        else:
            for k in range(total):
                chunk(0, k)

    def turned_chunk(self, pe, bank, h_hi, h_lo, done, out, i, k):
        self.chunk_split(pe, i, k)
        s = (self.chunks + k) % SPLIT
        for b in range(2):
            n = 2 * k + b
            pe.wait_ge(out.sem, i * (2 * BODY) + (out.base + n - 3))
            for kk in range(DK):
                w = slice((b * DK + kk) * P, (b * DK + kk + 1) * P)
                last = self.three(pe, bank[n % 4][:], self.hi[:, s, w], self.lo[:, s, w],
                                  h_hi[:, kk, :], h_lo[:, kk, :], kk == 0, kk == DK - 1)
            last.then_inc(done.sem, 1)

    def product_turned(self, tag, h_hi, h_lo, total, src, next_src, dst):
        done = self.counter("turned_done")
        out = self.counter("turned_out")
        with ExitStack() as ctx:
            self.split_tensors(ctx, tag)
            bank = self.banks(f"acc_{tag}", ctx, 4)
            with self.nc.Block() as block:
                @block.sync
                def _(sp):
                    self.load_rest(sp, total, src)
                    self.load_first(sp, total, next_src)

                @block.scalar
                def _(act):
                    def evacuate(i, k):
                        for b in range(2):
                            n = 2 * k + b
                            act.wait_ge(done.sem, i * (2 * BODY) + (done.base + n + 1))
                            at = (i * (2 * BODY) + n) * SEQ
                            act.activation(dst[:, bass.ds(at, SEQ)], bank[n % 4][:], ACT.Copy).then_inc(out.sem, 1)
                    self.ahead(act, total, lambda i, k: self.split_hi(act, (done, 2), i, k), evacuate)
                    act.wait_ge(out.sem, out.base + 2 * total)

                @block.vector
                def _(dve):
                    self.loop_chunks(dve, total, lambda i, k: self.split_lo(dve, i, k))

                @block.tensor
                def _(pe):
                    self.loop_chunks(pe, total, lambda i, k: self.turned_chunk(pe, bank, h_hi, h_lo, done, out, i, k))
            done.base += 2 * total
            out.base += 2 * total
            self.chunks += total

    def product_rows(self, tag, h_hi, h_lo, total, src, next_src, finish):
        done = self.counter("rows_done")
        out = self.counter("rows_out")
        with ExitStack() as ctx:
            self.split_tensors(ctx, tag)
            bank = self.banks(f"acc_{tag}", ctx, 8)
            with self.nc.Block() as block:
                @block.sync
                def _(sp):
                    self.load_rest(sp, total, src)
                    self.load_first(sp, total, next_src)

                @block.scalar
                def _(act):
                    self.loop_chunks(act, total, lambda i, k: self.split_hi(act, (done, TT), i, k))

                @block.vector
                def _(dve):
                    def evacuate(i, k):
                        if k % 2:
                            for m in range(TT):
                                dve.wait_ge(done.sem, i * (TT * BODY) + (done.base + TT * k + m + 1))
                                finish(dve, i * (BODY // 2) + k // 2, m, bank[(k // 2) % 2 * TT + m][:]).then_inc(out.sem, 1)
                    self.ahead(dve, total, lambda i, k: self.split_lo(dve, i, k), evacuate)
                    dve.wait_ge(out.sem, out.base + total * TT // 2)

                @block.tensor
                def _(pe):
                    def chunk(i, k):
                        self.chunk_split(pe, i, k)
                        s = (self.chunks + k) % SPLIT
                        for m in range(TT):
                            if k % 2 == 0:
                                pe.wait_ge(out.sem, i * (TT * BODY // 2) + (out.base + (k // 2 - 2) * TT + m + 1))
                            for kk in range(DK // 2):
                                w = slice(kk * 512, (kk + 1) * 512)
                                h = k % 2 * (DK // 2) + kk
                                t = slice(m * P, (m + 1) * P)
                                last = self.three(pe, bank[(k // 2) % 2 * TT + m][:], h_hi[:, h, t], h_lo[:, h, t],
                                                  self.hi[:, s, w], self.lo[:, s, w], h == 0, h == DK - 1)
                            last.then_inc(done.sem, 1)
                    self.loop_chunks(pe, total, chunk)
            done.base += TT * total
            out.base += TT * total // 2
            self.chunks += total


    def peer(self, layer, next_src):
        a = self.a
        wq = a["peer_wq"][layer]
        u = a["peer_u"][layer]
        v = a["peer_v"][layer].rearrange("(i1 i2) d -> i1 i2 d", i2=NKEY)
        wq_src = lambda c: wq[bass.ds(c, 1)].rearrange("a p n -> p a n")
        u_src = lambda c: u[bass.ds(c * 2, 2)].rearrange("b p n -> p b n")
        with ExitStack() as ctx:
            h_hi = self.tensor(f"h_hi_p{layer}", [P, DK, SEQ], F32R, ctx)
            h_lo = self.tensor(f"h_lo_p{layer}", [P, DK, SEQ], F32R, ctx)
            self.norm(f"p{layer}", 3 + layer, h_hi, h_lo)
            sub = self.tensor(f"sub{layer}", [P, UNITS * 2 * NKEY], ctx=ctx)
            with ExitStack() as q_ctx:
                qT = self.tensor(f"qT{layer}", [P, 2 * PH * SEQ], ctx=q_ctx)
                self.product_turned(f"pq{layer}", h_hi, h_lo, PH, wq_src, u_src, qT)
                self.sub_scores(layer, qT, sub)
            self.expert_acts(layer, h_hi, h_lo, u_src, sub, v)
        self.expert_sum(layer, v, next_src)

    def v_src(self, v):
        return lambda g, k: v[:, bass.ds(g * 8 + 4 * (k % 2), 4), 512 * (k // 2):512 * (k // 2) + 512]

    def sub_scores(self, layer, qT, sub):
        keys_sem = self.counter("keys_landed")
        done = self.counter("sub_done")
        out = self.counter("sub_out")
        fills = UNITS // 2
        with ExitStack() as ctx:
            keys = self.tensor(f"keys{layer}", [P, 2 * PH, NKEY], ctx=ctx)
            bank = self.banks(f"sub_acc{layer}", ctx, 4)
            with self.nc.Block() as block:
                @block.sync
                def _(sp):
                    sp.dma_start(keys[:], self.a["peer_keys"][layer]).then_inc(keys_sem.sem, 16)

                @block.scalar
                def _(act):
                    for n in range(fills):
                        act.wait_ge(done.sem, done.base + n + 1)
                        act.activation(sub[:, n * 512:(n + 1) * 512], bank[n % 4][:], ACT.Copy).then_inc(out.sem, 1)
                    act.wait_ge(out.sem, out.base + fills)

                @block.tensor
                def _(pe):
                    pe.wait_ge(keys_sem.sem, keys_sem.base + 16)
                    for n in range(fills):
                        m, pair = divmod(n, PH // 2)
                        if n >= 4:
                            pe.wait_ge(out.sem, out.base + n - 3)
                        for j in range(4):
                            hp = pair * 4 + j
                            last = pe.matmul(bank[n % 4][:, j * NKEY:(j + 1) * NKEY],
                                             qT[:, hp * SEQ + m * P:hp * SEQ + (m + 1) * P], keys[:, hp, :],
                                             start=True, stop=True)
                        last.then_inc(done.sem, 1)
            keys_sem.base += 16
            done.base += fills
            out.base += fills

    def router(self, ctx, layer, sub, best, picks):
        s = self.tensor(f"scores{layer}", [P, 2, NKEY], ctx=ctx)
        s2 = self.tensor(f"scores_less_8{layer}", [P, 2, NKEY], ctx=ctx)
        vals = self.tensor(f"vals{layer}", [P, 2, TOPK], ctx=ctx)
        idx = self.tensor(f"idx{layer}", [P, 2, TOPK], U32, ctx)
        idxf = self.tensor(f"idxf{layer}", [P, 2, TOPK], ctx=ctx)
        cand = self.tensor(f"cand{layer}", [P, TOPK * TOPK], ctx=ctx)
        cand2 = self.tensor(f"cand_less_8{layer}", [P, TOPK * TOPK], ctx=ctx)
        top = self.tensor(f"top{layer}", [P, TOPK], ctx=ctx)
        pos = self.tensor(f"pos{layer}", [P, TOPK], U32, ctx)
        posij = self.tensor(f"posij{layer}", [P, 2, TOPK], U32, ctx)
        posf = self.tensor(f"posf{layer}", [P, 2, TOPK], ctx=ctx)
        hot = self.tensor(f"hot{layer}", [P, 2, TOPK, TOPK], ctx=ctx)
        hot2 = self.tensor(f"hot_times_key{layer}", [P, 2, TOPK, TOPK], ctx=ctx)

        def top16(dve, link, values, rest, v16, i16):
            link(dve, dve.max(v16[:, 0:8], values))
            link(dve, dve.max_index(i16[:, 0:8], v16[:, 0:8], values))
            link(dve, dve.match_replace(rest, v16[:, 0:8], values, LOWEST))
            link(dve, dve.max(v16[:, 8:16], rest))
            link(dve, dve.max_index(i16[:, 8:16], v16[:, 8:16], rest))

        def one(dve, unit):
            link = self.dve.link
            link(dve, dve.tensor_copy(s[:].rearrange("p a k -> p (a k)"), sub[:, bass.ds(unit * (2 * NKEY), 2 * NKEY)]))
            for half in range(2):
                top16(dve, link, s[:, half, :], s2[:, half, :], vals[:, half, :], idx[:, half, :])
            link(dve, dve.tensor_copy(idxf[:], idx[:]))
            link(dve, dve.tensor_tensor(cand[:].rearrange("p (i j) -> p i j", i=TOPK),
                                        vals[:, 0, :].unsqueeze(2).to_broadcast([P, TOPK, TOPK]),
                                        vals[:, 1, :].unsqueeze(1).to_broadcast([P, TOPK, TOPK]), ALU.add))
            top16(dve, link, cand[:], cand2[:], top[:], pos[:])
            link(dve, dve.tensor_scalar(posij[:, 0, :], pos[:], 4, None, ALU.logical_shift_right))
            link(dve, dve.tensor_scalar(posij[:, 1, :], pos[:], TOPK - 1, None, ALU.bitwise_and))
            link(dve, dve.tensor_copy(posf[:], posij[:]))
            link(dve, dve.tensor_tensor(hot[:].rearrange("p a s c -> p (a s) c"),
                                        posf[:].rearrange("p a s -> p (a s)").unsqueeze(2).to_broadcast([P, 2 * TOPK, TOPK]),
                                        self.iota[:, 0:TOPK].unsqueeze(1).to_broadcast([P, 2 * TOPK, TOPK]), ALU.is_equal))
            for half in range(2):
                link(dve, dve.tensor_tensor(hot2[:, half], hot[:, half],
                                            idxf[:, half, :].unsqueeze(1).to_broadcast([P, TOPK, TOPK]), ALU.mult))
            link(dve, dve.tensor_reduce(picks[:, :, bass.ds(unit * TOPK, TOPK)], hot2[:], AX_X, ALU.add))
            link(dve, dve.tensor_copy(best[:, bass.ds(unit, 1), :].rearrange("p a s -> p (a s)"), top[:]))

        return one

    def expert_acts(self, layer, h_hi, h_lo, u_src, sub, v):
        c = self.counter
        total = NKEY // 2
        half = total // BODY // 2
        done, out = c("turned_done"), c("turned_out")
        ring_sem = [c(f"ring_stored{r}") for r in range(2)]
        routed, exped, gated, turned_n, turned_out, rounded, g_lo_n = (
            c(n) for n in ("routed", "gate_exp", "gated", "pick_turned", "pick_out", "gate_hi", "gate_lo"))
        hot1, hot2, diffed, absed, quad, quad_out = (
            c(n) for n in ("hot1_ready", "hot2_ready", "diff_ready", "abs_ready", "quad_done", "quad_out"))
        g_stored = [c(f"gates_stored{r}") for r in range(2)]
        NQ = 4
        assert (total // 2) * NQ * QUAD == SEQ
        with ExitStack() as ctx:
            t = lambda n, s, dt=F32: self.tensor(f"{n}{layer}", s, dt, ctx)
            self.split_tensors(ctx, f"pu{layer}")
            best = t("best", [P, UNITS, TOPK])
            picks = t("picks", [P, 2, UNITS * TOPK])
            ring = t("acts_ring", [P, 2, 2 * SEQ])
            small = t("gate_small", [P, 2, UNITS])
            turned = t("picks_turned", [P, 4, SEQ])
            g_hi = t("gate_hi_t", [P, SEQ], F32R)
            bank = self.banks(f"acc_pu{layer}", ctx, 4)
            qbank = self.banks(f"quad{layer}", ctx, 4)
            route = self.router(ctx, layer, sub, best, picks)
            gt = sub[:].rearrange("p (r i t) -> p r i t", r=2, t=GT)
            oh1 = t("hot1", [P, NQ, 2, QUAD, P], F32R)
            oh2 = t("hot2", [P, NQ, QUAD, P], F32R)
            diff = t("key_less_i2", [P, 2, QUAD, P])
            iota4 = self.iota[:].unsqueeze(1).to_broadcast([P, QUAD, P])

            H = half * BODY

            def at_quad(base, i, k, q):
                return i * (NQ * BODY) + (base + (k - H) * NQ + q)

            with self.nc.Block() as block:
                @block.sync
                def _(sp):
                    def put(i, k):
                        sp.wait_ge(out.sem, i * (2 * BODY) + (out.base + 2 * k + 2))
                        sp.dma_start(self.acts[bass.ds((i * BODY + k) * 2, 2)].rearrange("b p t -> p b t"),
                                     ring[:, k % 2, :].rearrange("p (b t) -> p b t", b=2)).then_inc(ring_sem[k % 2].sem, 16)

                    def put_gates(i, k):
                        if k % 2:
                            sp.wait_ge(quad_out.sem, at_quad(quad_out.base, i, k, NQ))
                            sp.dma_start(self.gates[bass.ds(i * 2 + (k - H) // 2, 1)].rearrange("a p i t -> p (a i t)"),
                                         gt[:, k // 2 % 2].rearrange("p i t -> p (i t)")).then_inc(g_stored[k // 2 % 2].sem, 16)

                    with sp.Fori(0, half) as i:
                        for k in range(BODY):
                            self.load_chunk(sp, u_src(i * BODY + (k + RAW)), i, k + RAW)
                            put(i, k)
                    with sp.Fori(0, half - 1) as i:
                        for k in range(H, H + BODY):
                            self.load_chunk(sp, u_src(i * BODY + (k + RAW)), i, k + RAW)
                            put(i, k)
                            put_gates(i, k)
                    for k in range(H, H + BODY):
                        put(half - 1, k)
                        put_gates(half - 1, k)
                    src = self.v_src(v)
                    self.load_first(sp, total, lambda k: src(0, k))
                    for r in range(2):
                        sp.wait_ge(ring_sem[r].sem, ring_sem[r].base + 16 * (total // 2))
                        sp.wait_ge(g_stored[r].sem, g_stored[r].base + 16 * half)

                @block.gpsimd
                def _(pool):
                    pool.wait_ge(turned_out.sem, turned_out.base + 2)
                    with pool.Fori(0, half) as i:
                        for k in range(H, H + BODY):
                            for q in range(NQ):
                                pool.wait_ge(hot2.sem, at_quad(hot2.base - 1, i, k, q))
                                at = i * (NQ * QUAD * BODY) + ((k - H) * NQ + q) * QUAD
                                pool.tensor_tensor(diff[:, q % 2], iota4,
                                                   turned[:, 1, bass.ds(at, QUAD)].unsqueeze(2).to_broadcast([P, QUAD, P]),
                                                   ALU.subtract).then_inc(diffed.sem, 1)

                @block.scalar
                def _(act):
                    def split(i, k):
                        self.split_hi(act, (done, 2), i, k)

                    def gelu(i, k):
                        for b in range(2):
                            n = 2 * k + b
                            act.wait_ge(done.sem, i * (2 * BODY) + (done.base + n + 1))
                            if b == 0:
                                act.wait_ge(ring_sem[k % 2].sem, i * (16 * BODY // 2) + (ring_sem[k % 2].base + 16 * (k // 2)))
                            act.activation(ring[:, k % 2, b * SEQ:(b + 1) * SEQ], bank[n % 4][:], ACT.Gelu).then_inc(out.sem, 1)

                    def hot(i, k):
                        for q in range(NQ):
                            act.wait_ge(diffed.sem, at_quad(diffed.base + 1, i, k, q))
                            act.activation(diff[:, q % 2], diff[:, q % 2], ACT.Abs).then_inc(absed.sem, 1)
                            act.wait_ge(absed.sem, at_quad(absed.base + 1, i, k, q))
                            act.wait_ge(quad.sem, at_quad(quad.base + 1 - NQ, i, k, q))
                            act.activation(oh2[:, q], diff[:, q % 2], ACT.Relu, bias=1.0, scale=-1.0).then_inc(hot2.sem, 1)

                    split(0, 0)
                    with act.Fori(0, half) as i:
                        for k in range(BODY):
                            split(i, k + 1)
                            gelu(i, k)
                    act.wait_ge(routed.sem, routed.base + 1)
                    act.activation(best[:], best[:], ACT.Exp).then_inc(exped.sem, 1)
                    for n in range(3):
                        act.wait_ge(turned_n.sem, turned_n.base + n + 1)
                        act.activation(turned[:, n, :], qbank[n][:], ACT.Copy).then_inc(turned_out.sem, 1)
                    act.activation(g_hi[:], qbank[2][:], ACT.Copy).then_inc(rounded.sem, 1)
                    with act.Fori(0, half - 1) as i:
                        for k in range(H, H + BODY):
                            split(i, k + 1)
                            hot(i, k)
                            gelu(i, k)
                    for k in range(H, H + BODY):
                        if k + 1 < H + BODY:
                            split(half - 1, k + 1)
                        hot(half - 1, k)
                        gelu(half - 1, k)

                @block.vector
                def _(dve):
                    ch = self.dve
                    self.split_lo(dve, 0, 0)
                    with dve.Fori(0, half) as i:
                        ch.close()
                        for k in range(BODY):
                            self.split_lo(dve, i, k + 1)
                            route(dve, i * BODY + k)
                        ch.rewind(dve)
                    ch.link(dve, dve.tensor_copy(small[:, 0, :], best[:, :, 0:1].rearrange("p u a -> p (u a)")))
                    ch.link(dve, dve.tensor_tensor(best[:], best[:], small[:, 0, :].unsqueeze(2).to_broadcast([P, UNITS, TOPK]), ALU.subtract))
                    dve.sem_inc(routed.sem, 1)
                    dve.wait_ge(exped.sem, exped.base + 1)
                    ch.link(dve, dve.tensor_reduce(small[:, 0, :], best[:], AX_X, ALU.add))
                    ch.link(dve, dve.reciprocal(small[:, 1, :], small[:, 0, :]))
                    dve.tensor_tensor(best[:], best[:], small[:, 1, :].unsqueeze(2).to_broadcast([P, UNITS, TOPK]), ALU.mult).then_inc(gated.sem, 1)
                    dve.wait_ge(rounded.sem, rounded.base + 1)
                    dve.tensor_tensor(turned[:, 3, :], turned[:, 2, :], g_hi[:].bitcast(F32), ALU.subtract).then_inc(g_lo_n.sem, 1)
                    dve.wait_ge(g_lo_n.sem, g_lo_n.base + 1)

                    def hot(i, k):
                        for q in range(NQ):
                            dve.wait_ge(quad.sem, at_quad(quad.base + 1 - NQ, i, k, q))
                            for r in range(QUAD):
                                at = i * (NQ * QUAD * BODY) + (((k - H) * NQ + q) * QUAD + r)
                                for part in range(2):
                                    last = dve.tensor_scalar(oh1[:, q, part, r, :], self.iota[:], turned[:, 0, bass.ds(at, 1)],
                                                             turned[:, 2 + part, bass.ds(at, 1)], ALU.is_equal, ALU.mult)
                            last.then_inc(hot1.sem, 1)

                    def gates_out(i, k):
                        if k % 2 == 0:
                            dve.wait_ge(g_stored[k // 2 % 2].sem, i * 16 + g_stored[k // 2 % 2].base)
                        for q in range(NQ):
                            dve.wait_ge(quad.sem, at_quad(quad.base + 1, i, k, q))
                            at = ((k % 2) * NQ + q) * QUAD
                            dve.tensor_copy(gt[:, k // 2 % 2, :, at:at + QUAD].rearrange("p i t -> p t i"),
                                            qbank[q][:].rearrange("p (t i) -> p t i", t=QUAD)).then_inc(quad_out.sem, 1)

                    with dve.Fori(0, half - 1) as i:
                        for k in range(H, H + BODY):
                            self.split_lo(dve, i, k + 1)
                            hot(i, k)
                            gates_out(i, k)
                    for k in range(H, H + BODY):
                        if k + 1 < H + BODY:
                            self.split_lo(dve, half - 1, k + 1)
                        hot(half - 1, k)
                        gates_out(half - 1, k)

                @block.tensor
                def _(pe):
                    def products(i, k):
                        self.turned_chunk(pe, bank, h_hi, h_lo, done, out, i, k)

                    def quads(i, k):
                        for q in range(NQ):
                            pe.wait_ge(hot1.sem, at_quad(hot1.base + 1, i, k, q))
                            pe.wait_ge(hot2.sem, at_quad(hot2.base + 1, i, k, q))
                            pe.wait_ge(quad_out.sem, at_quad(quad_out.base + 1 - NQ, i, k, q))
                            for r in range(QUAD):
                                for part in range(2):
                                    last = pe.matmul(qbank[q][:, r * P:(r + 1) * P], oh1[:, q, part, r, :], oh2[:, q, r, :],
                                                     start=part == 0, stop=part == 1)
                            last.then_inc(quad.sem, 1)

                    with pe.Fori(0, half) as i:
                        for k in range(BODY):
                            products(i, k)
                    products(0, H)
                    for n, src in enumerate((picks[:, 0, :], picks[:, 1, :], best[:].rearrange("p u s -> p (u s)"))):
                        if n == 0:
                            pe.wait_ge(gated.sem, gated.base + 1)
                        for m in range(TT):
                            last = pe.transpose(qbank[n][:, m * P:(m + 1) * P], src[:, m * P:(m + 1) * P], self.ident[:])
                        last.then_inc(turned_n.sem, 1)
                    pe.wait_ge(rounded.sem, rounded.base + 1)
                    with pe.Fori(0, half - 1) as i:
                        for k in range(H, H + BODY):
                            quads(i, k)
                            products(i, k + 1)
                    for k in range(H, H + BODY):
                        quads(half - 1, k)
                        if k + 1 < H + BODY:
                            products(half - 1, k + 1)
            self.dve.close()
            nq = SEQ // QUAD
            for s, n in ((done, 2 * total), (out, 2 * total), (ring_sem[0], 16 * (total // 2)), (ring_sem[1], 16 * (total // 2)),
                         (routed, 1), (exped, 1), (gated, 1), (turned_n, 3), (turned_out, 3), (rounded, 1), (g_lo_n, 1),
                         (hot1, nq), (hot2, nq), (diffed, nq), (absed, nq), (quad, nq), (quad_out, nq),
                         (g_stored[0], 16 * half), (g_stored[1], 16 * half)):
                s.base += n
            self.chunks += total

    def expert_sum(self, layer, v, next_src):
        nc = self.nc
        c = self.counter
        G = NKEY // 8
        BODY2 = 2 * BODY
        done, out, a_n, a_hi_n, a_lo_n = (c(n) for n in ("ys_done", "ys_added", "a_gated", "a_hi_ready", "a_lo_ready"))
        a_in = [c(f"a_in{r}") for r in range(2)]
        src = self.v_src(v)
        ch = self.chunks
        with ExitStack() as ctx:
            self.split_tensors(ctx, f"v{layer}")
            a_raw = self.tensor(f"a_raw{layer}", [P, 2, 4, SEQ], ctx=ctx)
            gate = self.tensor(f"a_gate{layer}", [P, 2, SEQ // GT, 4 * GT], ctx=ctx)
            a_hi = self.tensor(f"a_hi{layer}", [P, 2, 8, SEQ], F32R, ctx)
            a_lo = self.tensor(f"a_lo{layer}", [P, 2, 8, SEQ], F32R, ctx)
            bank = self.banks(f"y{layer}", ctx, 8)

            def pairs(eng, step):
                with eng.Fori(0, G // 2) as i:
                    for k in range(BODY2):
                        step(i, k)

            def ahead(eng, lead, follow, first):
                first()
                lead(0, 0)
                with eng.Fori(0, G // 2 - 1) as i:
                    for k in range(BODY2):
                        lead(i, k + 1)
                        follow(i, k, False)
                for k in range(BODY2):
                    if k + 1 < BODY2:
                        lead(G // 2 - 1, k + 1)
                    follow(G // 2 - 1, k, k >= BODY)

            def hi(act, i, k):
                act.wait_ge(self.raw_landed[(ch + k) % RAW], i * (16 * BODY2 // RAW) + 16 * ((ch + k) // RAW + 1))
                act.wait_ge(done.sem, i * (TT * BODY2) + (done.base + TT * (k + 1 - SPLIT)))
                act.activation(self.hi[:, (ch + k) % SPLIT, :], self.raw[:, (ch + k) % RAW, :], ACT.Copy).then_inc(self.hi_ready, 1)

            def lo(dve, i, k):
                dve.wait_ge(self.hi_ready, i * BODY2 + (ch + k + 1))
                dve.tensor_tensor(self.lo[:, (ch + k) % SPLIT, :], self.raw[:, (ch + k) % RAW, :],
                                  self.hi[:, (ch + k) % SPLIT, :].bitcast(F32), ALU.subtract).then_inc(self.lo_ready, 1)

            with nc.Block() as block:
                @block.sync
                def _(sp):
                    def load_a(g, j):
                        sp.dma_start(a_raw[:, j], self.acts[bass.ds(g * 8 + 4 * j, 4)].rearrange("i p t -> p i t")).then_inc(a_in[j].sem, 16)
                        sp.dma_start(gate[:, j], self.gates[:, :, bass.ds(g * 8 + 4 * j, 4), :]
                                     .rearrange("c p i t -> p c (i t)")).then_inc(a_in[j].sem, 16)
                    for j in range(2):
                        load_a(0, j)
                    for j in range(2):
                        sp.wait_ge(a_lo_n.sem, a_lo_n.base + j + 1)
                        load_a(1, j)

                    def load_v(i, k):
                        sp.wait_ge(self.lo_ready, i * BODY2 + (ch + k + 1))
                        slot = (ch + k) % RAW
                        sp.dma_start(self.raw[:, slot, :].rearrange("p (b n) -> p b n", b=4),
                                     src(i * 2 + k // 4, k % 4)).then_inc(self.raw_landed[slot], 16)
                    with sp.Fori(0, G // 2 - 1) as i:
                        for k in range(BODY2):
                            load_v(i, k + RAW)
                            if k % 2:
                                g, j = k // 4, k // 2 % 2
                                sp.wait_ge(a_lo_n.sem, i * 4 + (a_lo_n.base + 2 * (g + 1) + j + 1))
                                load_a(i * 2 + (g + 2), j)
                    for k in range(BODY2 - RAW):
                        load_v(G // 2 - 1, k + RAW)
                    self.load_first(sp, 4 * G, next_src)

                @block.scalar
                def _(act):
                    def a_split(i, g, j):
                        act.wait_ge(a_n.sem, i * 4 + (a_n.base + 2 * g + j + 1))
                        act.activation(a_hi[:, g % 2, 4 * j:4 * j + 4, :], a_raw[:, j], ACT.Copy).then_inc(a_hi_n.sem, 1)

                    def first():
                        for j in range(2):
                            a_split(0, 0, j)

                    def follow(i, k, last):
                        if last or k % 2:
                            return
                        g, j = k // 4 + 1, k // 2 % 2
                        if j == 0:
                            act.wait_ge(done.sem, i * (TT * BODY2) + (done.base + TT * k))
                        a_split(i, g, j)
                    ahead(act, lambda i, k: hi(act, i, k), follow, first)

                @block.vector
                def _(dve):
                    def a_gate(i, g, j):
                        dve.wait_ge(a_in[j].sem, i * 64 + (a_in[j].base + 32 * (g + 1)))
                        dve.tensor_tensor(a_raw[:, j].rearrange("p i (c t) -> p i c t", t=GT), a_raw[:, j].rearrange("p i (c t) -> p i c t", t=GT),
                                          gate[:, j].rearrange("p c (i t) -> p i c t", t=GT), ALU.mult).then_inc(a_n.sem, 1)

                    def a_split(i, g, j):
                        dve.wait_ge(a_hi_n.sem, i * 4 + (a_hi_n.base + 2 * g + j + 1))
                        dve.tensor_tensor(a_lo[:, g % 2, 4 * j:4 * j + 4, :], a_raw[:, j], a_hi[:, g % 2, 4 * j:4 * j + 4, :].bitcast(F32),
                                          ALU.subtract).then_inc(a_lo_n.sem, 1)

                    def first():
                        for j in range(2):
                            a_gate(0, 0, j)
                        for j in range(2):
                            a_split(0, 0, j)

                    def follow(i, k, last):
                        if not last:
                            (a_split if k % 2 else a_gate)(i, k // 4 + 1, k // 2 % 2)
                        if k % 2:
                            half = k // 2 % 2
                            for m in range(TT):
                                dve.wait_ge(done.sem, i * (TT * BODY2) + (done.base + TT * k + m + 1))
                                at = self.x[:, m, half * 512:half * 512 + 512]
                                dve.tensor_tensor(at, at, bank[half * TT + m][:], ALU.add).then_inc(out.sem, 1)
                    ahead(dve, lambda i, k: lo(dve, i, k), follow, first)
                    dve.wait_ge(out.sem, out.base + 2 * TT * G)

                @block.tensor
                def _(pe):
                    def chunk(i, k):
                        pe.wait_ge(self.lo_ready, i * BODY2 + (ch + k + 1 + RAW))
                        s = (ch + k) % SPLIT
                        r, half = k // 4, k // 2 % 2
                        if k % 4 == 0:
                            pe.wait_ge(a_lo_n.sem, i * 4 + (a_lo_n.base + 2 * r + 2))
                        for m in range(TT):
                            t = slice(m * P, (m + 1) * P)
                            if k % 2 == 0:
                                pe.wait_ge(out.sem, i * (4 * TT) + (out.base + (k // 2 - 2) * TT + m + 1))
                            for e in range(4):
                                j = 4 * (k % 2) + e
                                w = slice(e * 512, (e + 1) * 512)
                                last = self.three(pe, bank[half * TT + m][:], a_hi[:, r, j, t], a_lo[:, r, j, t],
                                                  self.hi[:, s, w], self.lo[:, s, w], j == 0, j == 7)
                            last.then_inc(done.sem, 1)
                    pairs(pe, chunk)
            for s, n in ((done, TT * 4 * G), (out, 2 * TT * G), (a_n, 2 * G), (a_hi_n, 2 * G), (a_lo_n, 2 * G), (a_in[0], 32 * G), (a_in[1], 32 * G)):
                s.base += n
            self.chunks += 4 * G


    def conv_mixer(self, next_src):
        a = self.a
        chain = self.dve
        taps_sem = self.counter("taps_landed")
        with ExitStack() as ctx:
            h_hi = self.tensor("h_hi_c", [P, DK, SEQ], F32R, ctx)
            h_lo = self.tensor("h_lo_c", [P, DK, SEQ], F32R, ctx)
            w_in = lambda c: a["a_w_in"][bass.ds(c, 1)].rearrange("a p n -> p a n")
            w_out = lambda c: a["a_w_out"][bass.ds(c, 1)].rearrange("a p n -> p a n")
            self.norm("c", 0, h_hi, h_lo)
            with ExitStack() as ctx2:
                bcu = self.tensor("bcu", [P, 3 * DK * SEQ], ctx=ctx2)
                self.product_turned("cin", h_hi, h_lo, 3 * DK // 2, w_in, w_out, dst=bcu)
                v = bcu[:].rearrange("p (g k t) -> p g k t", g=3, t=SEQ)
                b, c, u = v[:, 0], v[:, 1], v[:, 2]
                PAD = CONV_W - 1
                cu = self.tensor("cu", [P, DK, PAD + SEQ], ctx=ctx2)
                taps = self.tensor("taps", [P, CONV_W, DK], ctx=ctx2)
                with self.nc.Block() as block:
                    @block.sync
                    def _(sp):
                        sp.dma_start(taps[:], a["a_conv"].rearrange("w p k -> p w k")).then_inc(taps_sem.sem, 16)

                    @block.vector
                    def _(dve):
                        chain.link(dve, dve.memset(cu[:, :, 0:PAD], 0.0))
                        chain.link(dve, dve.tensor_tensor(cu[:, :, PAD:], c, u, ALU.mult))
                        dve.wait_ge(taps_sem.sem, taps_sem.base + 16)
                        for k in range(DK):
                            chain.link(dve, dve.tensor_scalar(c[:, k, :], cu[:, k, 0:SEQ], taps[:, 0, k:k + 1], None, ALU.mult))
                            for w in range(1, CONV_W):
                                chain.link(dve, dve.scalar_tensor_tensor(c[:, k, :], cu[:, k, w:w + SEQ], taps[:, w, k:k + 1],
                                                                         c[:, k, :], ALU.mult, ALU.add))
                        chain.link(dve, dve.tensor_tensor(b, b, c, ALU.mult))
                chain.close()
                taps_sem.base += 16
                self.split_rows("c", lambda k: b[:, k, :], h_hi, h_lo, DK)
            self.product_rows("cout", h_hi, h_lo, 4, w_out, next_src, self.add_to_x)

    def add_to_x(self, dve, nb, m, bank):
        at = self.x[:, m, bass.ds(nb * 512, 512)]
        return dve.tensor_tensor(at, at, bank, ALU.add)


    def ple(self, layer, next_src):
        a, nc = self.a, self.nc
        landed = self.counter("ple_landed")
        hi_n, lo_n, done, out, sig = (self.counter(n) for n in ("ple_hi", "ple_lo", "ple_done", "ple_out", "ple_sig"))
        KP = 2
        w_gate = lambda c: a["ple_wg"][layer][bass.ds(c, 1)].rearrange("a p n -> p a n")
        with ExitStack() as ctx:
            h_hi = self.tensor(f"h_hi_e{layer}", [P, DK, SEQ], F32R, ctx)
            h_lo = self.tensor(f"h_lo_e{layer}", [P, DK, SEQ], F32R, ctx)
            self.norm(f"e{layer}", 5 + layer, h_hi, h_lo)
            proj = self.tensor(f"proj{layer}", [P, TT, D], ctx=ctx)
            gate = self.tensor(f"gate{layer}", [P, TT, D], ctx=ctx)
            with ExitStack() as ctx2:
                t = lambda n, s, dt=F32: self.tensor(f"{n}{layer}", s, dt, ctx2)
                pt, pt_hi, pt_lo = t("pT", [P, KP, SEQ]), t("pT_hi", [P, KP, SEQ], F32R), t("pT_lo", [P, KP, SEQ], F32R)
                wp, wp_hi, wp_lo = t("wp", [P, KP, D]), t("wp_hi", [P, KP, D], F32R), t("wp_lo", [P, KP, D], F32R)
                bank = self.banks(f"pp{layer}", ctx2, 8)
                with nc.Block() as block:
                    @block.sync
                    def _(sp):
                        sp.dma_start(pt[:], a["p"][layer].rearrange("k p t -> p k t")).then_inc(landed.sem, 16)
                        sp.dma_start(wp[:], a["ple_wp"][layer].rearrange("k p n -> p k n")).then_inc(landed.sem, 16)

                    @block.scalar
                    def _(act):
                        act.wait_ge(landed.sem, landed.base + 32)
                        act.activation(pt_hi[:], pt[:], ACT.Copy).then_inc(hi_n.sem, 1)
                        act.activation(wp_hi[:], wp[:], ACT.Copy).then_inc(hi_n.sem, 1)

                    @block.vector
                    def _(dve):
                        dve.wait_ge(hi_n.sem, hi_n.base + 1)
                        dve.tensor_tensor(pt_lo[:], pt[:], pt_hi[:].bitcast(F32), ALU.subtract).then_inc(lo_n.sem, 1)
                        dve.wait_ge(hi_n.sem, hi_n.base + 2)
                        dve.tensor_tensor(wp_lo[:], wp[:], wp_hi[:].bitcast(F32), ALU.subtract).then_inc(lo_n.sem, 1)
                        for n in range(8):
                            dve.wait_ge(done.sem, done.base + n + 1)
                            m, nb = divmod(n, 2)
                            dve.tensor_copy(proj[:, m, nb * 512:(nb + 1) * 512], bank[n][:]).then_inc(out.sem, 1)
                        dve.wait_ge(out.sem, out.base + 8)

                    @block.tensor
                    def _(pe):
                        pe.wait_ge(lo_n.sem, lo_n.base + 2)
                        for n in range(8):
                            m, nb = divmod(n, 2)
                            for k in range(KP):
                                t_, w = slice(m * P, (m + 1) * P), slice(nb * 512, (nb + 1) * 512)
                                last = self.three(pe, bank[n][:], pt_hi[:, k, t_], pt_lo[:, k, t_], wp_hi[:, k, w], wp_lo[:, k, w],
                                                  k == 0, k == KP - 1)
                            last.then_inc(done.sem, 1)
                for s, n in ((landed, 32), (hi_n, 2), (lo_n, 2), (done, 8), (out, 8)):
                    s.base += n
            self.product_rows(f"e{layer}", h_hi, h_lo, 4, w_gate, next_src,
                              lambda dve, nb, m, bank: dve.tensor_copy(gate[:, m, bass.ds(nb * 512, 512)], bank))
            with nc.Block() as block:
                @block.scalar
                def _(act):
                    for m in range(TT):
                        act.activation(gate[:, m, :], gate[:, m, :], ACT.Sigmoid).then_inc(sig.sem, 1)

                @block.vector
                def _(dve):
                    for m in range(TT):
                        dve.wait_ge(sig.sem, sig.base + m + 1)
                        self.dve.link(dve, dve.tensor_tensor(gate[:, m, :], gate[:, m, :], proj[:, m, :], ALU.mult))
                        self.dve.link(dve, dve.tensor_tensor(self.x[:, m, :], self.x[:, m, :], gate[:, m, :], ALU.add))
            self.dve.close()
            sig.base += TT


    def rope_tables(self, ctx):
        nc, a, ch = self.nc, self.a, self.dve
        landed, const, folded, made = (self.counter(n) for n in ("pos_landed", "freq_ready", "angle_folded", "rope_made"))
        self.cos = self.tensor("rope_cos", [P, TT, HALF], ctx=ctx)
        self.sin = self.tensor("rope_sin", [P, TT, HALF], ctx=ctx)
        self.mask1 = self.tensor("mask_dilation1", [P, 2 * P], ctx=ctx)
        self.masks = [self.mask1] + [self.tensor(f"mask_dilation{d}", [P, SEQ], ctx=ctx) for d in DILATIONS[1:]]
        self.qk_gain = self.tensor("qk_gain", [P, 2, DH], ctx=ctx)
        freqs = (np.float32(1.0) / (np.float32(THETA) ** (np.arange(0, ROPE, 2, dtype=np.float32) / np.float32(ROPE)))).astype(np.float32)
        C1 = 6.28125
        C2 = float(np.float32(np.round((TWO_PI - C1) * 2 ** 21) / 2 ** 21))
        C3 = float(np.float32(TWO_PI - C1 - C2))
        MAGIC = 1.5 * 2 ** 23
        PI = float(np.nextafter(np.float32(np.pi), np.float32(0)))
        with ExitStack() as ctx2:
            t = lambda n, s, dt=F32: self.tensor(n, s, dt, ctx2)
            pos, posf, freq = t("pos", [P, TT], I32), t("pos_f", [P, TT]), t("freq", [P, HALF])
            ang, turns, fold = t("angle", [P, TT, HALF]), t("turns", [P, TT, HALF]), t("folded", [P, 2, TT, HALF])
            diff, dif2 = t("diff", [P, SEQ], I32), t("diff_mod", [P, SEQ], I32)
            with nc.Block() as block:
                @block.sync
                def _(sp):
                    sp.dma_start(pos[:], a["positions"]).then_inc(landed.sem, 16)
                    sp.dma_start(self.qk_gain[:, 0:1, :], a["k_norm"].partition_broadcast(P)).then_inc(landed.sem, 16)
                    sp.dma_start(self.qk_gain[:, 1:2, :], a["q_norm"].partition_broadcast(P)).then_inc(landed.sem, 16)
                    sp.wait_ge(landed.sem, landed.base + 48)

                @block.gpsimd
                def _(pool):
                    for j in range(HALF):
                        pool.memset(freq[:, j:j + 1], float(freqs[j])).then_inc(const.sem, 1)
                    pool.memset(self.mask1[:], 0.0).then_inc(const.sem, 1)
                    pool.iota(diff[:], pattern=[[-1, SEQ]], base=SEQ, channel_multiplier=1).then_inc(const.sem, 1)
                    pool.wait_ge(const.sem, const.base + HALF + 1)
                    pool.affine_select(out=self.mask1[:], in_=self.mask1[:], compare_op=ALU.is_ge, fill=LOWEST,
                                       base=P, pattern=[[-1, 2 * P]], channel_multiplier=1).then_inc(const.sem, 1)
                    pool.wait_ge(const.sem, const.base + HALF + 3)
                    pool.affine_select(out=self.mask1[:], in_=self.mask1[:], compare_op=ALU.is_ge, fill=LOWEST,
                                       base=0, pattern=[[1, 2 * P]], channel_multiplier=-1).then_inc(const.sem, 1)
                    for n in range(2):
                        mask = self.masks[n + 1]
                        pool.wait_ge(made.sem, made.base + n + 1)
                        pool.affine_select(out=mask[:], in_=mask[:], compare_op=ALU.is_ge, fill=LOWEST,
                                           base=SEQ - P, pattern=[[-1, SEQ]], channel_multiplier=1).then_inc(const.sem, 1)

                @block.vector
                def _(dve):
                    link = lambda ins: ch.link(dve, ins)
                    dve.wait_ge(const.sem, const.base + HALF + 2)
                    for n, d in enumerate(DILATIONS[1:]):
                        mask = self.masks[n + 1]
                        link(dve.tensor_scalar(dif2[:], diff[:], d - 1, None, ALU.bitwise_and))
                        link(dve.tensor_scalar(mask[:], dif2[:], 0.0, None, ALU.is_equal))
                        dve.tensor_scalar(mask[:], mask[:], -1.0, -LOWEST, ALU.add, ALU.mult).then_inc(made.sem, 1)
                    dve.wait_ge(landed.sem, landed.base + 48)
                    link(dve.tensor_copy(posf[:], pos[:]))
                    link(dve.tensor_tensor(ang[:], posf[:].unsqueeze(2).to_broadcast([P, TT, HALF]),
                                           freq[:].unsqueeze(1).to_broadcast([P, TT, HALF]), ALU.mult))
                    for n, quarter in enumerate((0.0, 0.25)):
                        f = fold[:, n]
                        link(dve.tensor_scalar(turns[:], ang[:], float(1 / TWO_PI), quarter, ALU.mult, ALU.add))
                        link(dve.tensor_scalar(turns[:], turns[:], MAGIC, None, ALU.add))
                        link(dve.tensor_scalar(turns[:], turns[:], -MAGIC, None, ALU.add))
                        link(dve.scalar_tensor_tensor(f, turns[:], -C1, ang[:], ALU.mult, ALU.add))
                        link(dve.scalar_tensor_tensor(f, turns[:], -C2, f, ALU.mult, ALU.add))
                        link(dve.scalar_tensor_tensor(f, turns[:], -C3, f, ALU.mult, ALU.add))
                        link(dve.tensor_scalar(f, f, float(quarter * TWO_PI), PI, ALU.add, ALU.min))
                        link(dve.tensor_scalar(f, f, -PI, None, ALU.max))
                    dve.sem_inc(folded.sem, 1)

                @block.scalar
                def _(act):
                    act.wait_ge(folded.sem, folded.base + 1)
                    act.activation(self.sin[:], fold[:, 0], ACT.Sin)
                    act.activation(self.cos[:], fold[:, 1], ACT.Sin)
            ch.close()
            for s, n in ((landed, 48), (const, HALF + 6), (folded, 1), (made, 2)):
                s.base += n

    def head_norm_rope(self, tag, buf, heads, gain):
        ch = self.dve
        sq, root_in, root = (self.counter(n) for n in ("head_squares", "head_root_in", "head_root"))
        with ExitStack() as ctx:
            t = lambda n, s: self.tensor(f"{n}_{tag}", s, F32, ctx)
            tmp = t("head_sq", [P, 2, heads * DH])
            st = t("head_stat", [P, 4, heads])
            rot = t("head_rot", [P, 4, heads, HALF])
            with self.nc.Block() as block:
                @block.scalar
                def _(act):
                    for m in range(TT):
                        if m >= 1:
                            act.wait_ge(root_in.sem, root_in.base + m)
                        act.activation(tmp[:, m % 2, :], buf[:, m, :], ACT.Square).then_inc(sq.sem, 1)
                        act.wait_ge(root_in.sem, root_in.base + m + 1)
                        act.activation(st[:, 3, :], st[:, 1, :], ACT.Sqrt).then_inc(root.sem, 1)

                @block.vector
                def _(dve):
                    link = lambda ins: ch.link(dve, ins)
                    for m in range(TT):
                        x3 = buf[:, m, :].rearrange("p (h d) -> p h d", d=DH)
                        ss, v, y, r = (st[:, n, :] for n in range(4))
                        dve.wait_ge(sq.sem, sq.base + m + 1)
                        link(dve.tensor_reduce(ss, tmp[:, m % 2, :].rearrange("p (h d) -> p h d", d=DH), AX_X, ALU.add))
                        dve.tensor_scalar(v, ss, 1.0 / DH, EPS, ALU.mult, ALU.add).then_inc(root_in.sem, 1)
                        self.rsqrt_steps(dve, lambda v, t: dve.wait_ge(root.sem, root.base + m + 1), v, y, r)
                        link(dve.tensor_tensor(x3, x3, y.unsqueeze(2).to_broadcast([P, heads, DH]), ALU.mult))
                        link(dve.tensor_tensor(x3, x3, gain.to_broadcast([P, heads, DH]), ALU.mult))
                        c = self.cos[:, m, :].unsqueeze(1).to_broadcast([P, heads, HALF])
                        s = self.sin[:, m, :].unsqueeze(1).to_broadcast([P, heads, HALF])
                        x1, x2 = x3[:, :, 0:HALF], x3[:, :, HALF:ROPE]
                        for n, (xx, w) in enumerate(((x1, c), (x2, s), (x2, c), (x1, s))):
                            link(dve.tensor_tensor(rot[:, n], xx, w, ALU.mult))
                        link(dve.tensor_tensor(x1, rot[:, 0], rot[:, 1], ALU.subtract))
                        link(dve.tensor_tensor(x2, rot[:, 2], rot[:, 3], ALU.add))
            ch.close()
            for s in (sq, root_in, root):
                s.base += TT

    def turn(self, tag, src, put_hi, put_lo=None):
        turned, hi_done, lo_done = (self.counter(n) for n in ("turn_turned", "turn_hi", "turn_lo"))
        last_done = lo_done if put_lo else hi_done
        with ExitStack() as ctx:
            bank = self.banks(f"turn_{tag}", ctx, 4)
            with self.nc.Block() as block:
                @block.scalar
                def _(act):
                    for k in range(DK):
                        act.wait_ge(turned.sem, turned.base + k + 1)
                        put_hi(act, k, bank[k % 4][:]).then_inc(hi_done.sem, 1)

                @block.vector
                def _(dve):
                    if put_lo:
                        for k in range(DK):
                            dve.wait_ge(hi_done.sem, hi_done.base + k + 1)
                            put_lo(dve, k, bank[k % 4][:]).then_inc(lo_done.sem, 1)

                @block.tensor
                def _(pe):
                    for k in range(DK):
                        if k >= 4:
                            pe.wait_ge(last_done.sem, last_done.base + k - 3)
                        for m in range(TT):
                            last = pe.transpose(bank[k % 4][:, m * P:(m + 1) * P], src[:, m, k * P:(k + 1) * P], self.ident[:])
                        last.then_inc(turned.sem, 1)
            turned.base += DK
            hi_done.base += DK
            if put_lo:
                lo_done.base += DK

    def attention_mixer(self, next_src):
        a = self.a
        part = lambda w: lambda c: w[bass.ds(c, 1)].rearrange("a p n -> p a n")
        wk, wv, wq, wo = part(a["w_k"]), part(a["w_v"]), part(a["b_w_q"]), part(a["b_w_o"])
        with ExitStack() as ctx:
            self.rope_tables(ctx)
            kT = self.tensor("kT", [P, KVH * SEQ], ctx=ctx)
            v_sb = self.tensor("v_sb", [P, TT, D], ctx=ctx)
            with ExitStack() as c2:
                h_hi = self.tensor("h_hi_kv", [P, DK, SEQ], F32R, c2)
                h_lo = self.tensor("h_lo_kv", [P, DK, SEQ], F32R, c2)
                self.norm("kv", 1, h_hi, h_lo)
                k_sb = self.tensor("k_sb", [P, TT, D], ctx=c2)
                copy_to = lambda dst: lambda dve, nb, m, bank: dve.tensor_copy(dst[:, m, bass.ds(nb * 512, 512)], bank)
                self.product_rows("k", h_hi, h_lo, 4, wk, wv, copy_to(k_sb))
                self.product_rows("v", h_hi, h_lo, 4, wv, wq, copy_to(v_sb))
                self.head_norm_rope("k", k_sb, KVH, self.qk_gain[:, 0:1, :])
                self.turn("k", k_sb, lambda act, k, bank: act.activation(kT[:, k * SEQ:(k + 1) * SEQ], bank, ACT.Copy))
            with ExitStack() as c2:
                q_sb = self.tensor("q_sb", [P, TT, GROUPS * D], ctx=c2)
                with ExitStack() as c3:
                    h_hi = self.tensor("h_hi_q", [P, DK, SEQ], F32R, c3)
                    h_lo = self.tensor("h_lo_q", [P, DK, SEQ], F32R, c3)
                    self.norm("q", 2, h_hi, h_lo)
                    self.product_rows("q", h_hi, h_lo, 12, wq, wo, copy_to(q_sb))
                self.head_norm_rope("q", q_sb, GROUPS * KVH, self.qk_gain[:, 1:2, :])
                o_sb = q_sb[:, :, 0:D]
                self.attend(q_sb, kT, v_sb, o_sb)
                h_hi = self.tensor("o_hi", [P, DK, SEQ], F32R, c2)
                h_lo = self.tensor("o_lo", [P, DK, SEQ], F32R, c2)
                self.turn("o", o_sb, lambda act, k, bank: act.activation(h_hi[:, k, :], bank, ACT.Copy),
                          lambda dve, k, bank: dve.tensor_tensor(h_lo[:, k, :], bank, h_hi[:, k, :].bitcast(F32), ALU.subtract))
                self.product_rows("o", h_hi, h_lo, 4, wo, next_src, self.add_to_x)

    def attend(self, q_sb, kT, v_sb, o_sb):
        nc, ch = self.nc, self.dve
        names = ("at_staged", "at_q_turned", "at_q_out", "at_scores", "at_masked", "at_max", "at_exp",
                 "at_weights", "at_w_turned", "at_w_out", "at_values", "at_out")
        staged, q_turned, q_out, scores, masked, maxed, exped, weights, w_turned, w_out, values, out = (self.counter(n) for n in names)
        with ExitStack() as ctx:
            t = lambda n, s: self.tensor(n, s, F32, ctx)
            qh = t("q_head", [P, TT, GROUPS, DH])
            qT = t("q_head_turned", [P, GROUPS, SEQ])
            S = t("scores_row", [P, 2, 2 * P + 2 * SEQ])
            W = t("weights_sum", [P, 2, SEQ])
            wT = t("weights_turned", [P, 2, SEQ])
            st = t("softmax_stat", [P, 4, TT])
            sets = [self.banks(f"s{r}_", ctx, GROUPS) for r in range(2)]
            w_bank, o_bank = self.banks("wv", ctx, 2)
            top, neg, den, inv = (st[:, n, :] for n in range(4))

            def spans(m):
                w = (m + 1) * P
                g0 = 0 if m else P
                return [(g0, 2 * P, g0), (2 * P, 2 * P + w, SEQ - w), (2 * P + w, 2 * P + 2 * w, SEQ - w)]

            with nc.Block() as block:
                @block.gpsimd
                def _(pool):
                    with pool.Fori(0, KVH) as h:
                        pool.wait_ge(q_turned.sem, h * GROUPS + q_turned.base)
                        for g in range(GROUPS):
                            last = pool.tensor_copy(qh[:, :, g, :], q_sb[:, :, bass.ds(h * DH + g * D, DH)])
                            last.then_inc(staged.sem, 1)

                @block.tensor
                def _(pe):
                    def score(h, m):
                        pe.wait_ge(masked.sem, h * TT + (masked.base + m - 1))
                        keys = max(m - 1, 0) * P
                        for g in range(GROUPS):
                            lo, hi, _ = spans(m)[g]
                            first = keys if g == 0 else 0
                            last = pe.matmul(sets[m % 2][g][:, 0:hi - lo], qT[:, g, m * P:(m + 1) * P],
                                             kT[:, bass.ds(h * SEQ + first, hi - lo)], start=True, stop=True)
                        last.then_inc(scores.sem, 1)

                    def value(h, m):
                        pe.wait_ge(weights.sem, h * TT + (weights.base + m + 1))
                        pe.wait_ge(w_out.sem, h * TT + (w_out.base + m))
                        for b in range(m + 1):
                            last = pe.transpose(w_bank[:, b * P:(b + 1) * P], W[:, m % 2, b * P:(b + 1) * P], self.ident[:])
                        last.then_inc(w_turned.sem, 1)
                        pe.wait_ge(w_out.sem, h * TT + (w_out.base + m + 1))
                        pe.wait_ge(out.sem, h * TT + (out.base + m))
                        for b in range(m + 1):
                            last = pe.matmul(o_bank[:, 0:DH], wT[:, m % 2, b * P:(b + 1) * P],
                                             v_sb[:].rearrange("p m d -> p (m d)")[:, bass.ds(h * DH + b * D, DH)],
                                             start=b == 0, stop=b == m)
                        last.then_inc(values.sem, 1)

                    with pe.Fori(0, KVH) as h:
                        pe.wait_ge(masked.sem, h * TT + masked.base)
                        for g in range(GROUPS):
                            pe.wait_ge(staged.sem, h * GROUPS + (staged.base + g + 1))
                            for m in range(TT):
                                last = pe.transpose(sets[1][g][:, m * P:(m + 1) * P], qh[:, m, g, :], self.ident[:])
                            last.then_inc(q_turned.sem, 1)
                        pe.wait_ge(q_out.sem, h * GROUPS + (q_out.base + GROUPS))
                        score(h, 0)
                        score(h, 1)
                        for m in range(TT):
                            if m + 2 < TT:
                                score(h, m + 2)
                            value(h, m)

                @block.scalar
                def _(act):
                    def exp(h, m):
                        act.wait_ge(maxed.sem, h * TT + (maxed.base + m + 1))
                        lo, hi = spans(m)[0][0], spans(m)[2][1]
                        act.activation(S[:, m % 2, lo:hi], S[:, m % 2, lo:hi], ACT.Exp, bias=neg[:, m:m + 1],
                                       accum_out=den[:, m:m + 1]).then_inc(exped.sem, 1)

                    def turned(h, m):
                        act.wait_ge(w_turned.sem, h * TT + (w_turned.base + m + 1))
                        act.wait_ge(values.sem, h * TT + (values.base + m - 1))
                        act.activation(wT[:, m % 2, 0:(m + 1) * P], w_bank[:, 0:(m + 1) * P], ACT.Copy).then_inc(w_out.sem, 1)

                    with act.Fori(0, KVH) as h:
                        act.wait_ge(scores.sem, h * TT + scores.base)
                        for g in range(GROUPS):
                            act.wait_ge(q_turned.sem, h * GROUPS + (q_turned.base + g + 1))
                            act.activation(qT[:, g, :], sets[1][g][:], ACT.Copy).then_inc(q_out.sem, 1)
                        exp(h, 0)
                        exp(h, 1)
                        for m in range(TT):
                            turned(h, m)
                            if m + 2 < TT:
                                exp(h, m + 2)

                @block.vector
                def _(dve):
                    link = lambda ins: ch.link(dve, ins)

                    def mask(h, m):
                        dve.wait_ge(scores.sem, h * TT + (scores.base + m + 1))
                        dve.wait_ge(weights.sem, h * TT + (weights.base + m - 1))
                        for g in range(GROUPS):
                            lo, hi, at = spans(m)[g]
                            last = dve.scalar_tensor_tensor(S[:, m % 2, lo:hi], sets[m % 2][g][:, 0:hi - lo], DH ** -0.5,
                                                            self.masks[g][:, at:at + hi - lo], ALU.mult, ALU.add)
                            if g < GROUPS - 1:
                                link(last)
                        last.then_inc(masked.sem, 1)
                        dve.wait_ge(masked.sem, h * TT + (masked.base + m + 1))
                        link(dve.tensor_reduce(top[:, m:m + 1], S[:, m % 2, spans(m)[0][0]:spans(m)[2][1]], AX_X, ALU.max))
                        dve.tensor_scalar(neg[:, m:m + 1], top[:, m:m + 1], -1.0, None, ALU.mult).then_inc(maxed.sem, 1)

                    def weigh(h, m):
                        dve.wait_ge(exped.sem, h * TT + (exped.base + m + 1))
                        dve.wait_ge(out.sem, h * TT + (out.base + m + 1 - TT))
                        link(dve.reciprocal(inv[:, m:m + 1], den[:, m:m + 1]))
                        dve.wait_ge(w_turned.sem, h * TT + (w_turned.base + m - 1))
                        row = S[:, m % 2, :]
                        sp0, sp1, sp2 = spans(m)
                        link(dve.tensor_tensor(W[:, m % 2, 0:(m + 1) * P], row[:, sp1[0]:sp1[1]], row[:, sp2[0]:sp2[1]], ALU.add))
                        at = W[:, m % 2, max(m - 1, 0) * P:(m + 1) * P]
                        dve.tensor_tensor(at, at, row[:, sp0[0]:sp0[1]], ALU.add).then_inc(weights.sem, 1)

                    def put(h, m):
                        dve.wait_ge(values.sem, h * TT + (values.base + m + 1))
                        dve.tensor_scalar(o_sb[:, m, bass.ds(h * DH, DH)], o_bank[:, 0:DH], inv[:, m:m + 1], None,
                                          ALU.mult).then_inc(out.sem, 1)

                    with dve.Fori(0, KVH) as h:
                        ch.close()
                        mask(h, 0)
                        mask(h, 1)
                        for m in range(TT):
                            weigh(h, m)
                            if m + 2 < TT:
                                mask(h, m + 2)
                            if m:
                                put(h, m - 1)
                        put(h, TT - 1)
                        ch.rewind(dve)
                    dve.wait_ge(out.sem, out.base + TT * KVH)
            for s, n in ((staged, GROUPS * KVH), (q_turned, GROUPS * KVH), (q_out, GROUPS * KVH)) + tuple(
                    (s, TT * KVH) for s in (scores, masked, maxed, exped, weights, w_turned, w_out, values, out)):
                s.base += n

    def finish(self, out):
        stored = self.counter("x_stored")
        with self.nc.Block() as block:
            @block.sync
            def _(sp):
                sp.dma_start(out.rearrange("(t p) d -> p t d", p=P), self.x[:]).then_inc(stored.sem, 16)
                sp.wait_ge(stored.sem, 16)


def build(nc, a, out):
    with ExitStack() as ctx:
        k = Kernel(nc, ctx, a)
        first = lambda w: lambda c: w[bass.ds(c, 1)].rearrange("a p n -> p a n")
        k.setup(first(a["a_w_in"]))
        k.conv_mixer(first(a["peer_wq"][0]))
        k.peer(0, first(a["ple_wg"][0]))
        k.ple(0, first(a["w_k"]))
        k.attention_mixer(first(a["peer_wq"][1]))
        k.peer(1, first(a["ple_wg"][1]))
        k.ple(1, None)
        k.finish(out)


def slices_turned(w):
    n = w.shape[-1] // (2 * P)
    return np.ascontiguousarray(w.reshape(DK, P, n, 2, P).transpose(2, 1, 3, 0, 4)).reshape(n, P, CHUNK)


def slices_rows(w):
    n = w.shape[-1] // 512
    return np.ascontiguousarray(w.reshape(2, DK // 2, P, n, 512).transpose(3, 0, 2, 1, 4)).reshape(2 * n, P, CHUNK)


def kernel(x, p, positions, a_norm, a_w_in, a_conv, a_w_out, kv_norm, w_kv, k_norm, b_norm, b_w_q, q_norm, b_w_o,
           ffn_norm, peer_w_q, peer_sub_keys, peer_u, peer_v, ple_norm, ple_w_gate, ple_w_proj):
    import concourse.bacc as bacc
    from concourse.bass_utils import run_bass_kernel_spmd

    f = np.asarray
    column = lambda g: f(g).reshape(DK, P).T
    layers = range(2)
    arrays = {
        "x": f(x)[0],
        "p": np.stack([np.ascontiguousarray(f(p)[i, 0].T).reshape(2, P, SEQ) for i in layers]),
        "positions": np.ascontiguousarray(f(positions).reshape(TT, P).T),
        "gains": np.stack([column(g) for g in (f(a_norm)[0], kv_norm, f(b_norm)[0], f(ffn_norm)[0], f(ffn_norm)[1],
                                               f(ple_norm)[0], f(ple_norm)[1])]),
        "a_w_in": slices_turned(f(a_w_in)[0]),
        "a_conv": np.ascontiguousarray(f(a_conv)[0].reshape(CONV_W, DK, P).transpose(0, 2, 1)),
        "a_w_out": slices_rows(f(a_w_out)[0]),
        "w_k": slices_rows(f(w_kv)[:, :D]),
        "w_v": slices_rows(f(w_kv)[:, D:]),
        "k_norm": f(k_norm).reshape(1, DH),
        "q_norm": f(q_norm).reshape(1, DH),
        "b_w_q": slices_rows(f(b_w_q)[0]),
        "b_w_o": slices_rows(f(b_w_o)[0]),
        "peer_wq": np.stack([slices_turned(f(peer_w_q)[i]) for i in layers]),
        "peer_keys": np.ascontiguousarray(f(peer_sub_keys).reshape(2, 2 * PH, NKEY, P).transpose(0, 3, 1, 2)),
        "peer_u": np.stack([np.ascontiguousarray(f(peer_u)[i].reshape(NKEY, NKEY, DK, P).transpose(1, 3, 2, 0))
                            .reshape(NKEY, P, DK * NKEY) for i in layers]),
        "peer_v": f(peer_v),
        "ple_wg": np.stack([slices_rows(f(ple_w_gate)[i]) for i in layers]),
        "ple_wp": f(ple_w_proj).reshape(2, 2, P, D),
    }
    nc = bacc.Bacc("TRN2", target_bir_lowering=False, num_devices=1)
    ins, aps = {}, {}
    for name, value in arrays.items():
        value = np.ascontiguousarray(value)
        ins[f"in_{name}"] = value
        aps[name] = nc.dram_tensor(f"in_{name}", value.shape, mybir.dt.from_np(value.dtype), kind="ExternalInput").ap()
    out = nc.dram_tensor("out_x", (SEQ, D), F32, kind="ExternalOutput").ap()
    build(nc, aps, out)
    r = run_bass_kernel_spmd(nc, [ins], core_ids=[0])
    return r.results[0]["out_x"].reshape(1, SEQ, D)
```

```python
from contextlib import ExitStack

import numpy as np

import concourse.bass as bass
from concourse import mybir

P = 128
ALU = mybir.AluOpType
ACT = mybir.ActivationFunctionType
F32 = mybir.dt.float32
F32R = mybir.dt.float32r
BF16 = mybir.dt.bfloat16
I32 = mybir.dt.int32
U32 = mybir.dt.uint32
AX_X = mybir.AxisListType.X

D = 1024
SEQ = 512
TT = SEQ // P
DK = D // P
CONV_W = 3
DH = 128
KVH = D // DH
GROUPS = 3
DILATIONS = (1, 4, 16)
ROPE = DH // 4
HALF = ROPE // 2
THETA = 500000.0
PH = 8
NKEY = 128
TOPK = 16
NSEL = PH * TOPK
UNITS = TT * PH
EPS = 1e-6
LOWEST = -3.0e38
CHUNK = 2048
RAW = 4
SPLIT = 2
BODY = 4
CREDITS = 32
GT = 32
QUAD = 4
TWO_PI = 2.0 * np.pi


class Counter:

    def __init__(self, sem, credits=0):
        self.sem = sem
        self.base = credits


class Chain:

    def __init__(self, counter):
        self.counter = counter
        self.n = 0

    def mark(self, ins):
        ins.then_inc(self.counter.sem, 1)
        self.n += 1
        return self.n

    def after(self, eng, n):
        eng.wait_ge(self.counter.sem, self.counter.base + n)

    def link(self, eng, ins):
        self.after(eng, self.mark(ins))

    def close(self):
        self.counter.base += self.n
        self.n = 0

    def rewind(self, eng):
        eng.sem_inc(self.counter.sem, -self.n)
        self.n = 0


class Kernel:
    def __init__(self, nc, ctx, a):
        self.nc, self.ctx, self.a = nc, ctx, a
        self.counters = {}
        self.raw = self.tensor("raw", [P, RAW, CHUNK])
        self.chunks = 0
        self.raw_landed = [self.counter(f"raw_landed{s}").sem for s in range(RAW)]
        self.hi_ready = self.counter("hi_ready").sem
        self.lo_ready = self.counter("lo_ready").sem
        for name in ("turned_done", "turned_out", "rows_done", "rows_out", "ring_stored0", "ring_stored1",
                     "quad_done", "quad_out", "hot1_ready", "hot_hi_ready", "hot_lo_ready", "gates_stored0", "gates_stored1", "ys_done", "ys_added", "at_scores",
                     "at_masked", "at_w_turned", "at_w_out", "at_values", "at_out", "at_weights"):
            self.counter(name, CREDITS)
        self.x = self.tensor("x_res", [P, TT, D])
        self.ident = self.tensor("ident", [P, P])
        self.zero = self.tensor("zero", [P, 1])
        self.gains = self.tensor("gains", [P, 7, DK])
        self.iota = self.tensor("iota", [P, P])
        self.acts = nc.dram_tensor("expert_acts", (NKEY, P, SEQ), F32, kind="Internal").ap()
        self.gates = nc.dram_tensor("expert_gates", (SEQ // GT, P, NKEY, GT), F32, kind="Internal").ap()
        self.dve = Chain(self.counter("dve_step"))
        self.looked = Chain(self.counter("keys_looked_up"))

    def counter(self, name, credits=0):
        if name not in self.counters:
            self.counters[name] = Counter(self.ctx.enter_context(self.nc.semaphore(name)), credits)
        return self.counters[name]

    def tensor(self, name, shape, dt=F32, ctx=None):
        return (ctx or self.ctx).enter_context(self.nc.sbuf_tensor(name, shape, dt))

    def banks(self, name, ctx, n, shape=(P, 512), dt=F32):
        return [ctx.enter_context(self.nc.psum_tensor(f"{name}{b}", list(shape), dt)) for b in range(n)]


    def load_chunk(self, sp, src, i, k):
        slot = (self.chunks + k) % RAW
        sp.wait_ge(self.lo_ready, i * BODY + (self.chunks + k + 1))
        out = self.raw[:, slot, :]
        if len(src.shape) == 3:
            out = out.rearrange("p (b n) -> p b n", b=src.shape[1])
        sp.dma_start(out, src).then_inc(self.raw_landed[slot], 16)

    def load_rest(self, sp, total, src):
        if total > RAW:
            with sp.Fori(0, total // BODY - 1) as i:
                for k in range(BODY):
                    self.load_chunk(sp, src(i * BODY + (k + RAW)), i, k + RAW)

    def load_first(self, sp, done, src):
        if src is None:
            return
        for k in range(RAW):
            slot = (self.chunks + done + k) % RAW
            sp.wait_ge(self.lo_ready, self.chunks + done + k + 1)
            s = src(k)
            out = self.raw[:, slot, :]
            if len(s.shape) == 3:
                out = out.rearrange("p (b n) -> p b n", b=s.shape[1])
            sp.dma_start(out, s).then_inc(self.raw_landed[slot], 16)

    def split_hi(self, act, used, i, k):
        c = self.chunks + k
        act.wait_ge(self.raw_landed[c % RAW], i * (16 * (BODY // RAW)) + 16 * (c // RAW + 1))
        products, per = used
        act.wait_ge(products.sem, i * (BODY * per) + (products.base + (k + 1 - SPLIT) * per))
        act.activation(self.hi[:, c % SPLIT, :], self.raw[:, c % RAW, :], ACT.Copy).then_inc(self.hi_ready, 1)

    def split_lo(self, dve, i, k):
        c = self.chunks + k
        dve.wait_ge(self.hi_ready, i * BODY + (c + 1))
        dve.tensor_tensor(self.lo[:, c % SPLIT, :], self.raw[:, c % RAW, :],
                          self.hi[:, c % SPLIT, :].bitcast(F32), ALU.subtract).then_inc(self.lo_ready, 1)

    def chunk_split(self, pe, i, k):
        pe.wait_ge(self.lo_ready, i * BODY + (self.chunks + k + 1 + RAW))

    def ahead(self, eng, total, lead, follow, chain=None):
        trips = total // BODY
        lead(0, 0)
        if trips > 1:
            with eng.Fori(0, trips - 1) as i:
                if chain:
                    chain.close()
                for k in range(BODY):
                    lead(i, k + 1)
                    follow(i, k)
                if chain and chain.n:
                    chain.rewind(eng)
        for k in range(BODY):
            if k + 1 < BODY:
                lead(trips - 1, k + 1)
            follow(trips - 1, k)

    def split_tensors(self, ctx, tag):
        self.hi = self.tensor(f"w_hi_{tag}", [P, SPLIT, CHUNK], F32R, ctx)
        self.lo = self.tensor(f"w_lo_{tag}", [P, SPLIT, CHUNK], F32R, ctx)

    def three(self, pe, out, lhi, llo, rhi, rlo, first, last):
        pe.matmul(out, lhi, rhi, start=first, stop=False)
        pe.matmul(out, lhi, rlo, start=False, stop=False)
        return pe.matmul(out, llo, rhi, start=False, stop=last)


    def setup(self, first_src):
        a, nc = self.a, self.nc
        const = self.counter("const_ready")
        landed = self.counter("setup_landed")
        iota_i = self.tensor("iota_int", [P, P], I32)
        with nc.Block() as block:
            @block.sync
            def _(sp):
                sp.sem_inc(self.lo_ready, RAW)
                sp.dma_start(self.x[:], a["x"].rearrange("(t p) d -> p t d", p=P)).then_inc(landed.sem, 16)
                sp.dma_start(self.gains[:], a["gains"].rearrange("g p k -> p g k")).then_inc(landed.sem, 16)
                self.load_first(sp, 0, first_src)
                sp.wait_ge(landed.sem, 32)

            @block.scalar
            def _(act):
                for counter in self.counters.values():
                    if counter.base:
                        act.sem_inc(counter.sem, counter.base)

            @block.gpsimd
            def _(pool):
                pool.memset(self.zero[:], 0.0).then_inc(const.sem, 1)
                pool.memset(self.ident[:], 0.0).then_inc(const.sem, 1)
                pool.iota(iota_i[:], pattern=[[1, P]], base=0, channel_multiplier=0).then_inc(const.sem, 1)
                pool.wait_ge(const.sem, 3)
                pool.tensor_copy(self.iota[:], iota_i[:]).then_inc(const.sem, 1)
                pool.affine_select(out=self.ident[:], in_=self.ident[:], compare_op=ALU.not_equal, fill=1.0,
                                   base=0, pattern=[[-1, P]], channel_multiplier=1).then_inc(const.sem, 1)
        const.base += 5
        landed.base += 32


    def rsqrt_steps(self, dve, act_sqrt, v, y, t):
        ch = self.dve
        act_sqrt(v, t)
        ch.link(dve, dve.reciprocal(y, t))
        ch.link(dve, dve.tensor_tensor(t, y, y, ALU.mult))
        ch.link(dve, dve.tensor_tensor(t, t, v, ALU.mult))
        ch.link(dve, dve.tensor_scalar(t, t, -0.5, 1.5, ALU.mult, ALU.add))
        ch.link(dve, dve.tensor_tensor(y, y, t, ALU.mult))

    def norm(self, tag, gain, h_hi, h_lo, xn=None, made=False):
        nc = self.nc
        sq = self.counter("norm_squares")
        root_in = self.counter("norm_root_in")
        root = self.counter("norm_root")
        inverse = self.counter("norm_inverse_root")
        scaled = [self.counter(f"norm_scaled_{e}") for e in ("dve", "act")]
        turned = self.counter("norm_turned")
        hi_done = self.counter("norm_hi")
        lo_done = self.counter("norm_lo")
        with ExitStack() as ctx:
            if xn is None:
                xn = self.tensor(f"xn_{tag}", [P, TT, D], ctx=ctx)
            junk = self.tensor(f"junk_{tag}", [P, D], ctx=ctx)
            st = self.tensor(f"stat_{tag}", [P, 4, TT], ctx=ctx)
            bank = self.banks(f"turn_{tag}", ctx, DK)
            ss, v, y, t = (st[:, n, :] for n in range(4))
            g = self.gains[:, gain, :]
            with nc.Block() as block:
                @block.scalar
                def _(act):
                    if not made:
                        for m in range(TT):
                            if m:
                                act.wait_ge(sq.sem, sq.base + m)
                            act.activation(junk[:], self.x[:, m, :], ACT.Square, accum_out=ss[:, m:m + 1]).then_inc(sq.sem, 1)
                        act.wait_ge(root_in.sem, root_in.base + 1)
                        act.activation(t, v, ACT.Sqrt).then_inc(root.sem, 1)
                        act.wait_ge(inverse.sem, inverse.base + 1)
                        for m in range(1, TT, 2):
                            act.activation(xn[:, m, :], self.x[:, m, :], ACT.Copy, scale=y[:, m:m + 1]).then_inc(scaled[1].sem, 1)
                    for k in range(DK):
                        act.wait_ge(turned.sem, turned.base + k + 1)
                        act.activation(h_hi[:, k, :], bank[k][:], ACT.Copy, scale=g[:, k:k + 1]).then_inc(hi_done.sem, 1)

                @block.vector
                def _(dve):
                    if not made:
                        dve.wait_ge(sq.sem, sq.base + TT)
                        dve.tensor_scalar(v, ss, 1.0 / D, EPS, ALU.mult, ALU.add).then_inc(root_in.sem, 1)
                        self.rsqrt_steps(dve, lambda v, t: dve.wait_ge(root.sem, root.base + 1), v, y, t)
                        dve.sem_inc(inverse.sem, 1)
                        for m in range(0, TT, 2):
                            dve.tensor_scalar(xn[:, m, :], self.x[:, m, :], y[:, m:m + 1], None, ALU.mult).then_inc(scaled[0].sem, 1)
                    for k in range(DK):
                        dve.wait_ge(hi_done.sem, hi_done.base + k + 1)
                        dve.scalar_tensor_tensor(h_lo[:, k, :], bank[k][:], g[:, k:k + 1], h_hi[:, k, :].bitcast(F32),
                                                 ALU.mult, ALU.subtract).then_inc(lo_done.sem, 1)
                    dve.wait_ge(lo_done.sem, lo_done.base + DK)

                @block.tensor
                def _(pe):
                    for m in range(TT):
                        if not made:
                            pe.wait_ge(scaled[m % 2].sem, scaled[m % 2].base + m // 2 + 1)
                        for k in range(DK):
                            last = pe.transpose(bank[k][:, m * P:(m + 1) * P], xn[:, m, k * P:(k + 1) * P], self.ident[:])
                            if m == TT - 1:
                                last.then_inc(turned.sem, 1)
            self.dve.close()
            if not made:
                for s, n in ((sq, TT), (root_in, 1), (root, 1), (inverse, 1), (scaled[0], TT // 2), (scaled[1], TT // 2)):
                    s.base += n
            for s in (turned, hi_done, lo_done):
                s.base += DK

    def split_rows(self, tag, src_slice, h_hi, h_lo, nk):
        hi_done = self.counter("rows_hi")
        lo_done = self.counter("rows_lo")
        with self.nc.Block() as block:
            @block.scalar
            def _(act):
                for k in range(nk):
                    act.activation(h_hi[:, k, :], src_slice(k), ACT.Copy).then_inc(hi_done.sem, 1)

            @block.vector
            def _(dve):
                for k in range(nk):
                    dve.wait_ge(hi_done.sem, hi_done.base + k + 1)
                    dve.tensor_tensor(h_lo[:, k, :], src_slice(k), h_hi[:, k, :].bitcast(F32), ALU.subtract).then_inc(lo_done.sem, 1)
                dve.wait_ge(lo_done.sem, lo_done.base + nk)
        hi_done.base += nk
        lo_done.base += nk


    def loop_chunks(self, eng, total, chunk):
        trips = total // BODY
        if trips > 1:
            with eng.Fori(0, trips) as i:
                for k in range(BODY):
                    chunk(i, k)
        else:
            for k in range(total):
                chunk(0, k)

    def turned_chunk(self, pe, bank, h_hi, h_lo, done, out, i, k, after=lambda b: None):
        self.chunk_split(pe, i, k)
        s = (self.chunks + k) % SPLIT
        for b in range(2):
            n = 2 * k + b
            pe.wait_ge(out.sem, i * (2 * BODY) + (out.base + n - 3))
            for kk in range(DK):
                w = slice((b * DK + kk) * P, (b * DK + kk + 1) * P)
                last = self.three(pe, bank[n % 4][:], self.hi[:, s, w], self.lo[:, s, w],
                                  h_hi[:, kk, :], h_lo[:, kk, :], kk == 0, kk == DK - 1)
            last.then_inc(done.sem, 1)
            after(b)

    def product_turned(self, tag, h_hi, h_lo, total, src, next_src, dst, beside=None):
        done = self.counter("turned_done")
        out = self.counter("turned_out")
        with ExitStack() as ctx:
            self.split_tensors(ctx, tag)
            bank = self.banks(f"acc_{tag}", ctx, 4)
            with self.nc.Block() as block:
                @block.sync
                def _(sp):
                    if beside:
                        beside.sync(sp)
                    self.load_rest(sp, total, src)
                    self.load_first(sp, total, next_src)

                @block.scalar
                def _(act):
                    def evacuate(i, k):
                        for b in range(2):
                            n = 2 * k + b
                            act.wait_ge(done.sem, i * (2 * BODY) + (done.base + n + 1))
                            at = (i * (2 * BODY) + n) * SEQ
                            act.activation(dst[:, bass.ds(at, SEQ)], bank[n % 4][:], ACT.Copy).then_inc(out.sem, 1)
                    self.ahead(act, total, lambda i, k: self.split_hi(act, (done, 2), i, k), evacuate)
                    act.wait_ge(out.sem, out.base + 2 * total)

                @block.vector
                def _(dve):
                    def follow(i, k):
                        if beside and isinstance(i, int):
                            beside.vector(dve, k, out)
                    self.ahead(dve, total, lambda i, k: self.split_lo(dve, i, k), follow)

                @block.tensor
                def _(pe):
                    self.loop_chunks(pe, total, lambda i, k: self.turned_chunk(pe, bank, h_hi, h_lo, done, out, i, k))
            done.base += 2 * total
            out.base += 2 * total
            self.dve.close()
            self.chunks += total

    def product_rows(self, tag, h_hi, h_lo, total, src, next_src, finish=None, beside=None, heads=None):
        done = self.counter("rows_done")
        out = self.counter("rows_out")
        with ExitStack() as ctx:
            self.split_tensors(ctx, tag)
            bank = self.banks(f"acc_{tag}", ctx, 8)
            with self.nc.Block() as block:
                @block.sync
                def _(sp):
                    if beside:
                        beside.sync(sp)
                    self.load_rest(sp, total, src)
                    self.load_first(sp, total, next_src)

                @block.scalar
                def _(act):
                    def follow(i, k):
                        if heads and k % 2:
                            heads.scalar(act, i, k, bank[k // 2 * TT:], done)
                        if beside:
                            beside.scalar(act, k)
                    self.ahead(act, total, lambda i, k: self.split_hi(act, (done, TT), i, k), follow)

                if beside and beside.gpsimd:
                    block.gpsimd(beside.gpsimd)

                @block.vector
                def _(dve):
                    def evacuate(i, k):
                        if k % 2 and heads:
                            heads.vector(dve, i, k, bank[k // 2 * TT:], out)
                        elif k % 2:
                            for m in range(TT):
                                dve.wait_ge(done.sem, i * (TT * BODY) + (done.base + TT * k + m + 1))
                                finish(dve, i * (BODY // 2) + k // 2, m, bank[(k // 2) % 2 * TT + m][:]).then_inc(out.sem, 1)
                        if beside:
                            beside.vector(dve, k)
                    self.ahead(dve, total, lambda i, k: self.split_lo(dve, i, k), evacuate, self.dve)
                    dve.wait_ge(out.sem, out.base + total * TT // 2)

                @block.tensor
                def _(pe):
                    def chunk(i, k):
                        self.chunk_split(pe, i, k)
                        s = (self.chunks + k) % SPLIT
                        for m in range(TT):
                            if k % 2 == 0:
                                pe.wait_ge(out.sem, i * (TT * BODY // 2) + (out.base + (k // 2 - 2) * TT + m + 1))
                            for kk in range(DK // 2):
                                w = slice(kk * 512, (kk + 1) * 512)
                                h = k % 2 * (DK // 2) + kk
                                t = slice(m * P, (m + 1) * P)
                                last = self.three(pe, bank[(k // 2) % 2 * TT + m][:], h_hi[:, h, t], h_lo[:, h, t],
                                                  self.hi[:, s, w], self.lo[:, s, w], h == 0, h == DK - 1)
                            last.then_inc(done.sem, 1)
                    self.loop_chunks(pe, total, chunk)
            done.base += TT * total
            out.base += TT * total // 2
            self.dve.close()
            self.chunks += total


    def peer(self, layer, next_src):
        a = self.a
        wq = a["peer_wq"][layer]
        u = a["peer_u"][layer]
        v = a["peer_v"][layer].rearrange("(i1 i2) d -> i1 i2 d", i2=NKEY)
        wq_src = lambda c: wq[bass.ds(c, 1)].rearrange("a p n -> p a n")
        u_src = lambda c: u[bass.ds(c * 2, 2)].rearrange("b p n -> p b n")
        with ExitStack() as ctx:
            h_hi = self.tensor(f"h_hi_p{layer}", [P, DK, SEQ], F32R, ctx)
            h_lo = self.tensor(f"h_lo_p{layer}", [P, DK, SEQ], F32R, ctx)
            self.norm(f"p{layer}", 3 + layer, h_hi, h_lo)
            sub = self.tensor(f"sub{layer}", [P, UNITS * 2 * NKEY], ctx=ctx)
            with ExitStack() as q_ctx:
                qT = self.tensor(f"qT{layer}", [P, 2 * PH * SEQ], ctx=q_ctx)
                keys = self.tensor(f"keys{layer}", [P, 2 * PH, NKEY], ctx=q_ctx)
                keys_sem = self.counter("keys_landed")

                class LoadKeys:
                    def sync(sp):
                        sp.dma_start(keys[:], a["peer_keys"][layer]).then_inc(keys_sem.sem, 16)

                    def vector(dve, k, out):
                        pass

                self.product_turned(f"pq{layer}", h_hi, h_lo, PH, wq_src, u_src, qT, beside=LoadKeys)
                self.sub_scores(qT, keys, keys_sem, sub, layer)
            self.expert_acts(layer, h_hi, h_lo, u_src, sub, v)
        self.expert_sum(layer, v, next_src)

    def v_src(self, v):
        return lambda g, k: v[:, bass.ds(g * 8 + 4 * (k % 2), 4), 512 * (k // 2):512 * (k // 2) + 512]

    def sub_scores(self, qT, keys, keys_sem, sub, layer):
        done = self.counter("sub_done")
        out = self.counter("sub_out")
        fills = UNITS // 2
        with ExitStack() as ctx:
            bank = self.banks(f"sub_acc{layer}", ctx, 4)
            with self.nc.Block() as block:
                @block.scalar
                def _(act):
                    for n in range(fills):
                        act.wait_ge(done.sem, done.base + n + 1)
                        act.activation(sub[:, n * 512:(n + 1) * 512], bank[n % 4][:], ACT.Copy).then_inc(out.sem, 1)
                    act.wait_ge(out.sem, out.base + fills)

                @block.tensor
                def _(pe):
                    pe.wait_ge(keys_sem.sem, keys_sem.base + 16)
                    for n in range(fills):
                        m, pair = divmod(n, PH // 2)
                        if n >= 4:
                            pe.wait_ge(out.sem, out.base + n - 3)
                        for j in range(4):
                            hp = pair * 4 + j
                            last = pe.matmul(bank[n % 4][:, j * NKEY:(j + 1) * NKEY],
                                             qT[:, hp * SEQ + m * P:hp * SEQ + (m + 1) * P], keys[:, hp, :],
                                             start=True, stop=True)
                        last.then_inc(done.sem, 1)
            keys_sem.base += 16
            done.base += fills
            out.base += fills

    def router(self, ctx, layer, sub, best, picks, located):
        s = self.tensor(f"scores{layer}", [P, 2, NKEY], ctx=ctx)
        s2 = self.tensor(f"scores_less_8{layer}", [P, 2, NKEY], ctx=ctx)
        vals = self.tensor(f"vals{layer}", [P, 2, TOPK], ctx=ctx)
        idx = self.tensor(f"idx{layer}", [P, 2, TOPK], U32, ctx)
        idxf = self.tensor(f"idxf{layer}", [P, 2, TOPK], ctx=ctx)
        cand = self.tensor(f"cand{layer}", [P, TOPK * TOPK], ctx=ctx)
        cand2 = self.tensor(f"cand_less_8{layer}", [P, TOPK * TOPK], ctx=ctx)
        top = self.tensor(f"top{layer}", [P, TOPK], ctx=ctx)
        pos = self.tensor(f"pos{layer}", [P, TOPK], U32, ctx)
        posij = self.tensor(f"posij{layer}", [P, 2, TOPK], U32, ctx)
        posf = self.tensor(f"posf{layer}", [P, 2, TOPK], ctx=ctx)
        hot = self.tensor(f"hot{layer}", [P, 2, TOPK, TOPK], ctx=ctx)
        hot2 = self.tensor(f"hot_times_key{layer}", [P, 2, TOPK, TOPK], ctx=ctx)

        def top16(dve, sets):
            ch = self.dve
            steps = (lambda v, r, v16, i16: dve.max(v16[:, 0:8], v),
                     lambda v, r, v16, i16: dve.max_index(i16[:, 0:8], v16[:, 0:8], v),
                     lambda v, r, v16, i16: dve.match_replace(r, v16[:, 0:8], v, LOWEST),
                     lambda v, r, v16, i16: dve.max(v16[:, 8:16], r),
                     lambda v, r, v16, i16: dve.max_index(i16[:, 8:16], v16[:, 8:16], r))
            marks = [None] * len(sets)
            for step in steps:
                for n, one_set in enumerate(sets):
                    if marks[n]:
                        ch.after(dve, marks[n])
                    marks[n] = ch.mark(step(*one_set))

        def locate(dve, unit):
            ch = self.dve
            ch.link(dve, dve.tensor_copy(s[:].rearrange("p a k -> p (a k)"), sub[:, bass.ds(unit * (2 * NKEY), 2 * NKEY)]))
            top16(dve, [(s[:, half, :], s2[:, half, :], vals[:, half, :], idx[:, half, :]) for half in range(2)])
            ch.after(dve, ch.n)
            ch.mark(dve.tensor_copy(idxf[:], idx[:]))
            ch.link(dve, dve.tensor_tensor(cand[:].rearrange("p (i j) -> p i j", i=TOPK),
                                           vals[:, 0, :].unsqueeze(2).to_broadcast([P, TOPK, TOPK]),
                                           vals[:, 1, :].unsqueeze(1).to_broadcast([P, TOPK, TOPK]), ALU.add))
            top16(dve, [(cand[:], cand2[:], top[:], pos[:])])
            ch.after(dve, ch.n)
            ch.mark(dve.tensor_scalar(posij[:, 0, :], pos[:], 4, None, ALU.logical_shift_right))
            ch.link(dve, dve.tensor_scalar(posij[:, 1, :], pos[:], TOPK - 1, None, ALU.bitwise_and))
            ch.mark(dve.tensor_copy(posf[:], posij[:]))
            ch.link(dve, dve.tensor_copy(best[:, bass.ds(unit, 1), :].rearrange("p a s -> p (a s)"), top[:]))
            dve.tensor_tensor(hot[:].rearrange("p a s c -> p (a s) c"),
                              posf[:].rearrange("p a s -> p (a s)").unsqueeze(2).to_broadcast([P, 2 * TOPK, TOPK]),
                              self.iota[:, 0:TOPK].unsqueeze(1).to_broadcast([P, 2 * TOPK, TOPK]), ALU.is_equal).then_inc(located.sem, 1)

        def look_up(pool, i, k):
            pool.wait_ge(located.sem, i * BODY + (located.base + k + 1))
            pool.tensor_tensor(hot2[:], hot[:], idxf[:].unsqueeze(2).to_broadcast([P, 2, TOPK, TOPK]), ALU.mult)\
                .then_inc(self.looked.counter.sem, 1)

        def pick(dve, unit):
            self.looked.n += 1
            self.looked.after(dve, self.looked.n)
            self.dve.link(dve, dve.tensor_reduce(picks[:, :, bass.ds(unit * TOPK, TOPK)], hot2[:], AX_X, ALU.add))

        return locate, look_up, pick, (hot, hot2)

    def expert_acts(self, layer, h_hi, h_lo, u_src, sub, v):
        c = self.counter
        total = NKEY // 2
        half = total // BODY // 2
        done, out = c("turned_done"), c("turned_out")
        ring_sem = [c(f"ring_stored{r}") for r in range(2)]
        routed, exped, gated, turned_n, turned_out, rounded, g_lo_n = (
            c(n) for n in ("routed", "gate_exp", "gated", "pick_turned", "pick_out", "gate_hi", "gate_lo"))
        located, diffed, absed, hot1, matched, hot_hi, hot_lo, quad, lo_out, quad_out = (
            c(n) for n in ("places_located", "diff_ready", "abs_ready", "hot1_ready", "match_ready", "hot_hi_ready", "hot_lo_ready",
                           "quad_done", "quad_lo_out", "quad_out"))
        g_stored = [c(f"gates_stored{r}") for r in range(2)]
        NQ = 4
        assert (total // 2) * NQ * QUAD == SEQ
        with ExitStack() as ctx:
            t = lambda n, s, dt=F32: self.tensor(f"{n}{layer}", s, dt, ctx)
            self.split_tensors(ctx, f"pu{layer}")
            best = t("best", [P, UNITS, TOPK])
            picks = t("picks", [P, 2, UNITS * TOPK])
            ring = t("acts_ring", [P, 2, 2 * SEQ])
            small = t("gate_small", [P, 2, UNITS])
            turned = t("picks_turned", [P, 4, SEQ])
            g_hi = t("gate_hi_t", [P, SEQ], F32R)
            bank = self.banks(f"acc_pu{layer}", ctx, 4)
            pair = self.banks(f"quad{layer}", ctx, 2, shape=(P, QUAD * 2 * P))
            qbank = [pair[n // 2][:, n % 2 * SEQ:(n % 2 + 1) * SEQ] for n in range(3)]
            locate, look_up, pick, spare = self.router(ctx, layer, sub, best, picks, located)
            gt = sub[:].rearrange("p (r i t) -> p r i t", r=2, t=GT)
            oh1 = t("hot1", [P, NQ, QUAD, P], F32R)
            oh2 = t("hot2", [P, NQ, QUAD, 2, P], F32R)
            diff = [r[:].rearrange("p a s c -> p (a s c)").rearrange("p (r k) -> p r k", k=P) for r in spare]
            match = t("match_i2", [P, 2, QUAD, P])
            iota4 = self.iota[:].unsqueeze(1).to_broadcast([P, QUAD, P])

            H = half * BODY

            def row(n, i, k, q):
                at = i * (NQ * QUAD * BODY) + ((k - H) * NQ + q) * QUAD
                tokens = g_hi[:].bitcast(F32)[:, bass.ds(at, QUAD)] if n == 2 else turned[:, n, bass.ds(at, QUAD)]
                return tokens.unsqueeze(2).to_broadcast([P, QUAD, P])

            def parts(q):
                return pair[q % 2][:].rearrange("p (t a i) -> p t a i", t=QUAD, a=2)

            def quad_gates(k, q):
                at = ((k % 2) * NQ + q) * QUAD
                return gt[:, k // 2 % 2, :, at:at + QUAD].rearrange("p i t -> p t i")

            def at_quad(base, i, k, q):
                return i * (NQ * BODY) + (base + (k - H) * NQ + q)

            with self.nc.Block() as block:
                @block.sync
                def _(sp):
                    def put(i, k):
                        sp.wait_ge(out.sem, i * (2 * BODY) + (out.base + 2 * k + 2))
                        sp.dma_start(self.acts[bass.ds((i * BODY + k) * 2, 2)].rearrange("b p t -> p b t"),
                                     ring[:, k % 2, :].rearrange("p (b t) -> p b t", b=2)).then_inc(ring_sem[k % 2].sem, 16)

                    def put_gates(i, k):
                        if k % 2:
                            sp.wait_ge(quad_out.sem, at_quad(quad_out.base, i, k, NQ))
                            sp.dma_start(self.gates[bass.ds(i * 2 + (k - H) // 2, 1)].rearrange("a p i t -> p (a i t)"),
                                         gt[:, k // 2 % 2].rearrange("p i t -> p (i t)")).then_inc(g_stored[k // 2 % 2].sem, 16)

                    with sp.Fori(0, half) as i:
                        for k in range(BODY):
                            self.load_chunk(sp, u_src(i * BODY + (k + RAW)), i, k + RAW)
                            put(i, k)
                    with sp.Fori(0, half - 1) as i:
                        for k in range(H, H + BODY):
                            self.load_chunk(sp, u_src(i * BODY + (k + RAW)), i, k + RAW)
                            put(i, k)
                            put_gates(i, k)
                    src = self.v_src(v)
                    for k in range(H, H + BODY):
                        self.load_chunk(sp, src(0, k - H), half - 1, k + RAW)
                        put(half - 1, k)
                        put_gates(half - 1, k)
                    for r in range(2):
                        sp.wait_ge(ring_sem[r].sem, ring_sem[r].base + 16 * (total // 2))
                        sp.wait_ge(g_stored[r].sem, g_stored[r].base + 16 * half)

                @block.gpsimd
                def _(pool):
                    def less(i, k, q):
                        pool.wait_ge(hot1.sem, at_quad(hot1.base - 1, i, k, q))
                        pool.tensor_tensor(diff[q % 2], iota4, row(0, i, k, q), ALU.subtract).then_inc(diffed.sem, 1)

                    with pool.Fori(0, half) as i:
                        for k in range(BODY):
                            look_up(pool, i, k)
                    pool.wait_ge(rounded.sem, rounded.base + 1)
                    with pool.Fori(0, half) as i:
                        for k in range(H, H + BODY):
                            for q in range(NQ):
                                if q % 2 == 0:
                                    less(i, k, q)
                                    less(i, k, q + 1)
                                pool.wait_ge(matched.sem, at_quad(matched.base + 1, i, k, q))
                                pool.wait_ge(quad.sem, at_quad(quad.base + 1 - NQ, i, k, q))
                                pool.tensor_tensor(oh2[:, q, :, 1, :], match[:, q % 2], row(3, i, k, q), ALU.mult).then_inc(hot_lo.sem, 1)

                @block.scalar
                def _(act):
                    def split(i, k):
                        self.split_hi(act, (done, 2), i, k)

                    def gelu(i, k):
                        for b in range(2):
                            n = 2 * k + b
                            act.wait_ge(done.sem, i * (2 * BODY) + (done.base + n + 1))
                            if b == 0:
                                act.wait_ge(ring_sem[k % 2].sem, i * (16 * BODY // 2) + (ring_sem[k % 2].base + 16 * (k // 2)))
                            act.activation(ring[:, k % 2, b * SEQ:(b + 1) * SEQ], bank[n % 4][:], ACT.Gelu).then_inc(out.sem, 1)

                    def one_hot(i, k, half_of):
                        for q in (2 * half_of, 2 * half_of + 1):
                            act.wait_ge(diffed.sem, at_quad(diffed.base + 1, i, k, q))
                            act.activation(diff[q % 2], diff[q % 2], ACT.Abs).then_inc(absed.sem, 1)
                            act.wait_ge(absed.sem, at_quad(absed.base + 1, i, k, q))
                            act.wait_ge(quad.sem, at_quad(quad.base + 1 - NQ, i, k, q))
                            act.activation(oh1[:, q], diff[q % 2], ACT.Relu, bias=1.0, scale=-1.0).then_inc(hot1.sem, 1)

                    def gates_lo(i, k, half_of):
                        if k % 2 == 0 and half_of == 0:
                            act.wait_ge(g_stored[k // 2 % 2].sem, i * 16 + g_stored[k // 2 % 2].base)
                        for q in (2 * half_of, 2 * half_of + 1):
                            act.wait_ge(quad.sem, at_quad(quad.base + 1, i, k, q))
                            act.activation(quad_gates(k, q), parts(q)[:, :, 1, :], ACT.Copy).then_inc(lo_out.sem, 1)

                    split(0, 0)
                    split(0, 1)
                    with act.Fori(0, half) as i:
                        for k in range(BODY):
                            gelu(i, k)
                            split(i, k + 2)
                    act.wait_ge(routed.sem, routed.base + 1)
                    act.activation(best[:], best[:], ACT.Exp).then_inc(exped.sem, 1)
                    gelu(0, H)
                    split(0, H + 2)
                    for n in range(3):
                        act.wait_ge(turned_n.sem, turned_n.base + n + 1)
                        act.activation(turned[:, n, :], qbank[n], ACT.Copy).then_inc(turned_out.sem, 1)
                    act.activation(g_hi[:], qbank[2], ACT.Copy).then_inc(rounded.sem, 1)
                    one_hot(0, H, 0)
                    one_hot(0, H, 1)
                    gates_lo(0, H, 0)
                    one_hot(0, H + 1, 0)
                    with act.Fori(0, half - 1) as i:
                        for k in range(H, H + BODY):
                            gelu(i, k + 1)
                            gates_lo(i, k, 1)
                            split(i, k + 3)
                            one_hot(i, k + 1, 1)
                            gates_lo(i, k + 1, 0)
                            one_hot(i, k + 2, 0)
                    for k in range(H, H + BODY):
                        if k + 1 < H + BODY:
                            gelu(half - 1, k + 1)
                        gates_lo(half - 1, k, 1)
                        if k + 3 < H + BODY:
                            split(half - 1, k + 3)
                        if k + 1 < H + BODY:
                            one_hot(half - 1, k + 1, 1)
                            gates_lo(half - 1, k + 1, 0)
                        if k + 2 < H + BODY:
                            one_hot(half - 1, k + 2, 0)

                @block.vector
                def _(dve):
                    ch = self.dve
                    self.split_lo(dve, 0, 0)
                    with dve.Fori(0, half) as i:
                        ch.close()
                        self.looked.close()
                        for k in range(BODY):
                            locate(dve, i * BODY + k)
                            self.split_lo(dve, i, k + 1)
                            pick(dve, i * BODY + k)
                        self.looked.rewind(dve)
                        ch.rewind(dve)
                    self.split_lo(dve, 0, H + 1)
                    ch.link(dve, dve.tensor_copy(small[:, 0, :], best[:, :, 0:1].rearrange("p u a -> p (u a)")))
                    ch.link(dve, dve.tensor_tensor(best[:], best[:], small[:, 0, :].unsqueeze(2).to_broadcast([P, UNITS, TOPK]), ALU.subtract))
                    dve.sem_inc(routed.sem, 1)
                    dve.wait_ge(exped.sem, exped.base + 1)
                    ch.link(dve, dve.tensor_reduce(small[:, 0, :], best[:], AX_X, ALU.add))
                    ch.link(dve, dve.reciprocal(small[:, 1, :], small[:, 0, :]))
                    dve.tensor_tensor(best[:], best[:], small[:, 1, :].unsqueeze(2).to_broadcast([P, UNITS, TOPK]), ALU.mult).then_inc(gated.sem, 1)
                    dve.wait_ge(rounded.sem, rounded.base + 1)
                    dve.tensor_tensor(turned[:, 3, :], turned[:, 2, :], g_hi[:].bitcast(F32), ALU.subtract).then_inc(g_lo_n.sem, 1)
                    dve.wait_ge(g_lo_n.sem, g_lo_n.base + 1)

                    def matches(i, k, half_of):
                        for q in (2 * half_of, 2 * half_of + 1):
                            dve.wait_ge(hot_lo.sem, at_quad(hot_lo.base - 1, i, k, q))
                            dve.wait_ge(hot_hi.sem, at_quad(hot_hi.base - 1, i, k, q))
                            dve.tensor_tensor(match[:, q % 2], iota4, row(1, i, k, q), ALU.is_equal).then_inc(matched.sem, 1)

                    def times_hi(i, k, half_of):
                        for q in (2 * half_of, 2 * half_of + 1):
                            dve.wait_ge(matched.sem, at_quad(matched.base + 1, i, k, q))
                            dve.wait_ge(quad.sem, at_quad(quad.base + 1 - NQ, i, k, q))
                            dve.tensor_tensor(oh2[:, q, :, 0, :], match[:, q % 2], row(2, i, k, q), ALU.mult).then_inc(hot_hi.sem, 1)

                    def gates_out(i, k, half_of):
                        for q in (2 * half_of, 2 * half_of + 1):
                            dve.wait_ge(lo_out.sem, at_quad(lo_out.base + 1, i, k, q))
                            dve.tensor_tensor(quad_gates(k, q), quad_gates(k, q), parts(q)[:, :, 0, :], ALU.add).then_inc(quad_out.sem, 1)

                    matches(0, H, 0)
                    times_hi(0, H, 0)
                    matches(0, H, 1)
                    with dve.Fori(0, half - 1) as i:
                        for k in range(H, H + BODY):
                            times_hi(i, k, 1)
                            self.split_lo(dve, i, k + 2)
                            matches(i, k + 1, 0)
                            gates_out(i, k, 0)
                            times_hi(i, k + 1, 0)
                            matches(i, k + 1, 1)
                            gates_out(i, k, 1)
                    for k in range(H, H + BODY):
                        more = k + 1 < H + BODY
                        times_hi(half - 1, k, 1)
                        if k + 2 < H + BODY:
                            self.split_lo(dve, half - 1, k + 2)
                        if more:
                            matches(half - 1, k + 1, 0)
                        gates_out(half - 1, k, 0)
                        if more:
                            times_hi(half - 1, k + 1, 0)
                            matches(half - 1, k + 1, 1)
                        gates_out(half - 1, k, 1)

                @block.tensor
                def _(pe):
                    def products(i, k, after=lambda b: None):
                        self.turned_chunk(pe, bank, h_hi, h_lo, done, out, i, k, after)

                    def quads(i, k, half_of):
                        for q in (2 * half_of, 2 * half_of + 1):
                            pe.wait_ge(hot1.sem, at_quad(hot1.base + 1, i, k, q))
                            pe.wait_ge(hot_hi.sem, at_quad(hot_hi.base + 1, i, k, q))
                            pe.wait_ge(hot_lo.sem, at_quad(hot_lo.base + 1, i, k, q))
                            pe.wait_ge(quad_out.sem, at_quad(quad_out.base - 1, i, k, q))
                            for r in range(QUAD):
                                last = pe.matmul(pair[q % 2][:, r * 2 * P:(r + 1) * 2 * P], oh1[:, q, r, :],
                                                 oh2[:, q, r].rearrange("p a i -> p (a i)"), start=True, stop=True)
                            last.then_inc(quad.sem, 1)

                    with pe.Fori(0, half) as i:
                        for k in range(BODY):
                            products(i, k)
                    products(0, H)
                    for n, src in enumerate((picks[:, 0, :], picks[:, 1, :], best[:].rearrange("p u s -> p (u s)"))):
                        if n % 2 == 0:
                            ready = (routed, None, gated)[n]
                            pe.wait_ge(ready.sem, ready.base + 1)
                        for m in range(TT):
                            last = pe.transpose(qbank[n][:, m * P:(m + 1) * P], src[:, m * P:(m + 1) * P], self.ident[:])
                        last.then_inc(turned_n.sem, 1)
                    pe.wait_ge(rounded.sem, rounded.base + 1)
                    with pe.Fori(0, half - 1) as i:
                        for k in range(H, H + BODY):
                            products(i, k + 1, lambda b: quads(i, k, b))
                    for k in range(H, H + BODY - 1):
                        products(half - 1, k + 1, lambda b: quads(half - 1, k, b))
                    for b in range(2):
                        quads(half - 1, H + BODY - 1, b)
            self.dve.close()
            nq = SEQ // QUAD
            for s, n in ((done, 2 * total), (out, 2 * total), (ring_sem[0], 16 * (total // 2)), (ring_sem[1], 16 * (total // 2)),
                         (routed, 1), (exped, 1), (gated, 1), (turned_n, 3), (turned_out, 3), (rounded, 1), (g_lo_n, 1),
                         (located, total // 2), (diffed, nq), (absed, nq), (hot1, nq), (lo_out, nq), (matched, nq), (hot_hi, nq), (hot_lo, nq), (quad, nq), (quad_out, nq),
                         (g_stored[0], 16 * half), (g_stored[1], 16 * half)):
                s.base += n
            self.chunks += total

    def expert_sum(self, layer, v, next_src):
        nc = self.nc
        c = self.counter
        G = NKEY // 8
        BODY2 = 2 * BODY
        done, out, a_n, a_hi_n, a_lo_n = (c(n) for n in ("ys_done", "ys_added", "a_gated", "a_hi_ready", "a_lo_ready"))
        a_in = [c(f"a_in{r}") for r in range(2)]
        src = self.v_src(v)
        ch = self.chunks
        with ExitStack() as ctx:
            self.split_tensors(ctx, f"v{layer}")
            a_raw = self.tensor(f"a_raw{layer}", [P, 2, 4, SEQ], ctx=ctx)
            gate = self.tensor(f"a_gate{layer}", [P, 2, SEQ // GT, 4 * GT], ctx=ctx)
            a_hi = self.tensor(f"a_hi{layer}", [P, 2, 8, SEQ], F32R, ctx)
            a_lo = self.tensor(f"a_lo{layer}", [P, 2, 8, SEQ], F32R, ctx)
            bank = self.banks(f"y{layer}", ctx, 8)

            def pairs(eng, step):
                with eng.Fori(0, G // 2) as i:
                    for k in range(BODY2):
                        step(i, k)

            def ahead(eng, lead, follow):
                with eng.Fori(0, G // 2 - 1) as i:
                    for k in range(BODY2):
                        lead(i, k + 1)
                        follow(i, k, False)
                for k in range(BODY2):
                    if k + 1 < BODY2:
                        lead(G // 2 - 1, k + 1)
                    follow(G // 2 - 1, k, k >= BODY)

            def hi(act, i, k):
                act.wait_ge(self.raw_landed[(ch + k) % RAW], i * (16 * BODY2 // RAW) + 16 * ((ch + k) // RAW + 1))
                act.wait_ge(done.sem, i * (TT * BODY2) + (done.base + TT * (k + 1 - SPLIT)))
                act.activation(self.hi[:, (ch + k) % SPLIT, :], self.raw[:, (ch + k) % RAW, :], ACT.Copy).then_inc(self.hi_ready, 1)

            def lo(dve, i, k):
                dve.wait_ge(self.hi_ready, i * BODY2 + (ch + k + 1))
                dve.tensor_tensor(self.lo[:, (ch + k) % SPLIT, :], self.raw[:, (ch + k) % RAW, :],
                                  self.hi[:, (ch + k) % SPLIT, :].bitcast(F32), ALU.subtract).then_inc(self.lo_ready, 1)

            with nc.Block() as block:
                @block.sync
                def _(sp):
                    def load_a(g, j):
                        sp.dma_start(a_raw[:, j], self.acts[bass.ds(g * 8 + 4 * j, 4)].rearrange("i p t -> p i t")).then_inc(a_in[j].sem, 16)
                        sp.dma_start(gate[:, j], self.gates[:, :, bass.ds(g * 8 + 4 * j, 4), :]
                                     .rearrange("c p i t -> p c (i t)")).then_inc(a_in[j].sem, 16)
                    for j in range(2):
                        load_a(0, j)
                    for j in range(2):
                        sp.wait_ge(a_lo_n.sem, a_lo_n.base + j + 1)
                        load_a(1, j)

                    def load_v(i, k):
                        sp.wait_ge(self.lo_ready, i * BODY2 + (ch + k + 1))
                        slot = (ch + k) % RAW
                        sp.dma_start(self.raw[:, slot, :].rearrange("p (b n) -> p b n", b=4),
                                     src(i * 2 + k // 4, k % 4)).then_inc(self.raw_landed[slot], 16)
                    with sp.Fori(0, G // 2 - 1) as i:
                        for k in range(BODY2):
                            load_v(i, k + RAW)
                            if k % 2:
                                g, j = k // 4, k // 2 % 2
                                sp.wait_ge(a_lo_n.sem, i * 4 + (a_lo_n.base + 2 * (g + 1) + j + 1))
                                load_a(i * 2 + (g + 2), j)
                    for k in range(BODY2 - RAW):
                        load_v(G // 2 - 1, k + RAW)
                    self.load_first(sp, 4 * G, next_src)

                @block.scalar
                def _(act):
                    def a_split(i, g, j):
                        act.wait_ge(a_n.sem, i * 4 + (a_n.base + 2 * g + j + 1))
                        act.activation(a_hi[:, g % 2, 4 * j:4 * j + 4, :], a_raw[:, j], ACT.Copy).then_inc(a_hi_n.sem, 1)

                    def first():
                        for j in range(2):
                            a_split(0, 0, j)

                    def follow(i, k, last):
                        if last or k % 2:
                            return
                        g, j = k // 4 + 1, k // 2 % 2
                        if j == 0:
                            act.wait_ge(done.sem, i * (TT * BODY2) + (done.base + TT * k))
                        a_split(i, g, j)
                    hi(act, 0, 0)
                    first()
                    ahead(act, lambda i, k: hi(act, i, k), follow)

                @block.vector
                def _(dve):
                    def a_gate(i, g, j):
                        dve.wait_ge(a_in[j].sem, i * 64 + (a_in[j].base + 32 * (g + 1)))
                        dve.tensor_tensor(a_raw[:, j].rearrange("p i (c t) -> p i c t", t=GT), a_raw[:, j].rearrange("p i (c t) -> p i c t", t=GT),
                                          gate[:, j].rearrange("p c (i t) -> p i c t", t=GT), ALU.mult).then_inc(a_n.sem, 1)

                    def a_split(i, g, j):
                        dve.wait_ge(a_hi_n.sem, i * 4 + (a_hi_n.base + 2 * g + j + 1))
                        dve.tensor_tensor(a_lo[:, g % 2, 4 * j:4 * j + 4, :], a_raw[:, j], a_hi[:, g % 2, 4 * j:4 * j + 4, :].bitcast(F32),
                                          ALU.subtract).then_inc(a_lo_n.sem, 1)

                    def first():
                        for j in range(2):
                            a_gate(0, 0, j)
                            a_split(0, 0, j)

                    def follow(i, k, last):
                        if not last:
                            (a_split if k % 2 else a_gate)(i, k // 4 + 1, k // 2 % 2)
                        if k % 2:
                            half = k // 2 % 2
                            for m in range(TT):
                                dve.wait_ge(done.sem, i * (TT * BODY2) + (done.base + TT * k + m + 1))
                                at = self.x[:, m, half * 512:half * 512 + 512]
                                dve.tensor_tensor(at, at, bank[half * TT + m][:], ALU.add).then_inc(out.sem, 1)
                    lo(dve, 0, 0)
                    first()
                    ahead(dve, lambda i, k: lo(dve, i, k), follow)
                    dve.wait_ge(out.sem, out.base + 2 * TT * G)

                @block.tensor
                def _(pe):
                    def chunk(i, k):
                        pe.wait_ge(self.lo_ready, i * BODY2 + (ch + k + 1 + RAW))
                        s = (ch + k) % SPLIT
                        r, half = k // 4, k // 2 % 2
                        if k % 4 < 2:
                            pe.wait_ge(a_lo_n.sem, i * 4 + (a_lo_n.base + 2 * r + k % 4 + 1))
                        for m in range(TT):
                            t = slice(m * P, (m + 1) * P)
                            if k % 2 == 0:
                                pe.wait_ge(out.sem, i * (4 * TT) + (out.base + (k // 2 - 2) * TT + m + 1))
                            for e in range(4):
                                j = 4 * (k % 2) + e
                                w = slice(e * 512, (e + 1) * 512)
                                last = self.three(pe, bank[half * TT + m][:], a_hi[:, r, j, t], a_lo[:, r, j, t],
                                                  self.hi[:, s, w], self.lo[:, s, w], j == 0, j == 7)
                            last.then_inc(done.sem, 1)
                    pairs(pe, chunk)
            for s, n in ((done, TT * 4 * G), (out, 2 * TT * G), (a_n, 2 * G), (a_hi_n, 2 * G), (a_lo_n, 2 * G), (a_in[0], 32 * G), (a_in[1], 32 * G)):
                s.base += n
            self.chunks += 4 * G


    def conv_mixer(self, next_src):
        a = self.a
        chain = self.dve
        taps_sem = self.counter("taps_landed")
        with ExitStack() as ctx:
            h_hi = self.tensor("h_hi_c", [P, DK, SEQ], F32R, ctx)
            h_lo = self.tensor("h_lo_c", [P, DK, SEQ], F32R, ctx)
            w_in = lambda c: a["a_w_in"][bass.ds(c, 1)].rearrange("a p n -> p a n")
            w_out = lambda c: a["a_w_out"][bass.ds(c, 1)].rearrange("a p n -> p a n")
            self.norm("c", 0, h_hi, h_lo)
            with ExitStack() as ctx2:
                cub = self.tensor("cub", [P, 3 * DK * SEQ], ctx=ctx2)
                c, u, b = (cub[:, g * DK * SEQ:(g + 1) * DK * SEQ].rearrange("p (k t) -> p k t", t=SEQ) for g in range(3))
                PAD = CONV_W - 1
                cu = self.tensor("cu", [P, DK, PAD + SEQ], ctx=ctx2)
                taps = self.tensor("taps", [P, CONV_W, DK], ctx=ctx2)

                class Conv:

                    def sync(sp):
                        sp.dma_start(taps[:], a["a_conv"].rearrange("w p k -> p w k")).then_inc(taps_sem.sem, 16)

                    def vector(dve, k, out):
                        if k == 0:
                            chain.mark(dve.memset(cu[:, :, 0:PAD], 0.0))
                            dve.wait_ge(taps_sem.sem, taps_sem.base + 16)
                            dve.wait_ge(out.sem, out.base + 2 * DK)
                        two = slice(2 * k, 2 * k + 2)
                        chain.link(dve, dve.tensor_tensor(cu[:, two, PAD:], c[:, two, :], u[:, two, :], ALU.mult))
                        marks = [chain.mark(dve.tensor_scalar(c[:, j, :], cu[:, j, 0:SEQ], taps[:, 0, j:j + 1], None, ALU.mult))
                                 for j in (2 * k, 2 * k + 1)]
                        for w in range(1, CONV_W):
                            for n, j in enumerate((2 * k, 2 * k + 1)):
                                chain.after(dve, marks[n])
                                marks[n] = chain.mark(dve.scalar_tensor_tensor(c[:, j, :], cu[:, j, w:w + SEQ], taps[:, w, j:j + 1],
                                                                               c[:, j, :], ALU.mult, ALU.add))
                        chain.after(dve, marks[1])
                        dve.wait_ge(out.sem, out.base + 2 * DK + 2 * k + 2)
                        chain.link(dve, dve.tensor_tensor(b[:, two, :], b[:, two, :], c[:, two, :], ALU.mult))

                self.product_turned("cin", h_hi, h_lo, 3 * DK // 2, w_in, w_out, dst=cub, beside=Conv)
                taps_sem.base += 16
                self.split_rows("c", lambda k: b[:, k, :], h_hi, h_lo, DK)
            self.product_rows("cout", h_hi, h_lo, 4, w_out, next_src, self.add_to_x)

    def add_to_x(self, dve, nb, m, bank):
        at = self.x[:, m, bass.ds(nb * 512, 512)]
        return dve.tensor_tensor(at, at, bank, ALU.add)


    def ple(self, layer, next_src, store=None):
        a, nc = self.a, self.nc
        landed = self.counter("ple_landed")
        hi_n, lo_n, done, out, sig = (self.counter(n) for n in ("ple_hi", "ple_lo", "ple_done", "ple_out", "ple_sig"))
        KP = 2
        w_gate = lambda c: a["ple_wg"][layer][bass.ds(c, 1)].rearrange("a p n -> p a n")
        with ExitStack() as ctx:
            h_hi = self.tensor(f"h_hi_e{layer}", [P, DK, SEQ], F32R, ctx)
            h_lo = self.tensor(f"h_lo_e{layer}", [P, DK, SEQ], F32R, ctx)
            self.norm(f"e{layer}", 5 + layer, h_hi, h_lo)
            gate = self.tensor(f"gate{layer}", [P, TT, D], ctx=ctx)
            t = lambda n, s, dt=F32: self.tensor(f"{n}{layer}", s, dt, ctx)
            pt, pt_hi, pt_lo = t("pT", [P, KP, SEQ]), t("pT_hi", [P, KP, SEQ], F32R), t("pT_lo", [P, KP, SEQ], F32R)
            wp, wp_hi, wp_lo = t("wp", [P, KP, D]), t("wp_hi", [P, KP, D], F32R), t("wp_lo", [P, KP, D], F32R)

            class Split:
                gpsimd = None

                """Loads and splits the embedding and its projection beside the gate's products"""

                def sync(sp):
                    sp.dma_start(pt[:], a["p"][layer].rearrange("k p t -> p k t")).then_inc(landed.sem, 16)
                    sp.dma_start(wp[:], a["ple_wp"][layer].rearrange("k p n -> p k n")).then_inc(landed.sem, 16)

                def scalar(act, k):
                    if k == 0:
                        act.wait_ge(landed.sem, landed.base + 32)
                        act.activation(pt_hi[:], pt[:], ACT.Copy).then_inc(hi_n.sem, 1)
                    if k == 1:
                        act.activation(wp_hi[:], wp[:], ACT.Copy).then_inc(hi_n.sem, 1)

                def vector(dve, k):
                    if k == 0:
                        dve.wait_ge(hi_n.sem, hi_n.base + 1)
                        dve.tensor_tensor(pt_lo[:], pt[:], pt_hi[:].bitcast(F32), ALU.subtract).then_inc(lo_n.sem, 1)
                    if k == 1:
                        dve.wait_ge(hi_n.sem, hi_n.base + 2)
                        dve.tensor_tensor(wp_lo[:], wp[:], wp_hi[:].bitcast(F32), ALU.subtract).then_inc(lo_n.sem, 1)
                    if k == BODY - 1:
                        dve.wait_ge(lo_n.sem, lo_n.base + 2)

            self.product_rows(f"e{layer}", h_hi, h_lo, 4, w_gate, next_src,
                              lambda dve, nb, m, bank: dve.tensor_copy(gate[:, m, bass.ds(nb * 512, 512)], bank), beside=Split)
            added, stored = self.counter("x_added"), self.counter("x_stored")
            with ExitStack() as ctx2:
                bank = self.banks(f"pp{layer}", ctx2, 8)
                with nc.Block() as block:
                    @block.sync
                    def _(sp):
                        if store is not None:
                            for m in range(TT):
                                sp.wait_ge(added.sem, added.base + 2 * (m + 1))
                                sp.dma_start(store[m * P:(m + 1) * P, :], self.x[:, m, :]).then_inc(stored.sem, 16)
                            sp.wait_ge(stored.sem, stored.base + 16 * TT)

                    @block.scalar
                    def _(act):
                        for m in range(TT):
                            act.activation(gate[:, m, :], gate[:, m, :], ACT.Sigmoid).then_inc(sig.sem, 1)

                    @block.vector
                    def _(dve):
                        for n in range(8):
                            m, nb = divmod(n, 2)
                            col = slice(nb * 512, (nb + 1) * 512)
                            if nb == 0:
                                dve.wait_ge(sig.sem, sig.base + m + 1)
                            dve.wait_ge(done.sem, done.base + n + 1)
                            dve.tensor_tensor(gate[:, m, col], gate[:, m, col], bank[n][:], ALU.mult).then_inc(out.sem, 1)
                            dve.wait_ge(out.sem, out.base + n + 1)
                            dve.tensor_tensor(self.x[:, m, col], self.x[:, m, col], gate[:, m, col], ALU.add).then_inc(added.sem, 1)
                        dve.wait_ge(added.sem, added.base + 8)

                    @block.tensor
                    def _(pe):
                        for n in range(8):
                            m, nb = divmod(n, 2)
                            for k in range(KP):
                                t_, w = slice(m * P, (m + 1) * P), slice(nb * 512, (nb + 1) * 512)
                                last = self.three(pe, bank[n][:], pt_hi[:, k, t_], pt_lo[:, k, t_], wp_hi[:, k, w], wp_lo[:, k, w],
                                                  k == 0, k == KP - 1)
                            last.then_inc(done.sem, 1)
            for s, n in ((landed, 32), (hi_n, 2), (lo_n, 2), (done, 8), (out, 8), (added, 8)):
                s.base += n
            self.dve.close()
            sig.base += TT


    def rope_tables(self, ctx, temp, room):
        nc, a, ch = self.nc, self.a, self.dve
        landed, const, folded, made = (self.counter(n) for n in ("pos_landed", "freq_ready", "angle_folded", "rope_made"))
        self.rope = self.tensor("rope_gain", [P, 2, 4, TT, HALF], ctx=ctx)
        self.mask1 = self.tensor("mask_dilation1", [P, 2 * P], ctx=ctx)
        self.masks = [self.mask1] + [self.tensor(f"mask_dilation{d}", [P, SEQ], ctx=ctx) for d in DILATIONS[1:]]
        self.qk_column = self.tensor("qk_column", [P, 2], ctx=ctx)
        freqs = (np.float32(1.0) / (np.float32(THETA) ** (np.arange(0, ROPE, 2, dtype=np.float32) / np.float32(ROPE)))).astype(np.float32)
        C1 = 6.28125
        C2 = float(np.float32(np.round((TWO_PI - C1) * 2 ** 21) / 2 ** 21))
        C3 = float(np.float32(TWO_PI - C1 - C2))
        MAGIC = 1.5 * 2 ** 23
        PI = float(np.nextafter(np.float32(np.pi), np.float32(0)))
        t = lambda n, s, dt=F32: self.tensor(n, s, dt, temp)
        pos, posf, freq = t("pos", [P, TT], I32), t("pos_f", [P, TT]), t("freq", [P, HALF])
        ang, turns, fold = t("angle", [P, TT, HALF]), t("turns", [P, TT, HALF]), t("folded", [P, 2, TT, HALF])
        diff, dif2 = (room[:, n, 0:SEQ].bitcast(I32) for n in range(2))
        qk_row = t("qk_row", [P, 2, DH])
        sines = self.counter("sines_made")
        link = lambda dve, ins: ch.link(dve, ins)

        class Rope:
            def sync(sp):
                sp.dma_start(pos[:], a["positions"]).then_inc(landed.sem, 16)
                for n, name in enumerate(("k_norm", "q_norm")):
                    sp.dma_start(qk_row[:, n:n + 1, :], a[name].partition_broadcast(P)).then_inc(landed.sem, 16)
                    sp.dma_start(self.qk_column[:, n:n + 1], a[name].rearrange("a d -> d a")).then_inc(landed.sem, 16)

            def gpsimd(pool):
                for j in range(HALF):
                    pool.memset(freq[:, j:j + 1], float(freqs[j])).then_inc(const.sem, 1)
                pool.memset(self.mask1[:], 0.0).then_inc(const.sem, 1)
                pool.iota(diff[:], pattern=[[-1, SEQ]], base=SEQ, channel_multiplier=1).then_inc(const.sem, 1)
                pool.wait_ge(const.sem, const.base + HALF + 1)
                pool.affine_select(out=self.mask1[:], in_=self.mask1[:], compare_op=ALU.is_ge, fill=LOWEST,
                                   base=P, pattern=[[-1, 2 * P]], channel_multiplier=1).then_inc(const.sem, 1)
                pool.wait_ge(const.sem, const.base + HALF + 3)
                pool.affine_select(out=self.mask1[:], in_=self.mask1[:], compare_op=ALU.is_ge, fill=LOWEST,
                                   base=0, pattern=[[1, 2 * P]], channel_multiplier=-1).then_inc(const.sem, 1)
                for n in range(2):
                    mask = self.masks[n + 1]
                    pool.wait_ge(made.sem, made.base + n + 1)
                    pool.affine_select(out=mask[:], in_=mask[:], compare_op=ALU.is_ge, fill=LOWEST,
                                       base=SEQ - P, pattern=[[-1, SEQ]], channel_multiplier=1).then_inc(const.sem, 1)

            def scalar(act, k):
                if k == 1:
                    act.wait_ge(folded.sem, folded.base + 1)
                    for n in range(2):
                        act.activation(fold[:, n], fold[:, n], ACT.Sin).then_inc(sines.sem, 1)

            def vector(dve, k):
                if k == 0:
                    dve.wait_ge(const.sem, const.base + HALF + 2)
                    for n, d in enumerate(DILATIONS[1:]):
                        mask = self.masks[n + 1]
                        link(dve, dve.tensor_scalar(dif2[:], diff[:], d - 1, None, ALU.bitwise_and))
                        link(dve, dve.tensor_scalar(mask[:], dif2[:], 0.0, None, ALU.is_equal))
                        dve.tensor_scalar(mask[:], mask[:], -1.0, -LOWEST, ALU.add, ALU.mult).then_inc(made.sem, 1)
                    dve.wait_ge(landed.sem, landed.base + 80)
                    ch.mark(dve.memset(self.qk_column[0:ROPE, :], 1.0))
                    link(dve, dve.tensor_copy(posf[:], pos[:]))
                    link(dve, dve.tensor_tensor(ang[:], posf[:].unsqueeze(2).to_broadcast([P, TT, HALF]),
                                                freq[:].unsqueeze(1).to_broadcast([P, TT, HALF]), ALU.mult))
                    for n, quarter in enumerate((0.0, 0.25)):
                        f = fold[:, n]
                        link(dve, dve.tensor_scalar(turns[:], ang[:], float(1 / TWO_PI), quarter, ALU.mult, ALU.add))
                        link(dve, dve.tensor_scalar(turns[:], turns[:], MAGIC, None, ALU.add))
                        link(dve, dve.tensor_scalar(turns[:], turns[:], -MAGIC, None, ALU.add))
                        link(dve, dve.scalar_tensor_tensor(f, turns[:], -C1, ang[:], ALU.mult, ALU.add))
                        link(dve, dve.scalar_tensor_tensor(f, turns[:], -C2, f, ALU.mult, ALU.add))
                        link(dve, dve.scalar_tensor_tensor(f, turns[:], -C3, f, ALU.mult, ALU.add))
                        link(dve, dve.tensor_scalar(f, f, float(quarter * TWO_PI), PI, ALU.add, ALU.min))
                        link(dve, dve.tensor_scalar(f, f, -PI, None, ALU.max))
                    dve.sem_inc(folded.sem, 1)
                if k == 2:
                    dve.wait_ge(sines.sem, sines.base + 2)
                    for r in range(2):
                        for n, (wave, half) in enumerate(((1, 0), (0, 1), (1, 1), (0, 0))):
                            gain = qk_row[:, r, half * HALF:(half + 1) * HALF].unsqueeze(1).to_broadcast([P, TT, HALF])
                            ch.mark(dve.tensor_tensor(self.rope[:, r, n], fold[:, wave], gain, ALU.mult))
                    ch.after(dve, ch.n)

        def close():
            for s, n in ((landed, 80), (const, HALF + 6), (folded, 1), (made, 2), (sines, 2)):
                s.base += n
        return Rope, close

    def head_norm_rope(self, ctx, tag, dst, which, squares):
        ch = self.dve
        sq, root_in, root = (self.counter(n) for n in ("head_squares", "head_root_in", "head_root"))
        t = lambda n, s: self.tensor(f"{n}_{tag}", s, F32, ctx)
        H = 512 // DH
        st = t("head_stat", [P, 4, TT * H])
        rot = t("head_rot", [P, 4, TT, H, HALF])
        ss, v, y, r = (st[:, n, :] for n in range(4))
        by_head = lambda x: x.rearrange("p (h d) -> p h d", d=DH)

        class Heads:
            def scalar(act, i, k, bank, done):
                for m in range(TT):
                    act.wait_ge(done.sem, i * (TT * BODY) + (done.base + TT * k + m + 1))
                    act.activation(squares[:, m, :], bank[m][:], ACT.Square).then_inc(sq.sem, 1)
                act.wait_ge(root_in.sem, i * (BODY // 2) + (root_in.base + k // 2 + 1))
                act.activation(r, v, ACT.Sqrt).then_inc(root.sem, 1)

            def vector(dve, i, k, bank, out):
                at = bass.ds((i * (BODY // 2) + k // 2) * 512, 512)
                for m in range(TT):
                    dve.wait_ge(sq.sem, i * (TT * BODY // 2) + (sq.base + TT * (k // 2) + m + 1))
                    ch.mark(dve.tensor_reduce(ss[:, m * H:(m + 1) * H], by_head(squares[:, m, :]), AX_X, ALU.add))
                ch.after(dve, ch.n)
                dve.tensor_scalar(v, ss, 1.0 / DH, EPS, ALU.mult, ALU.add).then_inc(root_in.sem, 1)
                self.rsqrt_steps(dve, lambda v, t: dve.wait_ge(root.sem, i * (BODY // 2) + (root.base + k // 2 + 1)), v, y, r)
                for m in range(TT):
                    dve.tensor_tensor(by_head(dst[:, m, at]), by_head(bank[m][:]),
                                      y[:, m * H:(m + 1) * H].unsqueeze(2).to_broadcast([P, H, DH]), ALU.mult).then_inc(out.sem, 1)
                dve.wait_ge(out.sem, i * (TT * BODY // 2) + (out.base + TT * (k // 2 + 1)))
                x4 = dst[:, :, at].rearrange("p m (h d) -> p m h d", d=DH)
                x1, x2 = x4[:, :, :, 0:HALF], x4[:, :, :, HALF:ROPE]
                for n, x in enumerate((x1, x2, x2, x1)):
                    table = self.rope[:, which, n].unsqueeze(2).to_broadcast([P, TT, H, HALF])
                    ch.mark(dve.tensor_tensor(rot[:, n], x, table, ALU.mult))
                ch.after(dve, ch.n)
                ch.mark(dve.tensor_tensor(x1, rot[:, 0], rot[:, 1], ALU.subtract))
                ch.link(dve, dve.tensor_tensor(x2, rot[:, 2], rot[:, 3], ALU.add))

        def close(blocks):
            sq.base += TT * blocks
            root_in.base += blocks
            root.base += blocks
        return Heads, close

    def turn_heads(self, tag, src, dst, slices, which):
        turned = self.counter("heads_turned")
        out = [self.counter(f"heads_out_{e}") for e in ("act", "dve")]
        gain = self.qk_column[:, which:which + 1]
        with ExitStack() as ctx:
            bank = self.banks(f"turn_{tag}", ctx, 8)
            with self.nc.Block() as block:
                @block.scalar
                def _(act):
                    for k in range(0, slices, 2):
                        act.wait_ge(turned.sem, turned.base + k + 1)
                        act.activation(dst[:, k * SEQ:(k + 1) * SEQ], bank[k % 8][:], ACT.Copy, scale=gain).then_inc(out[0].sem, 1)

                @block.vector
                def _(dve):
                    for k in range(1, slices, 2):
                        dve.wait_ge(turned.sem, turned.base + k + 1)
                        dve.tensor_scalar(dst[:, k * SEQ:(k + 1) * SEQ], bank[k % 8][:], gain, None, ALU.mult).then_inc(out[1].sem, 1)

                @block.tensor
                def _(pe):
                    for k in range(slices):
                        if k >= 8:
                            pe.wait_ge(out[k % 2].sem, out[k % 2].base + (k - 8) // 2 + 1)
                        for m in range(TT):
                            last = pe.transpose(bank[k % 8][:, m * P:(m + 1) * P], src[:, m, k * P:(k + 1) * P], self.ident[:])
                        last.then_inc(turned.sem, 1)
        turned.base += slices
        for s in out:
            s.base += slices // 2

    def turn(self, tag, src, put_hi, put_lo=None, slices=DK):
        turned, hi_done, lo_done = (self.counter(n) for n in ("turn_turned", "turn_hi", "turn_lo"))
        last_done = lo_done if put_lo else hi_done
        with ExitStack() as ctx:
            bank = self.banks(f"turn_{tag}", ctx, 4)
            with self.nc.Block() as block:
                @block.scalar
                def _(act):
                    for k in range(slices):
                        act.wait_ge(turned.sem, turned.base + k + 1)
                        put_hi(act, k, bank[k % 4][:]).then_inc(hi_done.sem, 1)

                @block.vector
                def _(dve):
                    if put_lo:
                        for k in range(slices):
                            dve.wait_ge(hi_done.sem, hi_done.base + k + 1)
                            put_lo(dve, k, bank[k % 4][:]).then_inc(lo_done.sem, 1)

                @block.tensor
                def _(pe):
                    for k in range(slices):
                        if k >= 4:
                            pe.wait_ge(last_done.sem, last_done.base + k - 3)
                        for m in range(TT):
                            last = pe.transpose(bank[k % 4][:, m * P:(m + 1) * P], src[:, m, k * P:(k + 1) * P], self.ident[:])
                        last.then_inc(turned.sem, 1)
            turned.base += slices
            hi_done.base += slices
            if put_lo:
                lo_done.base += slices

    def attention_mixer(self, next_src):
        a = self.a
        part = lambda w: lambda c: w[bass.ds(c, 1)].rearrange("a p n -> p a n")
        wk, wv, wq, wo = part(a["w_k"]), part(a["w_v"]), part(a["b_w_q"]), part(a["b_w_o"])
        with ExitStack() as ctx:
            kT = self.tensor("kT", [P, KVH * SEQ], ctx=ctx)
            v_sb = self.tensor("v_sb", [P, TT, D], ctx=ctx)
            q_sb = self.tensor("q_sb", [P, TT, GROUPS * D], ctx=ctx)
            k_sb, xn, o_sb = q_sb[:, :, 0:D], q_sb[:, :, D:2 * D], q_sb[:, :, 0:D]
            squares = q_sb[:, :, GROUPS * D - 512:]
            with ExitStack() as c2:
                rope, rope_close = self.rope_tables(ctx, c2, squares)
                h_hi = self.tensor("h_hi_a", [P, DK, SEQ], F32R, c2)
                h_lo = self.tensor("h_lo_a", [P, DK, SEQ], F32R, c2)
                self.norm("kv", 1, h_hi, h_lo, xn)
                self.product_rows("v", h_hi, h_lo, 4, wv, wk, beside=rope,
                                  finish=lambda dve, nb, m, bank: dve.tensor_copy(v_sb[:, m, bass.ds(nb * 512, 512)], bank))
                rope_close()
                with ExitStack() as c3:
                    heads, heads_close = self.head_norm_rope(c3, "k", k_sb, 0, squares)
                    self.product_rows("k", h_hi, h_lo, 4, wk, wq, heads=heads)
                    heads_close(2)
                self.norm("q", 2, h_hi, h_lo, xn, made=True)
                self.turn_heads("k", k_sb, kT, KVH, 0)
                with ExitStack() as c3:
                    heads, heads_close = self.head_norm_rope(c3, "q", q_sb, 1, squares)
                    self.product_rows("q", h_hi, h_lo, 12, wq, wo, heads=heads)
                    heads_close(6)
            with ExitStack() as c2:
                with ExitStack() as c3:
                    qT_all = self.tensor("qT_all", [P, GROUPS * KVH * SEQ], ctx=c3)
                    self.turn_heads("queries", q_sb, qT_all, GROUPS * KVH, 1)
                    self.attend(qT_all, kT, v_sb, o_sb, q_sb[:, :, D:])
                h_hi = self.tensor("o_hi", [P, DK, SEQ], F32R, c2)
                h_lo = self.tensor("o_lo", [P, DK, SEQ], F32R, c2)
                self.turn("o", o_sb, lambda act, k, bank: act.activation(h_hi[:, k, :], bank, ACT.Copy),
                          lambda dve, k, bank: dve.tensor_tensor(h_lo[:, k, :], bank, h_hi[:, k, :].bitcast(F32), ALU.subtract))
                self.product_rows("o", h_hi, h_lo, 4, wo, next_src, self.add_to_x)

    def attend(self, qT_all, kT, v_sb, o_sb, room):
        nc, ch = self.nc, self.dve
        names = ("at_staged", "at_scores", "at_masked", "at_max", "at_exp", "at_inverse", "at_half_sum",
                 "at_weights", "at_w_turned", "at_w_out", "at_values", "at_out")
        staged, scores, masked, maxed, exped, inverse, halves, weights, w_turned, w_out, values, out = (self.counter(n) for n in names)
        with ExitStack() as ctx:
            t = lambda n, s: self.tensor(n, s, F32, ctx)
            qT = t("q_head_turned", [P, 2, GROUPS, SEQ])
            S = room[:, :, 0:2 * P + 2 * SEQ]
            W = room[:, :, 2 * P + 2 * SEQ:2 * P + 3 * SEQ]
            wT = t("weights_turned", [P, 2, SEQ])
            st = t("softmax_stat", [P, 4, TT])
            sets = [self.banks(f"s{r}_", ctx, GROUPS) for r in range(2)]
            w_bank, o_bank = self.banks("wv", ctx, 2)
            top, neg, den, inv = (st[:, n, :] for n in range(4))

            def spans(m):
                w = (m + 1) * P
                g0 = 0 if m else P
                return [(g0, 2 * P, g0), (2 * P, 2 * P + w, SEQ - w), (2 * P + w, 2 * P + 2 * w, SEQ - w)]

            LEAD = 3

            def pairs(eng, head, chain=None):
                with eng.Fori(0, KVH // 2 - 1) as i:
                    if chain:
                        chain.close()
                    head(i, 0, True)
                    head(i, 1, True)
                    if chain:
                        chain.rewind(eng)
                head(KVH // 2 - 1, 0, True)
                head(KVH // 2 - 1, 1, False)

            with nc.Block() as block:
                @block.gpsimd
                def _(pool):
                    def weigh(i, n):
                        m = n % TT
                        pool.wait_ge(exped.sem, i * (2 * TT) + (exped.base + n + 1))
                        pool.wait_ge(w_turned.sem, i * (2 * TT) + (w_turned.base + n + 1 - TT))
                        row = S[:, m, :]
                        sp0, sp1, sp2 = spans(m)
                        pool.tensor_tensor(W[:, m, 0:(m + 1) * P], row[:, sp1[0]:sp1[1]], row[:, sp2[0]:sp2[1]], ALU.add)\
                            .then_inc(halves.sem, 1)
                        at = W[:, m, max(m - 1, 0) * P:(m + 1) * P]
                        pool.wait_ge(halves.sem, i * (2 * TT) + (halves.base + n + 1))
                        pool.tensor_tensor(at, at, row[:, sp0[0]:sp0[1]], ALU.add).then_inc(weights.sem, 1)

                    with pool.Fori(0, KVH // 2) as i:
                        for n in range(2 * TT):
                            weigh(i, n)

                @block.tensor
                def _(pe):
                    def score(i, n):
                        pe.wait_ge(masked.sem, i * (2 * TT) + (masked.base + n - 1))
                        r, m = n // TT, n % TT
                        if m == 0:
                            pe.wait_ge(staged.sem, i * (2 * GROUPS) + (staged.base + GROUPS * (r + 1)))
                        keys = max(m - 1, 0) * P
                        for g in range(GROUPS):
                            lo, hi, _ = spans(m)[g]
                            first = keys if g == 0 else 0
                            last = pe.matmul(sets[m % 2][g][:, 0:hi - lo], qT[:, r % 2, g, m * P:(m + 1) * P],
                                             kT[:, bass.ds(i * (2 * SEQ) + (r * SEQ + first), hi - lo)], start=True, stop=True)
                        last.then_inc(scores.sem, 1)

                    def turn_weights(i, n):
                        m = n % TT
                        pe.wait_ge(weights.sem, i * (2 * TT) + (weights.base + n + 1))
                        pe.wait_ge(w_out.sem, i * (2 * TT) + (w_out.base + n))
                        for b in range(m + 1):
                            last = pe.transpose(w_bank[:, b * P:(b + 1) * P], W[:, m, b * P:(b + 1) * P], self.ident[:])
                        last.then_inc(w_turned.sem, 1)

                    def value(i, n):
                        m = n % TT
                        pe.wait_ge(w_out.sem, i * (2 * TT) + (w_out.base + n + 1))
                        pe.wait_ge(out.sem, i * (2 * TT) + (out.base + n))
                        for b in range(m + 1):
                            last = pe.matmul(o_bank[:, 0:DH], wT[:, m % 2, b * P:(b + 1) * P],
                                             v_sb[:].rearrange("p m d -> p (m d)")[:, bass.ds(i * (2 * DH) + (n // TT * DH + b * D), DH)],
                                             start=b == 0, stop=b == m)
                        last.then_inc(values.sem, 1)

                    def head(i, r, more):
                        for m in range(TT):
                            turn_weights(i, r * TT + m)
                            if m + LEAD < TT or more:
                                score(i, r * TT + m + LEAD)
                            value(i, r * TT + m)
                    for n in range(LEAD):
                        score(0, n)
                    pairs(pe, head)

                @block.scalar
                def _(act):
                    def stage(i, r, g):
                        act.wait_ge(scores.sem, i * (2 * TT) + (scores.base + (r - 1) * TT))
                        act.activation(qT[:, r % 2, g, :], qT_all[:, bass.ds(i * (2 * SEQ) + (g * KVH + r) * SEQ, SEQ)], ACT.Copy)\
                            .then_inc(staged.sem, 1)

                    def exp(i, n):
                        m = n % TT
                        act.wait_ge(maxed.sem, i * (2 * TT) + (maxed.base + n + 1))
                        lo, hi = spans(m)[0][0], spans(m)[2][1]
                        act.activation(S[:, m, lo:hi], S[:, m, lo:hi], ACT.Exp, bias=neg[:, m:m + 1],
                                       accum_out=den[:, m:m + 1]).then_inc(exped.sem, 1)

                    def turned(i, n):
                        m = n % TT
                        act.wait_ge(w_turned.sem, i * (2 * TT) + (w_turned.base + n + 1))
                        act.wait_ge(values.sem, i * (2 * TT) + (values.base + n - 1))
                        act.activation(wT[:, m % 2, 0:(m + 1) * P], w_bank[:, 0:(m + 1) * P], ACT.Copy).then_inc(w_out.sem, 1)

                    def put(i, n):
                        m = n % TT
                        act.wait_ge(inverse.sem, i * (2 * TT) + (inverse.base + n + 1))
                        act.wait_ge(values.sem, i * (2 * TT) + (values.base + n + 1))
                        act.activation(o_sb[:, m, bass.ds(i * (2 * DH) + n // TT * DH, DH)], o_bank[:, 0:DH], ACT.Copy,
                                       scale=inv[:, m:m + 1]).then_inc(out.sem, 1)

                    def head(i, r, more):
                        for m in range(TT):
                            n = r * TT + m
                            turned(i, n)
                            put(i, n)
                            if m + LEAD < TT or more:
                                exp(i, n + LEAD)
                            if r == 0 or more:
                                for g in (range(GROUPS), (), (), ())[m]:
                                    stage(i, r + 1, g)
                    for g in range(GROUPS):
                        stage(0, 0, g)
                    for n in range(LEAD):
                        exp(0, n)
                    pairs(act, head)
                    act.wait_ge(out.sem, out.base + TT * KVH)

                @block.vector
                def _(dve):
                    link = lambda ins: ch.link(dve, ins)

                    def mask(i, n):
                        m = n % TT
                        dve.wait_ge(scores.sem, i * (2 * TT) + (scores.base + n + 1))
                        dve.wait_ge(weights.sem, i * (2 * TT) + (weights.base + n + 1 - TT))
                        for g in range(GROUPS):
                            lo, hi, at = spans(m)[g]
                            last = dve.scalar_tensor_tensor(S[:, m, lo:hi], sets[m % 2][g][:, 0:hi - lo], DH ** -0.5,
                                                            self.masks[g][:, at:at + hi - lo], ALU.mult, ALU.add)
                        last.then_inc(masked.sem, 1)
                        dve.wait_ge(masked.sem, i * (2 * TT) + (masked.base + n + 1))
                        link(dve.tensor_reduce(top[:, m:m + 1], S[:, m, spans(m)[0][0]:spans(m)[2][1]], AX_X, ALU.max))
                        dve.tensor_scalar(neg[:, m:m + 1], top[:, m:m + 1], -1.0, None, ALU.mult).then_inc(maxed.sem, 1)

                    def invert(i, n):
                        m = n % TT
                        dve.wait_ge(exped.sem, i * (2 * TT) + (exped.base + n + 1))
                        dve.wait_ge(out.sem, i * (2 * TT) + (out.base + n + 1 - TT))
                        dve.reciprocal(inv[:, m:m + 1], den[:, m:m + 1]).then_inc(inverse.sem, 1)

                    def head(i, r, more):
                        for m in range(TT):
                            n = r * TT + m
                            invert(i, n)
                            if m + LEAD < TT or more:
                                mask(i, n + LEAD)
                    for n in range(LEAD):
                        mask(0, n)
                    pairs(dve, head, ch)
                    ch.close()
            for s, n in ((staged, GROUPS * KVH),) + tuple(
                    (s, TT * KVH) for s in (scores, masked, maxed, exped, inverse, halves, weights, w_turned, w_out, values, out)):
                s.base += n


def build(nc, a, out):
    with ExitStack() as ctx:
        k = Kernel(nc, ctx, a)
        first = lambda w: lambda c: w[bass.ds(c, 1)].rearrange("a p n -> p a n")
        k.setup(first(a["a_w_in"]))
        k.conv_mixer(first(a["peer_wq"][0]))
        k.peer(0, first(a["ple_wg"][0]))
        k.ple(0, first(a["w_v"]))
        k.attention_mixer(first(a["peer_wq"][1]))
        k.peer(1, first(a["ple_wg"][1]))
        k.ple(1, None, store=out)


def slices_turned(w):
    n = w.shape[-1] // (2 * P)
    return np.ascontiguousarray(w.reshape(DK, P, n, 2, P).transpose(2, 1, 3, 0, 4)).reshape(n, P, CHUNK)


def slices_rows(w):
    n = w.shape[-1] // 512
    return np.ascontiguousarray(w.reshape(2, DK // 2, P, n, 512).transpose(3, 0, 2, 1, 4)).reshape(2 * n, P, CHUNK)


def kernel(x, p, positions, a_norm, a_w_in, a_conv, a_w_out, kv_norm, w_kv, k_norm, b_norm, b_w_q, q_norm, b_w_o,
           ffn_norm, peer_w_q, peer_sub_keys, peer_u, peer_v, ple_norm, ple_w_gate, ple_w_proj):
    import concourse.bacc as bacc
    from concourse.bass_utils import run_bass_kernel_spmd

    f = np.asarray
    column = lambda g: f(g).reshape(DK, P).T
    layers = range(2)
    arrays = {
        "x": f(x)[0],
        "p": np.stack([np.ascontiguousarray(f(p)[i, 0].T).reshape(2, P, SEQ) for i in layers]),
        "positions": np.ascontiguousarray(f(positions).reshape(TT, P).T),
        "gains": np.stack([column(g) for g in (f(a_norm)[0], kv_norm, f(b_norm)[0], f(ffn_norm)[0], f(ffn_norm)[1],
                                               f(ple_norm)[0], f(ple_norm)[1])]),
        "a_w_in": slices_turned(np.roll(f(a_w_in)[0], -D, axis=1)),
        "a_conv": np.ascontiguousarray(f(a_conv)[0].reshape(CONV_W, DK, P).transpose(0, 2, 1)),
        "a_w_out": slices_rows(f(a_w_out)[0]),
        "w_k": slices_rows(f(w_kv)[:, :D]),
        "w_v": slices_rows(f(w_kv)[:, D:]),
        "k_norm": f(k_norm).reshape(1, DH),
        "q_norm": f(q_norm).reshape(1, DH),
        "b_w_q": slices_rows(f(b_w_q)[0]),
        "b_w_o": slices_rows(f(b_w_o)[0]),
        "peer_wq": np.stack([slices_turned(f(peer_w_q)[i]) for i in layers]),
        "peer_keys": np.ascontiguousarray(f(peer_sub_keys).reshape(2, 2 * PH, NKEY, P).transpose(0, 3, 1, 2)),
        "peer_u": np.stack([np.ascontiguousarray(f(peer_u)[i].reshape(NKEY, NKEY, DK, P).transpose(1, 3, 2, 0))
                            .reshape(NKEY, P, DK * NKEY) for i in layers]),
        "peer_v": f(peer_v),
        "ple_wg": np.stack([slices_rows(f(ple_w_gate)[i]) for i in layers]),
        "ple_wp": f(ple_w_proj).reshape(2, 2, P, D),
    }
    nc = bacc.Bacc("TRN2", target_bir_lowering=False, num_devices=1)
    ins, aps = {}, {}
    for name, value in arrays.items():
        value = np.ascontiguousarray(value)
        ins[f"in_{name}"] = value
        aps[name] = nc.dram_tensor(f"in_{name}", value.shape, mybir.dt.from_np(value.dtype), kind="ExternalInput").ap()
    out = nc.dram_tensor("out_x", (SEQ, D), F32, kind="ExternalOutput").ap()
    build(nc, aps, out)
    r = run_bass_kernel_spmd(nc, [ins], core_ids=[0])
    return r.results[0]["out_x"].reshape(1, SEQ, D)
```
